# Optimizing a Trainium2 kernel written in Bass

```python
import jax, jax.numpy as jnp
from jax import lax
import numpy as np

D_MODEL = 1024
BATCH = 1
SEQ = 512
DEPTH = 2
DEC_BATCH = 8
DEC_SEQ = 1
PAST_LEN = 4096
PAGE_SIZE = 128

N_BRANCH = 4
N_HEADS = 4
HEAD_DIM = 64
W_MIX = N_HEADS * HEAD_DIM
RWKV_LORA_W = 64
RWKV_LORA_A = 64
CONV_W = 4
LRU_C = 8.0
RET_CHUNK = 128
GDN_CHUNK = 64
ROPE_BASE = 10000.0
EPS = 1e-6
RWKV_GN_EPS = 64e-5

A_SHIFT_W = 3 * W_MIX + RWKV_LORA_W + RWKV_LORA_A
A_W = A_SHIFT_W + W_MIX
B_W = 4 * W_MIX
C_W = 2 * W_MIX
D_QKV_W = 3 * W_MIX
D_W = D_QKV_W + 2 * N_HEADS + W_MIX
G_W = N_BRANCH * D_MODEL
OFF_A = 0
OFF_B = OFF_A + A_W
OFF_C = OFF_B + B_W
OFF_D = OFF_C + C_W
OFF_G = OFF_D + D_W
IN_W = OFF_G + G_W
N_STATES = 7

kernel_name = "hybrid_rwkv7_retnet_rglru_gdn_step"

def _f32(t):
    return t.astype(jnp.float32)

def rms_norm(x, gain=None, eps=EPS):
    xf = _f32(x)
    y = xf * lax.rsqrt(jnp.mean(xf * xf, axis=-1, keepdims=True) + eps)
    return y if gain is None else y * gain

def l2_normalize(x, eps=EPS):
    return x * lax.rsqrt(jnp.sum(x * x, axis=-1, keepdims=True) + eps)

def heads(t):
    return t.reshape(t.shape[:-1] + (N_HEADS, HEAD_DIM))

def chunk_len(T, C):
    return C if T % C == 0 else T

def to_chunks(t, C):
    B, T, H = t.shape[:3]
    t = t.reshape((B, T // C, C, H) + t.shape[3:])
    return jnp.moveaxis(t, (1, 3), (0, 2))

def from_chunks(t):
    t = jnp.moveaxis(t, (0, 2), (1, 3))
    B, n, C, H, D = t.shape
    return t.reshape(B, n * C, H, D)

def causal_conv(u, buf, w):
    T = u.shape[1]
    full = jnp.concatenate([_f32(buf), u], axis=1)
    out = sum(full[:, j:j + T] * w[j] for j in range(CONV_W))
    return out, full[:, T:]

def rotary(x, pos):
    half = HEAD_DIM // 2
    inv = ROPE_BASE ** (-jnp.arange(half, dtype=jnp.float32) / half)
    ang = pos.astype(jnp.float32)[:, None] * inv[None, :]
    cos = jnp.cos(ang)[None, :, None, :]
    sin = jnp.sin(ang)[None, :, None, :]
    x1, x2 = x[..., :half], x[..., half:]
    return jnp.concatenate([x1 * cos - x2 * sin, x1 * sin + x2 * cos], axis=-1)

def rwkv7_scan(r, w, k, v, a, b, S0):
    def step(S, inp):
        r_t, w_t, k_t, v_t, a_t, b_t = inp
        sa = jnp.einsum('bhvk,bhk->bhv', S, a_t)
        S = S * w_t[:, :, None, :] + sa[..., :, None] * b_t[..., None, :] + v_t[..., :, None] * k_t[..., None, :]
        return S, jnp.einsum('bhvk,bhk->bhv', S, r_t)
    xs = tuple(jnp.swapaxes(t, 0, 1) for t in (r, w, k, v, a, b))
    S, o = lax.scan(step, S0, xs)
    return jnp.swapaxes(o, 0, 1), S

def retention_chunked(q, k, v, log_gamma, S0, C):
    qc, kc, vc = (to_chunks(t, C) for t in (q, k, v))
    idx = jnp.arange(C, dtype=jnp.float32)
    rel = idx[:, None] - idx[None, :]
    causal = rel >= 0
    decay = jnp.where(causal, jnp.exp(log_gamma[:, None, None] * jnp.where(causal, rel, 0.0)), 0.0)
    q_dec = jnp.exp(log_gamma[:, None] * (idx + 1.0))[..., None]
    k_dec = jnp.exp(log_gamma[:, None] * (C - 1.0 - idx))[..., None]
    g_c = jnp.exp(log_gamma * C)[:, None, None]

    def step(S, inp):
        q_i, k_i, v_i = inp
        s_in = jnp.einsum('bhid,bhjd->bhij', q_i, k_i) * decay
        o = jnp.einsum('bhij,bhjv->bhiv', s_in, v_i) + jnp.einsum('bhik,bhkv->bhiv', q_i, S) * q_dec
        S = S * g_c + jnp.einsum('bhjk,bhjv->bhkv', k_i * k_dec, v_i)
        return S, o
    S, o = lax.scan(step, S0, (qc, kc, vc))
    return from_chunks(o), S

def gated_delta_chunked(q, k, v, g, beta, S0, C):
    qc, kc, vc = (to_chunks(t, C) for t in (q, k, v))
    gc = jnp.cumsum(to_chunks(g, C), axis=-1)
    bc = to_chunks(beta, C)
    idx = jnp.arange(C)
    lower = idx[:, None] >= idx[None, :]
    strict = idx[:, None] > idx[None, :]
    diff = gc[..., :, None] - gc[..., None, :]
    decay = jnp.where(lower, jnp.exp(jnp.where(lower, diff, 0.0)), 0.0)
    kb = kc * bc[..., None]
    a_mat = jnp.where(strict, jnp.einsum('nbhid,nbhjd->nbhij', kb, kc) * decay, 0.0)
    m = a_mat + jnp.eye(C, dtype=a_mat.dtype)
    u = lax.linalg.triangular_solve(m, vc * bc[..., None], left_side=True, lower=True)
    w = lax.linalg.triangular_solve(m, kb * jnp.exp(gc)[..., None], left_side=True, lower=True)
    qk = jnp.einsum('nbhid,nbhjd->nbhij', qc, kc) * decay
    g_last = gc[..., -1]
    k_out = kc * jnp.exp(g_last[..., None] - gc)[..., None]
    q_in = qc * jnp.exp(gc)[..., None]

    def step(S, inp):
        u_i, w_i, qk_i, q_i, k_i, gl_i = inp
        v_new = u_i - jnp.einsum('bhik,bhkv->bhiv', w_i, S)
        o = jnp.einsum('bhik,bhkv->bhiv', q_i, S) + jnp.einsum('bhij,bhjv->bhiv', qk_i, v_new)
        S = S * jnp.exp(gl_i)[..., None, None] + jnp.einsum('bhik,bhiv->bhkv', k_i, v_new)
        return S, o
    S, o = lax.scan(step, S0, (u, w, qk, q_in, k_out, g_last))
    return from_chunks(o), S

def rwkv7_branch(p, wkv0, shift0, mu, w0, w2, a0, a2, k_k, k_a, r_k, ln_g, ln_b):
    pa, z = p[..., :A_SHIFT_W], p[..., A_SHIFT_W:]
    prev = jnp.concatenate([_f32(shift0)[:, None], pa[:, :-1]], axis=1)
    pm = pa + (prev - pa) * mu
    r, k, v = (pm[..., i * W_MIX:(i + 1) * W_MIX] for i in range(3))
    wd = pm[..., 3 * W_MIX:3 * W_MIX + RWKV_LORA_W]
    ad = pm[..., 3 * W_MIX + RWKV_LORA_W:]
    w_log = -jax.nn.softplus(-(w0 + jnp.tanh(wd) @ w2)) - 0.5
    decay = jnp.exp(-jnp.exp(w_log))
    a = jax.nn.sigmoid(a0 + ad @ a2)
    kk = l2_normalize(heads(k * k_k))
    k = k * (1.0 + (a - 1.0) * k_a)
    r_h, k_h, v_h, a_h = heads(r), heads(k), heads(v), heads(a)
    o, wkv1 = rwkv7_scan(r_h, heads(decay), k_h, v_h, -kk, kk * a_h, _f32(wkv0))
    mean = jnp.mean(o, axis=-1, keepdims=True)
    var = jnp.mean(jnp.square(o - mean), axis=-1, keepdims=True)
    o = ((o - mean) * lax.rsqrt(var + RWKV_GN_EPS)).reshape(z.shape) * ln_g + ln_b
    bonus = (jnp.sum(r_h * k_h * r_k, axis=-1, keepdims=True) * v_h).reshape(z.shape)
    out = (o + bonus) * jax.nn.silu(z)
    return out, wkv1.astype(wkv0.dtype), pa[:, -1].astype(shift0.dtype)

def retention_branch(p, S0, pos):
    T = p.shape[1]
    q, k, v, z = (p[..., i * W_MIX:(i + 1) * W_MIX] for i in range(4))
    q = rotary(heads(q), pos)
    k = rotary(heads(k), pos) * HEAD_DIM ** -0.5
    log_gamma = jnp.log(1.0 - 2.0 ** (-5.0 - jnp.arange(N_HEADS, dtype=jnp.float32)))
    o, S1 = retention_chunked(q, k, heads(v), log_gamma, _f32(S0), chunk_len(T, RET_CHUNK))
    out = rms_norm(o).reshape(z.shape) * jax.nn.silu(z)
    return out, S1.astype(S0.dtype)

def rglru_branch(p, h0, conv0, conv_w, conv_b, gate_w, gate_b, lam):
    xr, z = p[..., :W_MIX], p[..., W_MIX:]
    xc, conv1 = causal_conv(xr, conv0, conv_w)
    xc = xc + conv_b
    gates = jnp.einsum('btnd,gnde->gbtne', heads(xc), gate_w)
    gates = gates.reshape((2,) + xc.shape) + gate_b[:, None, None, :]
    r_gate, i_gate = jax.nn.sigmoid(gates[0]), jax.nn.sigmoid(gates[1])
    log_a = -LRU_C * r_gate * jax.nn.softplus(-lam)
    a = jnp.exp(log_a)
    b = jnp.sqrt(-jnp.expm1(2.0 * log_a)) * (i_gate * xc)
    b = b.at[:, 0].add(a[:, 0] * _f32(h0))

    def combine(e1, e2):
        return (e1[0] * e2[0], e2[0] * e1[1] + e2[1])
    _, h = lax.associative_scan(combine, (a, b), axis=1)
    out = h * jax.nn.silu(z)
    return out, h[:, -1].astype(h0.dtype), conv1.astype(conv0.dtype)

def gdn_branch(p, S0, conv0, conv_w, A_log, dt_bias, norm_g):
    T = p.shape[1]
    qkv_raw = p[..., :D_QKV_W]
    b_raw = p[..., D_QKV_W:D_QKV_W + N_HEADS]
    a_raw = p[..., D_QKV_W + N_HEADS:D_QKV_W + 2 * N_HEADS]
    z = p[..., D_QKV_W + 2 * N_HEADS:]
    qkv, conv1 = causal_conv(qkv_raw, conv0, conv_w)
    qkv = jax.nn.silu(qkv)
    q = l2_normalize(heads(qkv[..., :W_MIX])) * HEAD_DIM ** -0.5
    k = l2_normalize(heads(qkv[..., W_MIX:2 * W_MIX]))
    v = heads(qkv[..., 2 * W_MIX:])
    beta = jax.nn.sigmoid(b_raw)
    g = -jnp.exp(A_log) * jax.nn.softplus(a_raw + dt_bias)
    o, S1 = gated_delta_chunked(q, k, v, g, beta, _f32(S0), chunk_len(T, GDN_CHUNK))
    out = rms_norm(o, norm_g).reshape(z.shape) * jax.nn.silu(z)
    return out, S1.astype(S0.dtype), conv1.astype(conv0.dtype)

def mixer_layer(x, c, pos, st, lp):
    wkv0, shift0, ret0, lru_h0, lru_conv0, gdn0, gdn_conv0 = st
    B, T, _ = x.shape
    mod = jax.nn.silu(_f32(c)) @ lp['ada_w'] + lp['ada_b']
    shift, scale, gate = jnp.split(mod, 3, axis=-1)
    h = rms_norm(x, lp['norm_g']) * (1.0 + scale[:, None]) + shift[:, None]
    proj = jnp.einsum('btd,de->bte', h, lp['w_in'])
    oA, wkv1, shift1 = rwkv7_branch(proj[..., OFF_A:OFF_B], wkv0, shift0, lp['rwkv_mu'], lp['rwkv_w0'],
                                    lp['rwkv_w2'], lp['rwkv_a0'], lp['rwkv_a2'], lp['rwkv_k_k'],
                                    lp['rwkv_k_a'], lp['rwkv_r_k'], lp['rwkv_ln_g'], lp['rwkv_ln_b'])
    oB, ret1 = retention_branch(proj[..., OFF_B:OFF_C], ret0, pos)
    oC, lru_h1, lru_conv1 = rglru_branch(proj[..., OFF_C:OFF_D], lru_h0, lru_conv0, lp['lru_conv_w'],
                                         lp['lru_conv_b'], lp['lru_gate_w'], lp['lru_gate_b'], lp['lru_lambda'])
    oD, gdn1, gdn_conv1 = gdn_branch(proj[..., OFF_D:OFF_G], gdn0, gdn_conv0, lp['gdn_conv_w'],
                                     lp['gdn_A_log'], lp['gdn_dt_bias'], lp['gdn_norm_g'])
    branches = jnp.stack([oA, oB, oC, oD], axis=2)
    up = jnp.einsum('btnw,nwd->btnd', branches, lp['w_up'])
    gl = proj[..., OFF_G:].reshape(B, T, N_BRANCH, D_MODEL)
    merged = jnp.sum(jax.nn.sigmoid(gl) * up, axis=2)
    out = merged @ lp['w_out']
    x_new = (_f32(x) + gate[:, None] * out).astype(x.dtype)
    return x_new, (wkv1, shift1, ret1, lru_h1, lru_conv1, gdn1, gdn_conv1)

def run_trunk(x, c, pos, layer_states, layer_params, final_g):
    new = []
    for l in range(DEPTH):
        x, st = mixer_layer(x, c, pos, layer_states[l], layer_params[l])
        new.append(st)
    stacked = [jnp.stack([s[i] for s in new], axis=0) for i in range(N_STATES)]
    y = rms_norm(x, _f32(final_g)).astype(x.dtype)
    return y, stacked

def setup_inputs(seed: int = 0) -> dict:
    key = jax.random.key(seed)
    ks = iter(jax.random.split(key, 48))
    f32 = jnp.float32

    def nrm(shape, s):
        return s * jax.random.normal(next(ks), shape, f32)

    def unif(shape, lo, hi):
        return jax.random.uniform(next(ks), shape, f32, lo, hi)

    L, D, W = DEPTH, D_MODEL, W_MIX
    s_lru = unif((L, W), 0.9, 0.999) ** (1.0 / LRU_C)
    dt = jnp.exp(unif((L, N_HEADS), float(np.log(1e-3)), float(np.log(1e-1))))
    return {
        'x_prompt': nrm((BATCH, SEQ, D), 1.0),
        'x_sample': nrm((DEC_BATCH, DEC_SEQ, D), 1.0),
        'c_prompt': nrm((BATCH, D), 1.0),
        'c_sample': nrm((DEC_BATCH, D), 1.0),
        'state_rwkv_wkv': nrm((L, DEC_BATCH, N_HEADS, HEAD_DIM, HEAD_DIM), 0.1),
        'state_rwkv_shift': nrm((L, DEC_BATCH, A_SHIFT_W), 1.0),
        'state_ret': nrm((L, DEC_BATCH, N_HEADS, HEAD_DIM, HEAD_DIM), 0.5),
        'state_lru_h': nrm((L, DEC_BATCH, W), 0.5),
        'state_lru_conv': nrm((L, DEC_BATCH, CONV_W - 1, W), 1.0),
        'state_gdn': nrm((L, DEC_BATCH, N_HEADS, HEAD_DIM, HEAD_DIM), 0.1),
        'state_gdn_conv': nrm((L, DEC_BATCH, CONV_W - 1, D_QKV_W), 1.0),
        'ada_w': nrm((L, D, 3 * D), 0.5 * D ** -0.5),
        'ada_b': nrm((L, 3 * D), 0.02),
        'norm_g': 1.0 + nrm((L, D), 0.02),
        'w_in': nrm((L, D, IN_W), D ** -0.5),
        'rwkv_mu': unif((L, A_SHIFT_W), 0.0, 1.0),
        'rwkv_w0': unif((L, W), -6.0, 0.0),
        'rwkv_w2': nrm((L, RWKV_LORA_W, W), 0.5 * RWKV_LORA_W ** -0.5),
        'rwkv_a0': nrm((L, W), 0.1),
        'rwkv_a2': nrm((L, RWKV_LORA_A, W), 0.5 * RWKV_LORA_A ** -0.5),
        'rwkv_k_k': 0.85 + nrm((L, W), 0.02),
        'rwkv_k_a': 1.0 + nrm((L, W), 0.02),
        'rwkv_r_k': nrm((L, N_HEADS, HEAD_DIM), 0.1),
        'rwkv_ln_g': 1.0 + nrm((L, W), 0.02),
        'rwkv_ln_b': nrm((L, W), 0.02),
        'lru_conv_w': nrm((L, CONV_W, W), 0.5),
        'lru_conv_b': nrm((L, W), 0.02),
        'lru_gate_w': nrm((L, 2, N_HEADS, HEAD_DIM, HEAD_DIM), HEAD_DIM ** -0.5),
        'lru_gate_b': nrm((L, 2, W), 0.02),
        'lru_lambda': jnp.log(s_lru) - jnp.log1p(-s_lru),
        'gdn_conv_w': nrm((L, CONV_W, D_QKV_W), 0.5),
        'gdn_A_log': jnp.log(unif((L, N_HEADS), 1.0, 16.0)),
        'gdn_dt_bias': dt + jnp.log(-jnp.expm1(-dt)),
        'gdn_norm_g': 1.0 + nrm((L, HEAD_DIM), 0.02),
        'w_up': nrm((L, N_BRANCH, W, D), W ** -0.5),
        'w_out': nrm((L, D, D), D ** -0.5),
        'final_g': 1.0 + nrm((D,), 0.02),
    }

def reference(x_prompt, x_sample, c_prompt, c_sample, state_rwkv_wkv, state_rwkv_shift, state_ret,
              state_lru_h, state_lru_conv, state_gdn, state_gdn_conv, ada_w, ada_b, norm_g, w_in,
              rwkv_mu, rwkv_w0, rwkv_w2, rwkv_a0, rwkv_a2, rwkv_k_k, rwkv_k_a, rwkv_r_k, rwkv_ln_g,
              rwkv_ln_b, lru_conv_w, lru_conv_b, lru_gate_w, lru_gate_b, lru_lambda, gdn_conv_w,
              gdn_A_log, gdn_dt_bias, gdn_norm_g, w_up, w_out, final_g):
    layer_params = [dict(
        ada_w=_f32(ada_w[l]), ada_b=_f32(ada_b[l]), norm_g=_f32(norm_g[l]), w_in=_f32(w_in[l]),
        rwkv_mu=_f32(rwkv_mu[l]), rwkv_w0=_f32(rwkv_w0[l]), rwkv_w2=_f32(rwkv_w2[l]),
        rwkv_a0=_f32(rwkv_a0[l]), rwkv_a2=_f32(rwkv_a2[l]), rwkv_k_k=_f32(rwkv_k_k[l]),
        rwkv_k_a=_f32(rwkv_k_a[l]), rwkv_r_k=_f32(rwkv_r_k[l]), rwkv_ln_g=_f32(rwkv_ln_g[l]),
        rwkv_ln_b=_f32(rwkv_ln_b[l]), lru_conv_w=_f32(lru_conv_w[l]), lru_conv_b=_f32(lru_conv_b[l]),
        lru_gate_w=_f32(lru_gate_w[l]), lru_gate_b=_f32(lru_gate_b[l]), lru_lambda=_f32(lru_lambda[l]),
        gdn_conv_w=_f32(gdn_conv_w[l]), gdn_A_log=_f32(gdn_A_log[l]), gdn_dt_bias=_f32(gdn_dt_bias[l]),
        gdn_norm_g=_f32(gdn_norm_g[l]), w_up=_f32(w_up[l]), w_out=_f32(w_out[l]))
        for l in range(DEPTH)]

    dt_p = x_prompt.dtype
    zero_states = [(
        jnp.zeros((BATCH, N_HEADS, HEAD_DIM, HEAD_DIM), dt_p),
        jnp.zeros((BATCH, A_SHIFT_W), dt_p),
        jnp.zeros((BATCH, N_HEADS, HEAD_DIM, HEAD_DIM), dt_p),
        jnp.zeros((BATCH, W_MIX), dt_p),
        jnp.zeros((BATCH, CONV_W - 1, W_MIX), dt_p),
        jnp.zeros((BATCH, N_HEADS, HEAD_DIM, HEAD_DIM), dt_p),
        jnp.zeros((BATCH, CONV_W - 1, D_QKV_W), dt_p)) for _ in range(DEPTH)]
    pos_p = jnp.arange(SEQ, dtype=jnp.int32)
    y_prompt, new_p = run_trunk(x_prompt, c_prompt, pos_p, zero_states, layer_params, final_g)
    p_wkv, p_shift, p_ret, p_lru_h, p_lru_conv, p_gdn, p_gdn_conv = new_p

    carried = [(state_rwkv_wkv[l], state_rwkv_shift[l], state_ret[l], state_lru_h[l], state_lru_conv[l],
                state_gdn[l], state_gdn_conv[l]) for l in range(DEPTH)]
    pos_s = PAST_LEN + jnp.arange(DEC_SEQ, dtype=jnp.int32)
    y_sample, new_s = run_trunk(x_sample, c_sample, pos_s, carried, layer_params, final_g)
    s_wkv, s_shift, s_ret, s_lru_h, s_lru_conv, s_gdn, s_gdn_conv = new_s

    return (y_prompt, y_sample, p_wkv, p_shift, p_ret, p_lru_h, p_lru_conv, p_gdn, p_gdn_conv,
            s_wkv, s_shift, s_ret, s_lru_h, s_lru_conv, s_gdn, s_gdn_conv)


_drawn_inputs = setup_inputs


def setup_inputs(seed=0):
    import zlib

    import numpy as np

    out = dict(_drawn_inputs(seed))
    spreads = {}
    factors = {'rwkv_ln_g': 8.0,
     'rwkv_ln_b': 8.0,
     'lru_gate_b': 6.303,
     'gdn_norm_g': 8.0,
     'final_g': 2.694}
    for name, (base, spread) in spreads.items():
        noise = np.random.default_rng([zlib.crc32(name.encode()), seed]).standard_normal(out[name].shape)
        drawn = base * np.exp(spread * noise) if base else spread * noise
        out[name] = __import__('jax').numpy.asarray(drawn.astype(out[name].dtype))
    for name, factor in factors.items():
        out[name] = (out[name] * factor).astype(out[name].dtype)
    return out
```

```python
import concourse.bass as bass
from concourse import mybir
from contextlib import ExitStack

D_MODEL, SEQ, DEPTH, NB = 1024, 512, 2, 8
HEADS, HD = 4, 64
W = HEADS * HD
LORA = 64
CONV = 4
A_SHIFT = 3 * W + 2 * LORA
QKV = 3 * W
OFF_B = A_SHIFT + W
OFF_C = OFF_B + 4 * W
OFF_D = OFF_C + 2 * W
OFF_BA = OFF_D + QKV
OFF_DZ = OFF_BA + 2 * HEADS
OFF_G = OFF_DZ + W
IN_W = OFF_G + 4 * D_MODEL
P = 128
KT = D_MODEL // P
TT = SEQ + NB
HALF = TT // 2
C = 128
NC = SEQ // C
RING = 4
W_DECAY = -0.5 * 0.6065306597126334
LRU_C = 8.0

CONST_COLS = {}
_at = 0
for _name, _n in (("ident", 128), ("bones", 128), ("ones", 128), ("rotp", 128), ("rmask", 512), ("negm", 128),
                  ("rdec", 512), ("qdec", 256), ("cos", TT), ("sin", TT), ("reset", TT), ("sel4", 512),
                  ("sel2", 256), ("kdec", 4), ("gc", 2), ("gam", 1), ("eps", 1), ("epsgn", 1)):
    CONST_COLS[_name] = (_at, _at + _n)
    _at += _n
CONST_N = _at

PARAM_ROWS = {}
_at = 0
for _name, _n in (("ada_b", 24), ("norm_g", 8), ("mu", 7), ("w0", 2), ("a0", 2), ("k_k", 2), ("k_a", 2), ("r_k", 2),
                  ("ln_g", 2), ("ln_b", 2), ("lru_w", 8), ("lru_b", 2), ("gate_b", 4), ("lam", 2), ("gdn_w", 24),
                  ("gdn_g", 1), ("final_g", 8)):
    PARAM_ROWS[_name] = _at
    _at += _n
PARAM_N = _at


class Track:

    def __init__(self, sem, order):
        self.sem, self.order, self.n, self.where = sem, order, 0, {}
        for i, name in enumerate(order or []):
            self.where.setdefault(name, []).append(i + 1)
        self.made = []

    def step(self, name):
        self.n += 1
        self.made.append(name)
        if self.order is not None:
            assert self.order[self.n - 1] == name, (name, self.n, self.order[self.n - 1])
        return self.sem, 1

    def at(self, name, i=0):
        if self.order is None:
            return self.sem, 1
        return self.sem, self.where[name][i]


def build_program(nc, a, o, order):
    F32, U8 = mybir.dt.float32, mybir.dt.uint8
    ALU, ACT, AX = mybir.AluOpType, mybir.ActivationFunctionType, mybir.AxisListType
    mult, add, sub = ALU.mult, ALU.add, ALU.subtract
    ctx = ExitStack()
    tracks = {}
    with ctx:
        def sb(name, shape, dt=F32):
            return ctx.enter_context(nc.sbuf_tensor(name, shape, dt))

        def sem(name):
            return ctx.enter_context(nc.semaphore(name))

        def track(name):
            tracks[name] = Track(sem(name), order.get(name) if order else None)
            return tracks[name]

        cst = sb("cst", [P, CONST_N])
        tmask = sb("tmask", [P, 14, P], U8)
        xT = sb("xT", [P, KT, TT])
        hT = sb("hT", [P, KT, TT])
        RA = sb("RA", [P, 9, TT])
        RB = sb("RB", [P, 8, TT])
        RC = sb("RC", [P, 4, TT])
        RD = sb("RD", [P, 8, TT])
        ws = sb("ws", [P, 18, TT])
        bg = sb("bg", [36, TT])
        ring = sb("ring", [P, RING, KT, P])
        upw = sb("upw", [P, RING, 2, P])
        rs = sb("rs", [P, TT])
        parT = sb("parT", [P, P])
        prow = sb("prow", [P, P])
        der = sb("der", [P, 40])
        stT = sb("stT", [P, 7, 64])
        srow = ws[0:64, 0:2, :].rearrange("p a b -> p (a b)")[:, 0:A_SHIFT]
        modT = sb("modT", [P, 24, 9])
        G = sb("G", [P, KT, 9])
        cT = sb("cT", [P, KT, 9])
        w2 = sb("w2", [P, W])
        gw = sb("gw", [P, 4, P])
        crow = sb("crow", [11, 15 * P])
        hrow = sb("hrow", [9, W])
        svA = sb("svA", [P, 6, NB, 2])
        svB = sb("svB", [P, 8, NB, 2])
        rowA = sb("rowA", [96, P])
        rowB = sb("rowB", [P, P])
        vecA = sb("vecA", [P, 6, HD])
        vecB = sb("vecB", [P, 8, HD])
        vv = sb("vv", [P, 3, 16])
        so = sb("so", [P, 3, 16])
        sa = sb("sa", [P, 2, 16])
        orow = sb("orow", [24, W])
        Mst = [sb(f"M{n}", [P, 2, HD]) for n in range(3)]
        mid = sb("mid", [P, 2, NC])
        pc = sb("pc", [P, 4, 2, NC])
        gp = sb("gp", [36, 4])
        colbg = sb("colbg", [P, 36])
        kdl = sb("kdl", [P, 8])
        mrow = sb("mrow", [HD, 2, P])
        psA = ctx.enter_context(nc.psum_tensor("psA", [P, 4, 512], F32))
        psB = ctx.enter_context(nc.psum_tensor("psB", [P, 4, 512], F32))
        scrA = nc.dram_tensor("scr_a", (6, NB, W), F32).ap()
        scrB = nc.dram_tensor("scr_b", (8, NB, W), F32).ap()
        scrO = nc.dram_tensor("scr_o", (3, NB, W), F32).ap()

        def cc(name, p0=0, p1=P):
            lo, hi = CONST_COLS[name]
            return cst[p0:p1, lo:hi]

        def par(name, j=0, n=1):
            r = PARAM_ROWS[name] + j
            return parT[:, r:r + n]

        def bc(ap, axis, n):
            ap = ap.unsqueeze(axis)
            s = list(ap.shape)
            s[axis] = n
            return ap.broadcast_to(s)

        ident, bones, ones = cc("ident"), cc("bones"), cc("ones")
        wf = ws[:, :, :].rearrange("p a b -> p (a b)")

        def wv(tile, n):
            return wf[:, tile * TT:tile * TT + n]

        q4 = lambda ap: ap.rearrange("p i (h c) -> p (i h) c", h=2)

        s_out, s_scr, s_vec, s_ss, s_oread, s_y = (sem(n) for n in ("outputs_written", "scratch_written", "decode_vectors_in",
                                                                    "decode_states_in", "decode_rows_in", "y_written"))
        N_OUTPUTS, N_VEC, N_SS = 26, 20, 12
        s_const, s_x, s_par, s_st, s_w2 = (sem(n) for n in ("const_in", "x_in", "params_in", "states_in", "small_weights_in"))
        s_w = [sem(f"ring_in{i}") for i in range(RING)]
        s_zero = sem("zeroed")
        s_seen = sem("register_wait_passed")
        TR = {n: track(n) for n in ("pe0", "act0", "dve0", "pe_f", "act_f", "dve_f", "pe_a", "act_a", "dve_a", "pe_d", "act_d",
                                    "dve_d", "pe_b", "act_b", "dve_b", "pe_c", "act_c", "dve_c", "pe_s", "act_s", "dve_s",
                                    "pool", "pe_m", "act_m", "dve_m", "pe9", "act9", "dve9")}
        pe0, act0, dve0 = TR["pe0"], TR["act0"], TR["dve0"]

        PROJ = ([(j * P, "A", j) for j in range(9)] + [(OFF_D + j * P, "D", j) for j in range(6)] + [(OFF_BA, "ba", 0)]
                + [(OFF_DZ + j * P, "D", 6 + j) for j in range(2)] + [(OFF_B + j * P, "B", j) for j in range(8)]
                + [(OFF_C + j * P, "C", j) for j in range(4)])
        N_ADA, N_PROJ, N_GATE, N_OUT = 24, len(PROJ), 4 * KT, KT
        R_PROJ, R_GATE, R_OUT = N_ADA, N_ADA + N_PROJ, N_ADA + N_PROJ + N_GATE
        N_RING = R_OUT + N_OUT
        RAW = {"A": RA, "B": RB, "C": RC, "D": RD}

        def ring_loads(r):
            n = 0
            for q in range(r % RING, r + 1, RING):
                n += 2 if (R_GATE <= q < R_OUT or (R_PROJ <= q < R_GATE and PROJ[q - R_PROJ][1] == "ba")) else 1
            return 16 * n

        with nc.Block() as block:
            @block.sync
            def _(sp):
                sp.dma_start(cst[:], a["consts"]).then_inc(s_const, 16)
                sp.dma_start(wv(10, 14 * P), a["tree_masks"]).then_inc(s_const, 16)
                for t in range(4):
                    sp.dma_start(hT[:, 2 * t:2 * t + 2, 0:512], a["x_prompt"][0, t * P:(t + 1) * P, :].rearrange("p (a c) -> p a c", a=2)).then_inc(s_x, 16)
                sp.dma_start(ws[0:8, 0:2, 0:512], a["x_sample"][:, 0, :].rearrange("p (a c) -> p a c", a=2)).then_inc(s_x, 16)
                sp.dma_start(ws[0:8, 2:4, 0:512], a["c_sample"].rearrange("p (a c) -> p a c", a=2)).then_inc(s_x, 16)
                sp.dma_start(ws[8:9, 2:4, 0:512], a["c_prompt"].rearrange("p (a c) -> p a c", a=2)).then_inc(s_x, 16)

            @block.gpsimd
            def _(pool):
                nc.gpsimd.memset(gw[:], 0.0).then_inc(s_zero, 1)
                nc.gpsimd.memset(bg[:], 0.0).then_inc(s_zero, 1)
                pool.wait_ge(s_zero, 2)

            @block.scalar
            def _(act):
                act.wait_ge(s_x, 16 * 7)
                nc.scalar.activation(ws[0:9, 4:6, 0:512], ws[0:9, 2:4, 0:512], ACT.Tanh, scale=0.5).then_inc(*act0.step("tanh_c"))
                for d in range(KT):
                    act.wait_ge(*pe0.at("x", d))
                    nc.scalar.copy(xT[:, d, 0:SEQ], psA[:, d % 4, :]).then_inc(*act0.step("x"))

            @block.vector
            def _(dve):
                dve.wait_ge(s_const, 32)
                nc.vector.tensor_copy(tmask[:], wv(10, 14 * P).rearrange("p (m t) -> p m t", m=14)).then_inc(*dve0.step("tmask"))
                dve.wait_ge(*act0.at("tanh_c"))
                nc.vector.scalar_tensor_tensor(ws[0:9, 4:6, 0:512], ws[0:9, 4:6, 0:512], 1.0, ws[0:9, 2:4, 0:512], add, mult).then_inc(*dve0.step("silu_c"))
                dve.wait_ge(*pe0.at("xs"))
                nc.vector.tensor_copy(xT[:, :, SEQ:TT], psB[:, 0, 0:64].rearrange("p (d b) -> p d b", d=KT)).then_inc(*dve0.step("xs"))
                dve.wait_ge(*pe0.at("c"))
                nc.vector.tensor_scalar(cT[:], psB[:, 1, 0:72].rearrange("p (d b) -> p d b", d=KT), 0.5, None, mult).then_inc(*dve0.step("c"))
                dve.wait_ge(*dve0.at("c"))

            @block.tensor
            def _(pe):
                pe.wait_ge(s_const, 32)
                pe.wait_ge(s_x, 16 * 7)
                for d in range(KT):
                    last = nc.tensor.transpose(psB[:, 0, 8 * d:8 * d + 8], ws[0:8, d // 4, (d % 4) * P:(d % 4 + 1) * P], ident[0:8, 0:8])
                last.then_inc(*pe0.step("xs"))
                pe.wait_ge(*dve0.at("silu_c"))
                for d in range(KT):
                    last = nc.tensor.transpose(psB[:, 1, 9 * d:9 * d + 9], ws[0:9, 4 + d // 4, (d % 4) * P:(d % 4 + 1) * P], ident[0:9, 0:9])
                last.then_inc(*pe0.step("c"))
                for d in range(KT):
                    if d >= 4:
                        pe.wait_ge(*act0.at("x", d - 4))
                    for t in range(4):
                        last = nc.tensor.transpose(psA[:, d % 4, t * P:(t + 1) * P], hT[:, 2 * t + d // 4, (d % 4) * P:(d % 4 + 1) * P], ident)
                    last.then_inc(*pe0.step("x"))

        nc.all_engine_barrier()

        with nc.Fori(0, DEPTH) as layer:
            with nc.Block() as block:
                pe_f, act_f, dve_f = TR["pe_f"], TR["act_f"], TR["dve_f"]
                pool_t = TR["pool"]

                def ring_done(r):
                    if r < R_PROJ:
                        return pe_f.at("ada", r)
                    if r < R_GATE:
                        return pe_f.at("proj", r - R_PROJ)
                    if r < R_OUT:
                        return TR["pe_m"].at("gate", r - R_GATE)
                    return TR["pe_m"].at("out", r - R_OUT)

                @block.sync
                def _(sp):
                    vec1 = [("ada_b", 24), ("norm_g", 8), ("rwkv_mu", 7), ("rwkv_w0", 2), ("rwkv_a0", 2), ("rwkv_k_k", 2),
                            ("rwkv_k_a", 2)]
                    rows = {"ada_b": "ada_b", "norm_g": "norm_g", "rwkv_mu": "mu", "rwkv_w0": "w0", "rwkv_a0": "a0",
                            "rwkv_k_k": "k_k", "rwkv_k_a": "k_a", "rwkv_ln_g": "ln_g", "rwkv_ln_b": "ln_b",
                            "lru_conv_b": "lru_b", "lru_lambda": "lam"}
                    for name, row in rows.items():
                        n = a[name].shape[1] // P
                        r0 = PARAM_ROWS[row]
                        sp.dma_start(prow[r0:r0 + n, :], a[name][layer].rearrange("(j p) -> j p", p=P)).then_inc(s_par, 16)
                    r0 = PARAM_ROWS["r_k"]
                    sp.dma_start(prow[r0:r0 + 2, :], a["rwkv_r_k"][layer].rearrange("(i g) d -> i (g d)", i=2)).then_inc(s_par, 16)
                    for name, row, n in (("lru_conv_w", "lru_w", 8), ("lru_gate_b", "gate_b", 4), ("gdn_conv_w", "gdn_w", 24)):
                        r0 = PARAM_ROWS[row]
                        sp.dma_start(prow[r0:r0 + n, :], a[name][layer].rearrange("t (j p) -> (t j) p", p=P)).then_inc(s_par, 16)
                    r0 = PARAM_ROWS["gdn_g"]
                    for g in range(2):
                        sp.dma_start(prow[r0:r0 + 1, g * HD:(g + 1) * HD], a["gdn_norm_g"][layer].unsqueeze(0)).then_inc(s_par, 16)
                    r0 = PARAM_ROWS["final_g"]
                    sp.dma_start(prow[r0:r0 + 8, :], a["final_g"].rearrange("(j p) -> j p", p=P)).then_inc(s_par, 16)
                    n_par = len(rows) + 1 + 3 + 2 + 1
                    sp.wait_ge(*dve_f.at("zero"))
                    sp.dma_start(srow[0:8, :], a["state_rwkv_shift"][layer]).then_inc(s_st, 16)
                    sp.dma_start(srow[8:16, 0:W], a["state_lru_h"][layer]).then_inc(s_st, 16)
                    sp.dma_start(srow[16:40, 0:W], a["state_lru_conv"][layer].rearrange("b t c -> (b t) c")).then_inc(s_st, 16)
                    sp.dma_start(srow[40:64, 0:QKV], a["state_gdn_conv"][layer].rearrange("b t c -> (b t) c")).then_inc(s_st, 16)
                    sp.dma_start(w2[0:64, :], a["rwkv_w2"][layer]).then_inc(s_w2, 16)
                    sp.dma_start(w2[64:128, :], a["rwkv_a2"][layer]).then_inc(s_w2, 16)
                    for g in range(2):
                        for hf in range(2):
                            sp.dma_start(gw[hf * HD:(hf + 1) * HD, 2 * g:2 * g + 2, hf * HD:(hf + 1) * HD],
                                         a["lru_gate_w"][layer, g].rearrange("(i f) d e -> f d i e", f=2)[hf]).then_inc(s_w2, 16)
                    sp.dma_start(gp[32:36, 0:1], a["gdn_A_log"][layer].unsqueeze(1)).then_inc(s_w2, 16)
                    sp.dma_start(gp[32:36, 1:2], a["gdn_dt_bias"][layer].unsqueeze(1)).then_inc(s_w2, 16)
                    for r in range(N_RING):
                        s = r % RING
                        if r >= RING:
                            sp.wait_ge(*ring_done(r - RING))
                        if r < R_PROJ:
                            src = a["ada_w"][layer, :, r * P:(r + 1) * P]
                        elif r < R_GATE:
                            col, name, _ = PROJ[r - R_PROJ]
                            if name == "ba":
                                for e in range(2):
                                    sp.dma_start(ring[:, s, :, 32 * e:32 * e + HEADS],
                                                 a["w_in"][layer, :, col + HEADS * e:col + HEADS * (e + 1)]
                                                 .rearrange("(k p) c -> p k c", p=P)).then_inc(s_w[s], 16)
                                continue
                            src = a["w_in"][layer, :, col:col + P]
                        elif r < R_OUT:
                            jd, n = divmod(r - R_GATE, 4)
                            src = a["w_in"][layer, :, OFF_G + n * D_MODEL + jd * P:OFF_G + n * D_MODEL + (jd + 1) * P]
                            sp.dma_start(upw[:, s, :, :], a["w_up"][layer, n, :, jd * P:(jd + 1) * P]
                                         .rearrange("(i p) c -> p i c", p=P)).then_inc(s_w[s], 16)
                        else:
                            src = a["w_out"][layer, :, (r - R_OUT) * P:(r - R_OUT + 1) * P]
                        sp.dma_start(ring[:, s, :, :], src.rearrange("(k p) c -> p k c", p=P)).then_inc(s_w[s], 16)

                N_PAR, N_ST, N_W2 = 18, 4, 8

                @block.gpsimd
                def _(pool):
                    n_out = 0
                    pool.wait_ge(*TR["act_a"].at("crow"))
                    for dst, src in ((o["p_shift"][layer], crow[2:3, 0:A_SHIFT]),
                                     (o["s_shift"][layer], crow[3:11, 0:A_SHIFT]),
                                     (o["p_lru_conv"][layer, 0], crow[0:3, 7 * P:9 * P]),
                                     (o["s_lru_conv"][layer, :, 2, :], crow[3:11, 7 * P:9 * P]),
                                     (o["p_gdn_conv"][layer, 0], crow[0:3, 9 * P:15 * P]),
                                     (o["s_gdn_conv"][layer, :, 2, :], crow[3:11, 9 * P:15 * P]),
                                     (o["s_lru_conv"][layer, :, 0:2, :], a["state_lru_conv"][layer, :, 1:3, :]),
                                     (o["s_gdn_conv"][layer, :, 0:2, :], a["state_gdn_conv"][layer, :, 1:3, :])):
                        pool.dma_start(dst, src).then_inc(s_out, 16)
                        n_out += 1
                    pool.wait_ge(*TR["act_a"].at("mrow"))
                    for i in range(2):
                        pool.dma_start(o["p_wkv"][layer, 0, 2 * i:2 * i + 2].rearrange("g v k -> v g k"),
                                       mrow[:, i, :].rearrange("v (g k) -> v g k", g=2)).then_inc(s_out, 16)
                        n_out += 1
                    for key, t, m in (("p_gdn", TR["dve_d"], Mst[2]), ("p_ret", TR["dve_b"], Mst[1])):
                        pool.wait_ge(*t.at("st", NC - 1))
                        pool.dma_start(o[key][layer, 0].rearrange("(i g) k v -> (g k) i v", g=2), m[:]).then_inc(s_out, 16)
                        n_out += 1
                    pool.wait_ge(*TR["act_c"].at("hrow"))
                    pool.dma_start(o["p_lru_h"][layer], hrow[0:1, :]).then_inc(s_out, 16)
                    pool.dma_start(o["s_lru_h"][layer], hrow[1:9, :]).then_inc(s_out, 16)
                    n_out += 2
                    pool.wait_ge(*TR["dve_c"].at("h"))
                    ss = wf[:, 0:3072].rearrange("p (n x) -> p n x", n=3)
                    for q in range(4):
                        pool.dma_start(ss[32 * q:32 * q + 32, 0, :], a["state_rwkv_wkv"][layer].rearrange("b h (q v) k -> q (b h) (v k)", q=4)[q]).then_inc(s_ss, 16)
                        for n, key in ((1, "state_ret"), (2, "state_gdn")):
                            pool.dma_start(ss[32 * q:32 * q + 32, n, :].rearrange("p (k v) -> p k v", v=16),
                                           a[key][layer].rearrange("b h k (q v) -> q (b h) k v", q=4)[q]).then_inc(s_ss, 16)
                    pool.wait_ge(*TR["act_s"].at("rows"))
                    pool.dma_start(scrA.rearrange("n b (i c) -> (n b i) c", i=2), rowA[:]).then_inc(s_scr, 16)
                    pool.dma_start(scrB.rearrange("n b (i c) -> (n b i) c", i=2), rowB[:]).then_inc(s_scr, 16)
                    pool.wait_ge(s_scr, layer * 96 + 32)
                    pool.sem_inc(s_seen, 1)
                    for q in range(4):
                        pr = slice(32 * q, 32 * q + 32)
                        pool.dma_start(vecA[pr], scrA.rearrange("n b (h d) -> (b h) n d", h=HEADS)).then_inc(s_vec, 16)
                        pool.dma_start(vecB[pr], scrB.rearrange("n b (h d) -> (b h) n d", h=HEADS)).then_inc(s_vec, 16)
                        for m, (scr, n) in enumerate(((scrA, 3), (scrB, 2), (scrB, 5))):
                            pool.dma_start(vv[pr, m, :], scr[n].rearrange("b (h q v) -> q (b h) v", h=HEADS, q=4)[q]).then_inc(s_vec, 16)
                    pool.wait_ge(*TR["dve_s"].at("so"))
                    for q in range(4):
                        pr = slice(32 * q, 32 * q + 32)
                        pool.dma_start(scrO.rearrange("n b (h q v) -> q (b h) n v", h=HEADS, q=4)[q], so[pr]).then_inc(s_scr, 16)
                        pool.dma_start(o["s_wkv"][layer].rearrange("b h (q v) k -> q (b h) (v k)", q=4)[q], ss[pr, 0, :]).then_inc(s_out, 16)
                        for n, key in ((1, "s_ret"), (2, "s_gdn")):
                            pool.dma_start(o[key][layer].rearrange("b h k (q v) -> q (b h) k v", q=4)[q],
                                           ss[pr, n, :].rearrange("p (k v) -> p k v", v=16)).then_inc(s_out, 16)
                        n_out += 3
                    pool.wait_ge(s_scr, layer * 96 + 96)
                    pool.sem_inc(s_seen, 1)
                    pool.dma_start(orow[:], scrO.rearrange("n b c -> (n b) c")).then_inc(s_oread, 16)
                    assert n_out == N_OUTPUTS
                    pool.wait_ge(s_out, layer * (16 * N_OUTPUTS) + 16 * N_OUTPUTS)

                def headsum(src):
                    s4 = q4(src)
                    for k in range(4):
                        last = nc.tensor.matmul(psB[:, k, 0:HALF], bones, s4[:, k, :], start=True, stop=True)
                    return last

                def slot(h):
                    return 2 * (h % 2) + h // 2

                def hp(h):
                    return slice(HD * (h % 2), HD * (h % 2) + HD)

                def mats(base, sizes):
                    out, at = [], base
                    for n in sizes:
                        out.append(wf[:, at:at + n])
                        at += n
                    return out
                GRa, Ta, Va, Ya, rowsa, X1a, Ua = mats(0, (2048, 512, 512, 512, 768, 256, 256))
                Dd, GRd, Td, Vd, Yd, rowsd, X1d, Ud = mats(10 * TT, (512, 1024, 512, 512, 512, 512, 256, 256))
                h4 = lambda ap: ap.rearrange("p (h t) -> p h t", h=HEADS)
                GRa4, GRd4 = h4(GRa), h4(GRd)
                AtA, AtD = GRa4[:, :, 0:P], GRd4[:, :, 0:P]
                ARa = wv(10, 2048).rearrange("p (i c x t) -> p i c x t", i=2, c=NC, x=2)
                ARd = RD[:, 0:4, :].rearrange("p a b -> p (a b)")[:, 0:2048].rearrange("p (i c x t) -> p i c x t", i=2, c=NC, x=2)
                ch = lambda c: slice(c * C, (c + 1) * C)
                G1b, krb, vrb = mats(4 * TT, (512, 256, 256))

                def pe_tree(pe, tp, td, ta, At, T, V, Y, c):
                    T4, V4, Y4 = h4(T), h4(V), h4(Y)
                    for h in range(HEADS):
                        last = nc.tensor.matmul(psB[:, 2, h * P:(h + 1) * P], At[:, h, :], ident, start=True, stop=True)
                    last.then_inc(*tp.step("z"))
                    for lv in range(1, 7):
                        pe.wait_ge(*td.at("t", 7 * c + lv - 1))
                        for h in range(HEADS):
                            last = nc.tensor.matmul(psB[:, 3, h * P:(h + 1) * P], At[:, h, :], T4[:, h, :], start=True, stop=True)
                        last.then_inc(*tp.step("y"))
                        pe.wait_ge(*ta.at("y", 6 * c + lv - 1))
                        for h in range(HEADS):
                            if lv < 6:
                                nc.tensor.matmul(psB[:, 2, h * P:(h + 1) * P], V4[:, h, :], Y4[:, h, :], start=True, stop=True)
                            last = nc.tensor.matmul(psB[:, 1, h * P:(h + 1) * P], Y4[:, h, :], V4[:, h, :], start=True, stop=True)
                        last.then_inc(*tp.step("z"))

                def act_tree(act, tp, ta, Y, c):
                    for lv in range(1, 7):
                        act.wait_ge(*tp.at("y", 6 * c + lv - 1))
                        nc.scalar.copy(Y, psB[:, 3, :]).then_inc(*ta.step("y"))

                def dve_tree(dve, tp, td, At, T, V, c):
                    T4, V4 = h4(T), h4(V)
                    for lv in range(7):
                        dve.wait_ge(*tp.at("z", 7 * c + lv))
                        zt = At if lv == 0 else h4(psB[:, 1, :])
                        if lv < 6:
                            nc.vector.copy_predicated(T4, bc(tmask[:, lv, :], 1, HEADS), h4(psB[:, 2, :]))
                        nc.vector.copy_predicated(V4, bc(tmask[:, 7 + lv, :], 1, HEADS), zt).then_inc(*td.step("t"))
                        dve.wait_ge(*td.at("t", 7 * c + lv))

                @block.tensor
                def _(pe):
                    pa, pd, pb, pcc, pss, pm = (TR[n] for n in ("pe_a", "pe_d", "pe_b", "pe_c", "pe_s", "pe_m"))
                    pe.wait_ge(s_par, 16 * N_PAR)
                    nc.tensor.transpose(psB[:, 0, 0:PARAM_N], prow[0:PARAM_N, :], ident[0:PARAM_N, 0:PARAM_N]).then_inc(*pe_f.step("par"))
                    pe.wait_ge(s_st, 16 * N_ST)
                    for j in range(7):
                        last = nc.tensor.transpose(psB[:, 1, 64 * j:64 * j + 64], srow[:, j * P:(j + 1) * P], ident[0:64, 0:64])
                    last.then_inc(*pe_f.step("st"))
                    for r in range(N_ADA):
                        s = r % RING
                        pe.wait_ge(s_w[s], ring_loads(r))
                        if r % 4 == 0 and r >= 16:
                            pe.wait_ge(*act_f.at("modrow", r // 4 - 4))
                        for k in range(KT):
                            last = nc.tensor.matmul(psA[0:9, (r // 4) % 4, (r % 4) * P:(r % 4 + 1) * P], cT[:, k, :], ring[:, s, k, :],
                                                    start=(k == 0), stop=(k == KT - 1))
                        last.then_inc(*pe_f.step("ada"))
                    for d in range(KT):
                        pe.wait_ge(*act_f.at("sq", d))
                        for hf in range(2):
                            last = nc.tensor.matmul(psB[:, 2 + hf, 0:HALF], ones, ws[:, 10 + d, hf * HALF:(hf + 1) * HALF],
                                                    start=(d == 0), stop=(d == KT - 1))
                    last.then_inc(*pe_f.step("ss"))
                    pe.wait_ge(*act_f.at("modrow", 5))
                    pe.wait_ge(*dve_f.at("stT"))
                    for r in range(24):
                        last = nc.tensor.transpose(psB[:, 1, 9 * r:9 * r + 9], ws[0:9, 4 + r // 4, (r % 4) * P:(r % 4 + 1) * P], ident[0:9, 0:9])
                    last.then_inc(*pe_f.step("mod"))
                    pe.wait_ge(*dve_f.at("hs"))
                    for idx, (col, name, j) in enumerate(PROJ):
                        r = R_PROJ + idx
                        s = r % RING
                        m = P if name != "ba" else 36
                        pe.wait_ge(s_w[s], ring_loads(r))
                        if idx >= 2:
                            pe.wait_ge(*act_f.at("proj", idx - 2))
                        for k in range(KT):
                            for hf in range(2):
                                last = nc.tensor.matmul(psA[0:m, 2 * (idx % 2) + hf, 0:HALF], ring[:, s, k, 0:m], hT[:, k, hf * HALF:(hf + 1) * HALF],
                                                        start=(k == 0), stop=(k == KT - 1))
                        last.then_inc(*pe_f.step("proj"))

                    pe.wait_ge(*act_f.at("proj", N_PROJ - 1))
                    tiles = [RA[:, j] for j in range(7)] + [RC[:, j] for j in range(2)] + [RD[:, j] for j in range(6)]
                    for n, t in enumerate(tiles):
                        last = nc.tensor.transpose(psB[0:11, n // 4, (n % 4) * P:(n % 4 + 1) * P], t[:, SEQ - 3:TT], ident)
                    last.then_inc(*pa.step("crow"))

                    aa, da = TR["act_a"], TR["dve_a"]
                    pe.wait_ge(*aa.at("twd"))
                    pe.wait_ge(*aa.at("crow"))
                    pe.wait_ge(s_w2, 16 * N_W2)
                    for g in range(2):
                        gr = slice(64 * g, 64 * g + 64)
                        if g:
                            pe.wait_ge(*aa.at("thw"))
                        for i in range(2):
                            for hf in range(2):
                                last = nc.tensor.matmul(psB[:, 2 * i + hf, 0:HALF], w2[gr, i * P:(i + 1) * P], RA[gr, 6, hf * HALF:(hf + 1) * HALF],
                                                        start=True, stop=True)
                        last.then_inc(*pa.step("lora"))
                    pe.wait_ge(*aa.at("kk2"))
                    headsum(ws[:, 10:12, :]).then_inc(*pa.step("kks"))
                    pe.wait_ge(*da.at("bt"))
                    headsum(ws[:, 6:8, :]).then_inc(*pa.step("bsum"))
                    pe.wait_ge(*da.at("prep"))
                    Ma = Mst[0]
                    for c in range(NC):
                        if c:
                            pe.wait_ge(*da.at("st", c - 1))
                            pe.wait_ge(*aa.at("o", c - 1))
                        for h in range(HEADS):
                            i = h // 2
                            for x, t in enumerate((14, 16)):
                                last = nc.tensor.matmul(psB[:, h, 256 * x:256 * x + 256], ws[hp(h), t + i, ch(c)], ARa[hp(h), i, c, :, :],
                                                        start=True, stop=True)
                        last.then_inc(*pa.step("gram"))
                        pe.wait_ge(*da.at("gr", c))
                        for n, src in enumerate((ws[:, 14], ws[:, 15], ws[:, 16], ws[:, 17], RA[:, 4], RA[:, 5])):
                            last = nc.tensor.transpose(psB[:, n // 4, (n % 4) * P:(n % 4 + 1) * P], src[:, ch(c)], ident)
                        last.then_inc(*pa.step("tr"))
                        pe.wait_ge(*aa.at("rows", c))
                        pe_tree(pe, pa, da, aa, AtA, Ta, Va, Ya, c)
                        pe.wait_ge(*da.at("t", 7 * c + 6))
                        V4 = h4(Va)
                        for h in range(HEADS):
                            out = psB[:, h % 2, (h // 2) * HD:(h // 2 + 1) * HD]
                            nc.tensor.matmul(out, ARa[hp(h), h // 2, c, 0, :], Ma[hp(h), h // 2, :], start=True, stop=False)
                            last = nc.tensor.matmul(out, GRa4[:, h, 256:384], rowsa[:, 512 + h * HD:512 + (h + 1) * HD], start=False, stop=True)
                        last.then_inc(*pa.step("x1"))
                        pe.wait_ge(*aa.at("x1", c))
                        for h in range(HEADS):
                            last = nc.tensor.matmul(psB[:, 2, h * HD:(h + 1) * HD], V4[:, h, :], X1a[:, h * HD:(h + 1) * HD], start=True, stop=True)
                        last.then_inc(*pa.step("u"))
                        pe.wait_ge(*da.at("u", c))
                        for h in range(HEADS):
                            out = psB[hp(h), h % 2, (h // 2) * P:(h // 2 + 1) * P]
                            nc.tensor.matmul(out, Ma[hp(h), h // 2, :], ARa[hp(h), h // 2, c, 1, :], start=True, stop=False)
                            nc.tensor.matmul(out, Ua[:, h * HD:(h + 1) * HD], GRa4[:, h, 128:256], start=False, stop=False)
                            nc.tensor.matmul(out, rowsa[:, 512 + h * HD:512 + (h + 1) * HD], GRa4[:, h, 384:512], start=False, stop=True)
                        for i in range(2):
                            s2 = slice(i * P, (i + 1) * P)
                            nc.tensor.matmul(psB[:, 3, s2], rowsa[:, i * P:(i + 1) * P], Ua[:, s2], start=True, stop=False)
                            last = nc.tensor.matmul(psB[:, 3, s2], rowsa[:, 256 + i * P:256 + (i + 1) * P], rowsa[:, 512 + i * P:512 + (i + 1) * P], start=False, stop=True)
                        last.then_inc(*pa.step("o"))
                    pe.wait_ge(*da.at("st", NC - 1))
                    pe.wait_ge(*aa.at("o", NC - 1))
                    for i in range(2):
                        last = nc.tensor.transpose(psB[0:HD, 0, i * P:(i + 1) * P], Ma[:, i, :], ident)
                    last.then_inc(*pa.step("mt"))
                    pe.wait_ge(*aa.at("mrow"))

                    ad, dd = TR["act_d"], TR["dve_d"]
                    pe.wait_ge(*ad.at("sq"))
                    headsum(RD[:, 0:2, :]).then_inc(*pd.step("qs"))
                    pe.wait_ge(*ad.at("lnq"))
                    headsum(RD[:, 2:4, :]).then_inc(*pd.step("ks"))
                    pe.wait_ge(*ad.at("rn"))
                    pe.wait_ge(*dd.at("gc"))
                    sel2 = cc("sel2").rearrange("p (i t) -> p i t", i=2)
                    for g in range(2):
                        gr = slice(32 * g, 32 * g + HEADS)
                        if g:
                            pe.wait_ge(*dd.at("ar"))
                        for i in range(2):
                            nc.tensor.matmul(psB[:, i, :], sel2[gr, i, :], bg[gr, 0:SEQ], start=True, stop=True)
                        for i in range(2):
                            last = nc.tensor.matmul(psB[:, 2, 8 * i:8 * i + 8], sel2[gr, i, :], bg[gr, SEQ:TT], start=True, stop=True)
                        last.then_inc(*pd.step("bcast"))
                    pe.wait_ge(*dd.at("prep"))
                    Md = Mst[2]
                    sel4 = h4(cc("sel4"))
                    rd4 = h4(GRd)
                    for c in range(NC):
                        if c:
                            pe.wait_ge(*dd.at("st", c - 1))
                            pe.wait_ge(*ad.at("o", c - 1))
                        for h in range(HEADS):
                            nc.tensor.matmul(psB[:, 0, h * P:(h + 1) * P], sel4[32:36, h, :], bg[32:36, ch(c)], start=True, stop=True)
                        nc.tensor.transpose(psB[:, 1, 0:36], bg[:, ch(c)], ident[0:36, 0:36]).then_inc(*pd.step("gb"))
                        for h in range(HEADS):
                            last = nc.tensor.matmul(psB[:, 2 + h % 2, (h // 2) * 256:(h // 2) * 256 + 256], ws[hp(h), 2 + h // 2, ch(c)],
                                                    ARd[hp(h), h // 2, c, :, :], start=True, stop=True)
                        last.then_inc(*pd.step("gram"))
                        pe.wait_ge(*dd.at("dm", c))
                        for n in range(4):
                            last = nc.tensor.transpose(psB[:, 0, n * P:(n + 1) * P], ws[:, 2 + n, ch(c)], ident)
                        last.then_inc(*pd.step("tr"))
                        pe.wait_ge(*dd.at("gr", c))
                        pe.wait_ge(*ad.at("col", c))
                        pe_tree(pe, pd, dd, ad, AtD, Td, Vd, Yd, c)
                        pe.wait_ge(*dd.at("rows", c))
                        pe.wait_ge(*dd.at("t", 7 * c + 6))
                        for h in range(HEADS):
                            last = nc.tensor.matmul(psB[:, h % 2, (h // 2) * HD:(h // 2 + 1) * HD], RD[hp(h), 4 + h // 2, ch(c)], Md[hp(h), h // 2, :], start=True, stop=True)
                        last.then_inc(*pd.step("x1"))
                        pe.wait_ge(*dd.at("x1", c))
                        for h in range(HEADS):
                            last = nc.tensor.matmul(psB[:, 2, h * HD:(h + 1) * HD], h4(Vd)[:, slot(h), :], X1d[:, h * HD:(h + 1) * HD], start=True, stop=True)
                        last.then_inc(*pd.step("u"))
                        pe.wait_ge(*ad.at("u", c))
                        for h in range(HEADS):
                            out = psB[hp(h), h % 2, (h // 2) * P:(h // 2 + 1) * P]
                            nc.tensor.matmul(out, Md[hp(h), h // 2, :], ws[hp(h), 6 + h // 2, ch(c)], start=True, stop=False)
                            nc.tensor.matmul(out, Ud[:, h * HD:(h + 1) * HD], rd4[:, slot(h), 128:256], start=False, stop=True)
                        for i in range(2):
                            s2 = slice(i * P, (i + 1) * P)
                            last = nc.tensor.matmul(psB[:, 3, s2], rowsd[:, s2], Ud[:, s2], start=True, stop=True)
                        last.then_inc(*pd.step("o"))

                    ab, db = TR["act_b"], TR["dve_b"]
                    pe.wait_ge(*dd.at("st", NC - 1))
                    pe.wait_ge(*ad.at("o", NC - 1))
                    for n in range(2):
                        if n:
                            pe.wait_ge(*db.at("rot", 0))
                        s4 = q4(RB[:, 2 * n:2 * n + 2, :])
                        for k in range(4):
                            last = nc.tensor.matmul(psB[:, k, 0:HALF], cc("rotp"), s4[:, k, :], start=True, stop=True)
                        last.then_inc(*pb.step("rot"))
                    pe.wait_ge(*db.at("prep"))
                    Mb = Mst[1]
                    for c in range(NC):
                        if c:
                            pe.wait_ge(*db.at("st", c - 1))
                            pe.wait_ge(*ab.at("o", c - 1))
                        for h in range(HEADS):
                            last = nc.tensor.matmul(psB[:, h % 2, (h // 2) * P:(h // 2 + 1) * P], RB[hp(h), 2 + h // 2, ch(c)], RB[hp(h), h // 2, ch(c)], start=True, stop=True)
                        last.then_inc(*pb.step("gram"))
                        for n in range(4):
                            last = nc.tensor.transpose(psB[:, 2, n * P:(n + 1) * P], RB[:, 2 + n, ch(c)], ident)
                        last.then_inc(*pb.step("tr"))
                        pe.wait_ge(*db.at("gr", c))
                        pe.wait_ge(*db.at("rows", c))
                        for h in range(HEADS):
                            out = psB[hp(h), h % 2, (h // 2) * P:(h // 2 + 1) * P]
                            nc.tensor.matmul(out, Mb[hp(h), h // 2, :], ws[hp(h), 2 + h // 2, ch(c)], start=True, stop=False)
                            nc.tensor.matmul(out, vrb[:, h * HD:(h + 1) * HD], h4(G1b)[:, h, :], start=False, stop=True)
                        for i in range(2):
                            s2 = slice(i * P, (i + 1) * P)
                            last = nc.tensor.matmul(psB[:, 3, s2], krb[:, s2], vrb[:, s2], start=True, stop=True)
                        last.then_inc(*pb.step("o"))

                    ac, dc = TR["act_c"], TR["dve_c"]
                    pe.wait_ge(*db.at("st", NC - 1))
                    pe.wait_ge(*ab.at("o", NC - 1))
                    pe.wait_ge(*dc.at("xc"))
                    for g in range(2):
                        if g:
                            pe.wait_ge(*ac.at("thr"))
                        for i in range(2):
                            for hf in range(2):
                                last = nc.tensor.matmul(psB[:, 2 * i + hf, 0:HALF], gw[:, 2 * g + i, :], ws[:, i, hf * HALF:(hf + 1) * HALF], start=True, stop=True)
                        last.then_inc(*pcc.step("gates"))
                    pe.wait_ge(*ac.at("thi"))
                    pe.wait_ge(*dc.at("h"))
                    for i in range(2):
                        last = nc.tensor.transpose(psB[0:9, 0, i * P:(i + 1) * P], RC[:, i, SEQ - 1:TT], ident)
                    last.then_inc(*pcc.step("hrow"))

                    as_, ds = TR["act_s"], TR["dve_s"]
                    pe.wait_ge(*db.at("sv"))
                    nc.tensor.transpose(psB[0:96, 1, 0:P], svA[:].rearrange("p n b i -> p (n b i)"), ident)
                    nc.tensor.transpose(psB[:, 1, P:2 * P], svB[:].rearrange("p n b i -> p (n b i)"), ident).then_inc(*pss.step("rows"))
                    pe.wait_ge(s_oread, layer * 16 + 16)
                    pe.sem_inc(s_seen, 1)
                    for i in range(2):
                        last = nc.tensor.transpose(psB[:, 2, 24 * i:24 * i + 24], orow[:, i * P:(i + 1) * P], ident[0:24, 0:24])
                    last.then_inc(*pss.step("oT"))

                    pe.wait_ge(*ds.at("oT"))
                    headsum(RA[:, 2:4, :]).then_inc(*pm.step("mean"))
                    for n in range(3):
                        pe.wait_ge(*TR["act_m"].at("sq", n))
                        pe.wait_ge(*(TR["dve_m"].at("cen") if n == 0 else TR["act_m"].at("ln", n - 1)))
                        headsum(ws[:, 2 * n:2 * n + 2, :]).then_inc(*pm.step("var"))

                    am, dm = TR["act_m"], TR["dve_m"]
                    pe.wait_ge(*am.at("ln", 2))
                    outs = (RA[:, 2:4, :], RB[:, 4:6, :], RC[:, 0:2, :], RD[:, 4:6, :])
                    pe.wait_ge(*dm.at("gated", 3))
                    for idx in range(N_GATE):
                        r = R_GATE + idx
                        s, b = r % RING, 2 * (idx % 2)
                        n = idx % 4
                        pe.wait_ge(s_w[s], ring_loads(r))
                        if idx >= 2:
                            pe.wait_ge(*am.at("th", idx - 2))
                        for k in range(KT):
                            for hf in range(2):
                                last = nc.tensor.matmul(psA[:, b + hf, 0:HALF], ring[:, s, k, :], hT[:, k, hf * HALF:(hf + 1) * HALF],
                                                        start=(k == 0), stop=(k == KT - 1))
                        last.then_inc(*pm.step("gl"))
                        if idx >= 2:
                            pe.wait_ge(*dm.at("mg", idx - 2))
                        for i in range(2):
                            for hf in range(2):
                                last = nc.tensor.matmul(psB[:, b + hf, 0:HALF], upw[:, s, i, :], outs[n][:, i, hf * HALF:(hf + 1) * HALF],
                                                        start=(i == 0), stop=(i == 1))
                        last.then_inc(*pm.step("gate"))
                    pe.wait_ge(*dm.at("mg", N_GATE - 1))
                    for e in range(KT):
                        r = R_OUT + e
                        s, b = r % RING, 2 * (e % 2)
                        pe.wait_ge(s_w[s], ring_loads(r))
                        if e >= 2:
                            pe.wait_ge(*dm.at("x", e - 2))
                        for k in range(KT):
                            for hf in range(2):
                                last = nc.tensor.matmul(psA[:, b + hf, 0:HALF], ring[:, s, k, :], ws[:, k, hf * HALF:(hf + 1) * HALF],
                                                        start=(k == 0), stop=(k == KT - 1))
                        last.then_inc(*pm.step("out"))

                @block.scalar
                def _(act):
                    A = nc.scalar.activation
                    eps = cc("eps")
                    half = lambda ap: ap.rearrange("p (h c) -> p h c", h=2)
                    act.wait_ge(*dve_f.at("zero"))
                    for d in range(KT):
                        A(ws[:, 10 + d, :], xT[:, d, :], ACT.Square).then_inc(*act_f.step("sq"))
                    for g in range(6):
                        act.wait_ge(*pe_f.at("ada", 4 * g + 3))
                        nc.scalar.copy(ws[0:9, 4 + g, 0:512], psA[0:9, g % 4, :]).then_inc(*act_f.step("modrow"))
                    act.wait_ge(*pe_f.at("ss"))
                    A(half(rs[:]), psB[:, 2:4, 0:HALF], ACT.Ln, bias=eps, scale=1.0 / D_MODEL).then_inc(*act_f.step("lnx"))
                    act.wait_ge(*act_f.at("lnx"))
                    A(rs[:], rs[:], ACT.Exp, scale=-0.5).then_inc(*act_f.step("rs"))
                    act.wait_ge(*dve_f.at("der"))
                    A(der[:, 20:22], par("lam", 0, 2), ACT.Abs).then_inc(*act_f.step("lam_abs"))
                    act.wait_ge(*act_f.at("lam_abs"))
                    A(der[:, 22:24], der[:, 20:22], ACT.Exp, scale=-1.0).then_inc(*act_f.step("lam_z"))
                    act.wait_ge(s_w2, 16 * N_W2)
                    A(gp[32:36, 2:3], gp[32:36, 0:1], ACT.Exp).then_inc(*act_f.step("expA"))
                    for idx, (col, name, j) in enumerate(PROJ):
                        b = 2 * (idx % 2)
                        act.wait_ge(*pe_f.at("proj", idx))
                        if name == "ba":
                            A(half(bg[0:4, :]), psA[0:4, b:b + 2, 0:HALF], ACT.Tanh, scale=0.5)
                            A(half(bg[32:36, :]), psA[32:36, b:b + 2, 0:HALF], ACT.Identity, bias=gp[32:36, 1:2]).then_inc(*act_f.step("proj"))
                        else:
                            nc.scalar.copy(half(RAW[name][:, j, :]), psA[:, b:b + 2, 0:HALF]).then_inc(*act_f.step("proj"))

                    pa, aa, da = TR["pe_a"], TR["act_a"], TR["dve_a"]
                    act.wait_ge(*pa.at("crow"))
                    nc.scalar.copy(crow[:, 0:12 * P].rearrange("p (b c) -> p b c", b=3), psB[0:11, 0:3, :])
                    nc.scalar.copy(crow[:, 12 * P:15 * P], psB[0:11, 3, 0:3 * P]).then_inc(*aa.step("crow"))
                    act.wait_ge(*da.at("pm"))
                    A(RA[0:64, 6, :], RA[0:64, 6, :], ACT.Tanh).then_inc(*aa.step("twd"))
                    for g, (nm, hb, t) in enumerate((("thw", 0, 0), ("tha", 2, 8))):
                        act.wait_ge(*pa.at("lora", g))
                        for i in range(2):
                            last = A(half(ws[:, t + i, :]), psB[:, 2 * i:2 * i + 2, 0:HALF], ACT.Tanh, bias=der[:, hb + i:hb + i + 1], scale=0.5)
                        last.then_inc(*aa.step(nm))
                    act.wait_ge(*da.at("kk"))
                    A(ws[:, 10:12, :], ws[:, 6:8, :], ACT.Square).then_inc(*aa.step("kk2"))
                    act.wait_ge(*aa.at("tha"))
                    for i in range(2):
                        last = A(ws[:, 12 + i, :], ws[:, 8 + i, :], ACT.Identity, bias=der[:, 6 + i:7 + i], scale=der[:, 4 + i:5 + i])
                    last.then_inc(*aa.step("kf"))
                    act.wait_ge(*pa.at("kks"))
                    A(q4(ws[:, 10:12, :]), psB[:, :, 0:HALF], ACT.Ln, bias=eps).then_inc(*aa.step("lnk"))
                    act.wait_ge(*aa.at("lnk"))
                    A(ws[:, 10:12, :], ws[:, 10:12, :], ACT.Exp, scale=-0.5).then_inc(*aa.step("rn"))
                    act.wait_ge(*da.at("lex"))
                    A(ws[:, 4:6, :], ws[:, 2:4, :], ACT.Exp, scale=W_DECAY)
                    A(pc[:, 0], mid[:], ACT.Exp, scale=W_DECAY)
                    A(ws[:, 0:2, 0:SEQ], ws[:, 0:2, 0:SEQ], ACT.Exp, scale=W_DECAY).then_inc(*aa.step("decay"))
                    act.wait_ge(*aa.at("decay"))
                    A(ws[:, 2:4, 0:SEQ], ws[:, 2:4, 0:SEQ], ACT.Exp, scale=-W_DECAY).then_inc(*aa.step("exps"))
                    for c in range(NC):
                        act.wait_ge(*pa.at("tr", c))
                        nc.scalar.copy(rowsa[:, 0:512], psB[:, 0, :])
                        nc.scalar.copy(rowsa[:, 512:768], psB[:, 1, 0:256]).then_inc(*aa.step("rows"))
                        act_tree(act, pa, aa, Ya, c)
                        act.wait_ge(*pa.at("x1", c))
                        nc.scalar.copy(X1a.rearrange("p (i g v) -> p i g v", i=2, g=2), psB[:, 0:2, 0:P].rearrange("p g (i v) -> p i g v", i=2)).then_inc(*aa.step("x1"))
                        act.wait_ge(*pa.at("o", c))
                        for g in range(2):
                            pr = slice(g * HD, (g + 1) * HD)
                            last = nc.scalar.copy(RA[pr, 2:4, ch(c)], psB[pr, g, 0:256].rearrange("p (i t) -> p i t", i=2))
                        last.then_inc(*aa.step("o"))
                    act.wait_ge(*pa.at("mt"))
                    nc.scalar.copy(mrow[:], psB[0:HD, 0, 0:256].rearrange("p (i t) -> p i t", i=2)).then_inc(*aa.step("mrow"))

                    pd, ad, dd = TR["pe_d"], TR["act_d"], TR["dve_d"]
                    act.wait_ge(*da.at("st", NC - 1))
                    for t in range(6):
                        last = A(ws[:, t, 0:SEQ], RD[:, t, 0:SEQ], ACT.Identity, scale=par("gdn_w", 18 + t))
                    last.then_inc(*ad.step("cv0"))
                    A(ws[32:36, 10, :], bg[32:36, :], ACT.Abs).then_inc(*ad.step("gabs"))
                    act.wait_ge(*ad.at("gabs"))
                    A(ws[32:36, 11, :], ws[32:36, 10, :], ACT.Exp, scale=-1.0).then_inc(*ad.step("gz"))
                    act.wait_ge(*dd.at("cv"))
                    A(RD[:, 0:6, :], ws[:, 0:6, :], ACT.Tanh, scale=0.5).then_inc(*ad.step("ths"))
                    act.wait_ge(*dd.at("silu2"))
                    A(RD[:, 0:4, :], ws[:, 0:4, :], ACT.Square).then_inc(*ad.step("sq"))
                    act.wait_ge(*pd.at("qs"))
                    A(q4(RD[:, 0:2, :]), psB[:, :, 0:HALF], ACT.Ln, bias=eps, scale=0.25).then_inc(*ad.step("lnq"))
                    act.wait_ge(*pd.at("ks"))
                    A(q4(RD[:, 2:4, :]), psB[:, :, 0:HALF], ACT.Ln, bias=eps, scale=0.25).then_inc(*ad.step("lnk"))
                    act.wait_ge(*ad.at("lnk"))
                    A(RD[:, 0:4, :], RD[:, 0:4, :], ACT.Exp, scale=-0.5).then_inc(*ad.step("rn"))
                    act.wait_ge(*pd.at("bcast", 1))
                    A(ws[:, 6:8, 0:SEQ], psB[:, 0:2, :], ACT.Exp)
                    A(ws[:, 6:8, SEQ:TT], psB[:, 2, 0:16].rearrange("p (i b) -> p i b", i=2), ACT.Exp).then_inc(*ad.step("egc"))
                    for c in range(NC):
                        act.wait_ge(*pd.at("gb", c))
                        nc.scalar.copy(colbg[:], psB[:, 1, 0:36]).then_inc(*ad.step("col"))
                        act.wait_ge(*dd.at("dm", c))
                        A(Dd, Dd, ACT.Exp)
                        A(kdl[:], kdl[:], ACT.Exp).then_inc(*ad.step("dexp"))
                        act_tree(act, pd, ad, Yd, c)
                        act.wait_ge(*pd.at("u", c))
                        nc.scalar.copy(Ud, psB[:, 2, 0:256]).then_inc(*ad.step("u"))
                        act.wait_ge(*pd.at("o", c))
                        for g in range(2):
                            pr = slice(g * HD, (g + 1) * HD)
                            last = nc.scalar.copy(RD[pr, 4:6, ch(c)], psB[pr, g, 0:256].rearrange("p (i t) -> p i t", i=2))
                        last.then_inc(*ad.step("o"))

                    pb, ab, db = TR["pe_b"], TR["act_b"], TR["dve_b"]
                    for c in range(NC):
                        act.wait_ge(*pb.at("o", c))
                        for g in range(2):
                            pr = slice(g * HD, (g + 1) * HD)
                            last = nc.scalar.copy(RB[pr, 4:6, ch(c)], psB[pr, g, 0:256].rearrange("p (i t) -> p i t", i=2))
                        last.then_inc(*ab.step("o"))

                    pcc, ac, dc = TR["pe_c"], TR["act_c"], TR["dve_c"]
                    act.wait_ge(*db.at("st", NC - 1))
                    for i in range(2):
                        last = A(ws[:, i, 0:SEQ], RC[:, i, 0:SEQ], ACT.Identity, bias=par("lru_b", i), scale=par("lru_w", 6 + i))
                    last.then_inc(*ac.step("cv0"))
                    for g, (nm, t) in enumerate((("thr", 2), ("thi", 4))):
                        act.wait_ge(*pcc.at("gates", g))
                        for i in range(2):
                            last = A(half(ws[:, t + i, :]), psB[:, 2 * i:2 * i + 2, 0:HALF], ACT.Tanh, bias=der[:, 8 + 2 * g + i:9 + 2 * g + i], scale=0.5)
                        last.then_inc(*ac.step(nm))
                    act.wait_ge(*ac.at("thr"))
                    for i in range(2):
                        A(ws[:, 6 + i, :], ws[:, 2 + i, :], ACT.Exp, bias=der[:, 14 + i:15 + i], scale=der[:, 14 + i:15 + i])
                        last = A(ws[:, 8 + i, :], ws[:, 2 + i, :], ACT.Tanh, bias=der[:, 12 + i:13 + i], scale=der[:, 12 + i:13 + i])
                    last.then_inc(*ac.step("au"))
                    act.wait_ge(*dc.at("u2"))
                    A(ws[:, 10:12, :], ws[:, 10:12, :], ACT.Ln)
                    A(ws[:, 12:14, :], ws[:, 8:10, :], ACT.Ln, bias=cc("ones")[:, 0:1]).then_inc(*ac.step("lnu"))
                    act.wait_ge(*dc.at("lndiff"))
                    A(ws[:, 10:12, :], ws[:, 10:12, :], ACT.Exp, scale=0.5).then_inc(*ac.step("root"))
                    act.wait_ge(*pcc.at("hrow"))
                    nc.scalar.copy(hrow[:], psB[0:9, 0, 0:W]).then_inc(*ac.step("hrow"))

                    as_ = TR["act_s"]
                    act.wait_ge(*TR["pe_s"].at("rows"))
                    nc.scalar.copy(rowA[:], psB[0:96, 1, 0:P])
                    nc.scalar.copy(rowB[:], psB[:, 1, P:2 * P]).then_inc(*as_.step("rows"))

                    pm, am, dm = TR["pe_m"], TR["act_m"], TR["dve_m"]
                    act.wait_ge(*TR["dve_s"].at("oT"))
                    srcs = (RA[:, 2:4, :], RB[:, 4:6, :], RD[:, 4:6, :])
                    zs = (RA[:, 7:9, :], RB[:, 6:8, :], RC[:, 2:4, :], RD[:, 6:8, :])
                    for n in range(3):
                        if n == 0:
                            act.wait_ge(*dm.at("cen"))
                        A(ws[:, 2 * n:2 * n + 2, :], srcs[n], ACT.Square).then_inc(*am.step("sq"))
                    for n in range(3):
                        act.wait_ge(*pm.at("var", n))
                        A(q4(ws[:, 2 * n:2 * n + 2, :]), psB[:, :, 0:HALF], ACT.Ln, bias=cc("epsgn") if n == 0 else eps, scale=1.0 / HD).then_inc(*am.step("ln"))
                    act.wait_ge(*am.at("ln", 2))
                    A(ws[:, 0:6, :], ws[:, 0:6, :], ACT.Exp, scale=-0.5).then_inc(*am.step("rn"))
                    for n in range(4):
                        A(ws[:, 6 + 2 * n:8 + 2 * n, :], zs[n], ACT.Tanh, scale=0.5).then_inc(*am.step("tz"))
                    for idx in range(N_GATE):
                        b = 2 * (idx % 2)
                        act.wait_ge(*pm.at("gl", idx))
                        if idx >= 2:
                            act.wait_ge(*dm.at("mul", idx - 2))
                        elif idx == 0:
                            act.wait_ge(*dm.at("gated", 3))
                        A(half(ws[:, 8 + idx % 2, :]), psA[:, b:b + 2, 0:HALF], ACT.Tanh, scale=0.5).then_inc(*am.step("th"))

                @block.vector
                def _(dve):
                    v = nc.vector
                    T_, S_, STT = v.tensor_tensor, v.tensor_scalar, v.scalar_tensor_tensor

                    def did(track_, name, ins, i=0):
                        ins.then_inc(*track_.step(name))
                        dve.wait_ge(*track_.at(name, i))

                    half = lambda ap: ap.rearrange("p (h c) -> p h c", h=2)
                    v.memset(ws[0:64, 0:2, :], 0.0)
                    for m in Mst:
                        last = v.memset(m[:], 0.0)
                    last.then_inc(*dve_f.step("zero"))
                    dve.wait_ge(*pe_f.at("par"))
                    did(dve_f, "parT", v.tensor_copy(parT[:, 0:PARAM_N], psB[:, 0, 0:PARAM_N]))
                    S_(der[:, 0:2], par("w0", 0, 2), 0.5, None, mult)
                    S_(der[:, 2:4], par("a0", 0, 2), 0.5, None, mult)
                    S_(der[:, 4:6], par("k_a", 0, 2), 0.5, None, mult)
                    S_(der[:, 6:8], par("k_a", 0, 2), -0.5, 1.0, mult, add)
                    did(dve_f, "der", S_(der[:, 8:12], par("gate_b", 0, 4), 0.5, None, mult))
                    dve.wait_ge(*pe_f.at("st"))
                    did(dve_f, "stT", v.tensor_copy(stT[:], psB[:, 1, 0:448].rearrange("p (j r) -> p j r", j=7)))

                    def log1p(tr, pre, z, t, t2, acc):
                        did(tr, pre + "1", S_(t, z, 2.0, None, add))
                        did(tr, pre + "2", v.reciprocal(t2, t))
                        did(tr, pre + "3", T_(t, z, t2, mult))
                        did(tr, pre + "4", T_(t2, t, t, mult))
                        did(tr, pre + "5", S_(acc, t2, 2.0 / 17, 2.0 / 15, mult, add))
                        for n in (13, 11, 9, 7, 5, 3, 1):
                            did(tr, pre + f"m{n}", T_(acc, acc, t2, mult))
                            did(tr, pre + f"a{n}", S_(acc, acc, 2.0 / n, None, add))
                        did(tr, pre + "6", T_(acc, acc, t, mult))

                    dve.wait_ge(*act_f.at("lam_z"))
                    log1p(dve_f, "lam", der[:, 22:24], der[:, 24:26], der[:, 26:28], der[:, 28:30])
                    did(dve_f, "lam_y", S_(der[:, 30:32], par("lam", 0, 2), -1.0, 0.0, mult, ALU.max))
                    did(dve_f, "lam_sp", T_(der[:, 30:32], der[:, 30:32], der[:, 28:30], add))
                    S_(der[:, 12:14], der[:, 30:32], LRU_C / 2, None, mult)
                    S_(der[:, 14:16], der[:, 30:32], -LRU_C / 2, None, mult)
                    dve.wait_ge(*pe_f.at("mod"))
                    did(dve_f, "modT", T_(modT[:], psB[:, 1, 0:216].rearrange("p (r s) -> p r s", r=24), bc(par("ada_b", 0, 24), 2, 9), add))
                    STT(G[:], modT[:, 8:16, :], 1.0, bc(par("norm_g", 0, 8), 2, 9), add, mult)
                    did(dve_f, "G", S_(modT[:, 16:24, :], modT[:, 16:24, :], 0.5, None, mult))
                    dve.wait_ge(*act_f.at("rs"))
                    for d in range(KT):
                        last = T_(hT[:, d, :], xT[:, d, :], rs[:], mult)
                    did(dve_f, "xn", last)
                    for d in range(KT):
                        S_(hT[:, d, 0:SEQ], hT[:, d, 0:SEQ], G[:, d, 8:9], modT[:, d, 8:9], mult, add)
                    did(dve_f, "hg", T_(hT[:, :, SEQ:TT], hT[:, :, SEQ:TT], G[:, :, 0:8], mult))
                    did(dve_f, "hs", T_(hT[:, :, SEQ:TT], hT[:, :, SEQ:TT], modT[:, 0:8, 0:8], add))

                    pa, aa, da = TR["pe_a"], TR["act_a"], TR["dve_a"]
                    dve.wait_ge(*act_f.at("proj", N_PROJ - 1))
                    T_(ws[:, 0:7, 1:SEQ], RA[:, 0:7, 0:SEQ - 1], RA[:, 0:7, 1:SEQ], sub)
                    S_(ws[:, 0:7, 0:1], RA[:, 0:7, 0:1], -1.0, None, mult)
                    did(da, "diff", T_(ws[:, 0:7, SEQ:TT], stT[:, :, 0:8], RA[:, 0:7, SEQ:TT], sub))
                    dve.wait_ge(*pa.at("crow"))
                    for j in range(7):
                        last = STT(RA[:, j, :], ws[:, j, :], par("mu", j), RA[:, j, :], mult, add)
                    did(da, "pm", last)
                    for i in range(2):
                        last = S_(ws[:, 6 + i, :], RA[:, 2 + i, :], par("k_k", i), None, mult)
                    did(da, "kk", last)
                    dve.wait_ge(*aa.at("thw"))
                    did(da, "lw1", S_(ws[:, 0:2, :], ws[:, 0:2, :], 1.0, None, add))
                    for i in range(2):
                        last = v.tensor_tensor_scan(ws[:, 2 + i, :], cc("reset"), ws[:, i, :], 0.0, mult, add)
                    did(da, "scan", last)
                    L4 = ws[:, 2:4, 0:SEQ].rearrange("p i (c t) -> p i c t", c=NC)
                    did(da, "mid", v.tensor_copy(mid[:], L4[:, :, :, C // 2 - 1]))
                    did(da, "lrel", T_(L4, L4, bc(mid[:], 3, C), sub))
                    did(da, "lex", T_(ws[:, 0:2, 0:SEQ], ws[:, 2:4, 0:SEQ], ws[:, 0:2, 0:SEQ], sub))
                    dve.wait_ge(*aa.at("kf"))
                    S_(ws[:, 8:10, :], ws[:, 8:10, :], 0.5, 0.5, mult, add)
                    T_(RA[:, 2:4, :], RA[:, 2:4, :], ws[:, 12:14, :], mult)
                    dve.wait_ge(*aa.at("rn"))
                    did(da, "kkn", T_(ws[:, 6:8, :], ws[:, 6:8, :], ws[:, 10:12, :], mult))
                    did(da, "bv", T_(ws[:, 8:10, :], ws[:, 8:10, :], ws[:, 6:8, :], mult))
                    dve.wait_ge(*aa.at("exps"))
                    svt = lambda sv, n: sv[:, n].rearrange("p b i -> p i b")
                    for n, src in ((0, RA[:, 0:2]), (1, ws[:, 4:6]), (2, RA[:, 2:4]), (3, RA[:, 4:6]), (5, ws[:, 8:10])):
                        v.tensor_copy(svt(svA, n), src[:, :, SEQ:TT])
                    S_(svt(svA, 4), ws[:, 6:8, SEQ:TT], -1.0, None, mult)
                    s4 = lambda t: ws[:, t, 0:SEQ].rearrange("p (c t) -> p c t", c=NC)
                    for i in range(2):
                        STT(ARa[:, i, :, 0, :], s4(6 + i), -1.0, s4(i), mult, mult)
                        T_(ARa[:, i, :, 1, :], RA[:, i, 0:SEQ].rearrange("p (c t) -> p c t", c=NC), s4(4 + i), mult)
                    T_(ws[:, 14:16, 0:SEQ], ws[:, 8:10, 0:SEQ], ws[:, 2:4, 0:SEQ], mult)
                    T_(ws[:, 16:18, 0:SEQ], RA[:, 2:4, 0:SEQ], ws[:, 2:4, 0:SEQ], mult)
                    E4 = ws[:, 4:6, 0:SEQ].rearrange("p i (c t) -> p i c t", c=NC)
                    did(da, "pend", v.tensor_copy(pc[:, 1], E4[:, :, :, C - 1]))
                    T_(pc[:, 2, :, 0:NC - 1], pc[:, 1, :, 0:NC - 1], pc[:, 0, :, 1:NC], mult)
                    v.tensor_copy(pc[:, 2, :, NC - 1:NC], pc[:, 1, :, NC - 1:NC])
                    for i in range(2):
                        last = STT(ws[:, 6 + i, :], RA[:, i, :], par("r_k", i), RA[:, 2 + i, :], mult, mult)
                    did(da, "bt", last)
                    dve.wait_ge(*pa.at("bsum"))
                    did(da, "prep", T_(q4(RA[:, 0:2, :]), psB[:, :, 0:HALF], q4(RA[:, 4:6, :]), mult))
                    Ma = Mst[0]
                    for c in range(NC):
                        dve.wait_ge(*pa.at("gram", c))
                        v.tensor_copy(h4(Ta), bc(ident, 1, HEADS))
                        v.tensor_copy(h4(Va), bc(ident, 1, HEADS))
                        did(da, "gr", T_(GRa4, psB[:], bc(cc("rmask"), 1, HEADS), mult), c)
                        dve_tree(dve, pa, da, AtA, Ta, Va, c)
                        dve.wait_ge(*pa.at("u", c))
                        v.tensor_copy(Ua, psB[:, 2, 0:256]).then_inc(*da.step("u"))
                        dve.wait_ge(*pa.at("o", c))
                        for g in range(2):
                            pr = slice(g * HD, (g + 1) * HD)
                            last = T_(Ma[pr], psB[pr, 3, 0:256].rearrange("p (i x) -> p i x", i=2)[:, :, g * HD:(g + 1) * HD], Ma[pr], add)
                        did(da, "sum", last, c)
                        did(da, "st", T_(Ma[:], Ma[:], bc(pc[:, 2, :, c], 2, HD), mult), c)

                    pd, ad, dd = TR["pe_d"], TR["act_d"], TR["dve_d"]
                    dve.wait_ge(*pa.at("mt"))

                    def conv(tr, raw, n, wname, st0):
                        w0 = PARAM_ROWS[wname]
                        for tap in range(2, -1, -1):
                            sh = CONV - 1 - tap
                            for t in range(n):
                                last = STT(ws[:, t, sh:SEQ], raw[:, t, 0:SEQ - sh], par(wname, tap * n + t), ws[:, t, sh:SEQ], mult, add)
                            did(tr, "cvt", last, 2 - tap)
                        stc = stT[:, 0:n, st0:st0 + 24].rearrange("p i (b j) -> p i b j", j=3)
                        wt = parT[:, w0:w0 + 3 * n].rearrange("p (j i) -> p i j", i=n)
                        tmp = wv(14, n * 24).rearrange("p (i b j) -> p i b j", i=n, b=NB)
                        new = wv(15, n * NB).rearrange("p (i b) -> p i b", i=n)
                        did(tr, "cs1", T_(tmp, stc, bc(wt, 2, NB), mult))
                        v.tensor_reduce(ws[:, 0:n, SEQ:TT], tmp, AX.X, add)
                        did(tr, "cs2", T_(new, raw[:, 0:n, SEQ:TT], bc(parT[:, w0 + 3 * n:w0 + 4 * n], 2, NB), mult))
                        did(tr, "cs3", T_(ws[:, 0:n, SEQ:TT], ws[:, 0:n, SEQ:TT], new, add))

                    dve.wait_ge(*ad.at("cv0"))
                    conv(dd, RD, 6, "gdn_w", 40)
                    v.tensor_copy(colbg[:, 0:1], cc("eps")).then_inc(*dd.step("cv"))
                    dve.wait_ge(*ad.at("gz"))
                    g_ = lambda t: ws[32:36, t, :]
                    log1p(dd, "g", g_(11), g_(12), g_(13), g_(14))
                    S_(gp[32:36, 3:4], gp[32:36, 2:3], -1.0, None, mult)
                    did(dd, "gmax", S_(g_(12), bg[32:36, :], 0.0, None, ALU.max))
                    did(dd, "gsp", T_(g_(12), g_(12), g_(14), add))
                    did(dd, "gneg", S_(g_(12), g_(12), gp[32:36, 3:4], None, mult))
                    S_(bg[0:4, :], bg[0:4, :], 0.5, 0.5, mult, add)
                    did(dd, "gc", v.tensor_tensor_scan(bg[32:36, :], cc("reset", 32, 36), g_(12), 0.0, mult, add))
                    dve.wait_ge(*ad.at("ths"))
                    did(dd, "silu2", STT(ws[:, 0:6, :], RD[:, 0:6, :], 1.0, ws[:, 0:6, :], add, mult))
                    dve.wait_ge(*ad.at("rn"))
                    STT(ws[:, 0:2, :], ws[:, 0:2, :], 0.5 * HD ** -0.5, RD[:, 0:2, :], mult, mult)
                    did(dd, "qk", STT(ws[:, 2:4, :], ws[:, 2:4, :], 0.5, RD[:, 2:4, :], mult, mult))
                    dve.wait_ge(*pd.at("bcast", 0))
                    for i in range(2):
                        STT(ARd[:, i, :, 0, :], s4(2 + i), -1.0, psB[:, i, :].rearrange("p (c t) -> p c t", c=NC), mult, mult)
                        v.tensor_copy(ARd[:, i, :, 1, :], s4(i))
                    v.tensor_copy(svt(svB, 3), ws[:, 0:2, SEQ:TT])
                    v.tensor_copy(svt(svB, 4), ws[:, 2:4, SEQ:TT])
                    S_(svt(svB, 5), ws[:, 4:6, SEQ:TT], 0.5, None, mult)
                    did(dd, "ar", v.tensor_copy(svt(svB, 6), psB[:, 2, 0:16].rearrange("p (i b) -> p i b", i=2)))
                    dve.wait_ge(*ad.at("egc"))
                    v.tensor_copy(svt(svB, 7), ws[:, 6:8, SEQ:TT])
                    for i in range(2):
                        last = T_(RD[:, 4 + i, 0:SEQ].rearrange("p (c t) -> p c t", c=NC), ARd[:, i, :, 0, :], s4(6 + i), mult)
                    did(dd, "kbe", last)
                    did(dd, "prep", T_(ws[:, 6:8, 0:SEQ], ws[:, 0:2, 0:SEQ], ws[:, 6:8, 0:SEQ], mult))
                    Md = Mst[2]
                    D4 = h4(Dd)
                    for c in range(NC):
                        dve.wait_ge(*ad.at("col", c))
                        pg = h4(psB[:, 0, :])
                        for h in range(HEADS):
                            STT(D4[:, slot(h), :], pg[:, h, :], colbg[:, 32 + h:33 + h], cc("negm"), sub, add)
                        T_(kdl[:, 0:4], pg[:, :, C - 1], colbg[:, 32:36], sub)
                        v.tensor_copy(kdl[:, 4:8], pg[:, :, C - 1]).then_inc(*dd.step("dm"))
                        dve.wait_ge(*pd.at("gram", c))
                        v.tensor_copy(h4(Td), bc(ident, 1, HEADS))
                        v.tensor_copy(h4(Vd), bc(ident, 1, HEADS))
                        dve.wait_ge(*ad.at("dexp", c))
                        did(dd, "gr", T_(GRd.rearrange("p (h x t) -> p h x t", h=HEADS, x=2),
                                         psB[:, 2:4, :].rearrange("p b (h x t) -> p (b h) x t", h=2, x=2), bc(D4, 2, 2), mult), c)
                        dve.wait_ge(*pd.at("tr", c))
                        T_(h4(rowsd[:, 0:256]), h4(psB[:, 0, 0:256]), bc(kdl[:, 0:4], 2, HD), mult)
                        STT(h4(rowsd[:, 256:512]), h4(psB[:, 0, 256:512]), 0.5, bc(colbg[:, 0:4], 2, HD), mult, mult).then_inc(*dd.step("rows"))
                        dve_tree(dve, pd, dd, AtD, Td, Vd, c)
                        dve.wait_ge(*pd.at("x1", c))
                        dve.wait_ge(*dd.at("rows", c))
                        T_(X1d.rearrange("p (i g v) -> p i g v", i=2, g=2), psB[:, 0:2, 0:P].rearrange("p g (i v) -> p i g v", i=2),
                           rowsd[:, 256:512].rearrange("p (i g v) -> p i g v", i=2, g=2), add).then_inc(*dd.step("x1"))
                        dve.wait_ge(*pd.at("o", c))
                        for h in range(HEADS):
                            i, g = h // 2, h % 2
                            last = STT(Md[hp(h), i, :], Md[hp(h), i, :], kdl[hp(h), 4 + h:5 + h], psB[hp(h), 3, i * P + g * HD:i * P + (g + 1) * HD], mult, add)
                        did(dd, "st", last, c)

                    pb, ab, db = TR["pe_b"], TR["act_b"], TR["dve_b"]
                    rd = lambda n, hf_: RB[:, 2 * n:2 * n + 2, :]
                    for n, sc in ((0, 1.0), (1, HD ** -0.5)):
                        dve.wait_ge(*pb.at("rot", n))
                        for i in range(2):
                            STT(half(ws[:, i, :]), psB[:, 2 * i:2 * i + 2, 0:HALF], sc, half(cc("sin")), mult, mult)
                        for i in range(2):
                            last = STT(RB[:, 2 * n + i, :], RB[:, 2 * n + i, :], sc, cc("cos"), mult, mult)
                        did(db, "rot", last, n)
                        did(db, "rope", T_(RB[:, 2 * n:2 * n + 2, :], RB[:, 2 * n:2 * n + 2, :], ws[:, 0:2, :], add), n)
                    for n in range(2):
                        v.tensor_copy(svt(svB, n), RB[:, 2 * n:2 * n + 2, SEQ:TT])
                    v.tensor_copy(svt(svB, 2), RB[:, 4:6, SEQ:TT]).then_inc(*db.step("sv"))
                    q_c = RB[:, 0:2, 0:SEQ].rearrange("p i (c t) -> p i c t", c=NC)
                    did(db, "prep", T_(ws[:, 2:4, 0:SEQ].rearrange("p i (c t) -> p i c t", c=NC), q_c,
                                       bc(cc("qdec").rearrange("p (i t) -> p i t", i=2), 2, NC), mult))
                    Mb = Mst[1]
                    for c in range(NC):
                        dve.wait_ge(*pb.at("gram", c))
                        T_(G1b.rearrange("p (i g t) -> p i g t", i=2, g=2), psB[:, 0:2, 0:256].rearrange("p g (i t) -> p i g t", i=2),
                           cc("rdec").rearrange("p (i g t) -> p i g t", i=2, g=2), mult).then_inc(*db.step("gr"))
                        dve.wait_ge(*pb.at("tr", c))
                        T_(h4(krb), h4(psB[:, 2, 0:256]), bc(cc("kdec"), 2, HD), mult)
                        v.tensor_copy(vrb, psB[:, 2, 256:512]).then_inc(*db.step("rows"))
                        dve.wait_ge(*pb.at("o", c))
                        for h in range(HEADS):
                            i, g = h // 2, h % 2
                            last = STT(Mb[hp(h), i, :], Mb[hp(h), i, :], cc("gc")[hp(h), i:i + 1], psB[hp(h), 3, i * P + g * HD:i * P + (g + 1) * HD], mult, add)
                        did(db, "st", last, c)

                    pcc, ac, dc = TR["pe_c"], TR["act_c"], TR["dve_c"]
                    dve.wait_ge(*ac.at("cv0"))
                    conv(dc, RC, 2, "lru_w", 16)
                    did(dc, "xc", T_(ws[:, 0:2, SEQ:TT], ws[:, 0:2, SEQ:TT], bc(par("lru_b", 0, 2), 2, NB), add))
                    dve.wait_ge(*ac.at("au"))
                    S_(ws[:, 10:12, :], ws[:, 8:10, :], 2.0, 1e-18, mult, ALU.max).then_inc(*dc.step("u2"))
                    did(dc, "ix", STT(ws[:, 4:6, :], ws[:, 4:6, :], 1.0, ws[:, 0:2, :], add, mult))
                    dve.wait_ge(*ac.at("lnu"))
                    T_(ws[:, 10:12, :], ws[:, 10:12, :], ws[:, 12:14, :], sub).then_inc(*dc.step("lndiff"))
                    dve.wait_ge(*ac.at("root"))
                    T_(ws[:, 0:2, SEQ:TT], ws[:, 6:8, SEQ:TT], stT[:, 0:2, 8:16], mult)
                    did(dc, "b", STT(ws[:, 4:6, :], ws[:, 4:6, :], 0.5, ws[:, 10:12, :], mult, mult))
                    for i in range(2):
                        v.tensor_tensor_scan(RC[:, i, 0:SEQ], ws[:, 6 + i, 0:SEQ], ws[:, 4 + i, 0:SEQ], 0.0, mult, add)
                    did(dc, "h", T_(RC[:, 0:2, SEQ:TT], ws[:, 0:2, SEQ:TT], ws[:, 4:6, SEQ:TT], add))

                    ds = TR["dve_s"]
                    SS = [wf[:, 1024 * n:1024 * (n + 1)] for n in range(3)]
                    tmp = wf[:, 3072:4096]
                    vk = lambda ap: ap.rearrange("p (v k) -> p v k", v=16)
                    kv = lambda ap: ap.rearrange("p (k v) -> p k v", v=16)
                    kvT = lambda ap: ap.rearrange("p (k v) -> p v k", v=16)
                    dve.wait_ge(s_vec, layer * (16 * N_VEC) + 16 * N_VEC)
                    dve.wait_ge(s_ss, layer * (16 * N_SS) + 16 * N_SS)
                    r_, w_, k_, a_, b_ = (vecA[:, n, :] for n in (0, 1, 2, 4, 5))
                    row = lambda x: bc(x, 1, 16)
                    did(ds, "1", T_(vk(tmp), vk(SS[0]), row(a_), mult))
                    v.tensor_reduce(sa[:, 0, :], vk(tmp), AX.X, add)
                    did(ds, "2", T_(vk(SS[0]), vk(SS[0]), row(w_), mult))
                    did(ds, "3", T_(vk(tmp), bc(sa[:, 0, :], 2, HD), row(b_), mult))
                    did(ds, "4", T_(SS[0], SS[0], tmp, add))
                    did(ds, "5", T_(vk(tmp), bc(vv[:, 0, :], 2, HD), row(k_), mult))
                    did(ds, "6", T_(SS[0], SS[0], tmp, add))
                    did(ds, "7", T_(vk(tmp), vk(SS[0]), row(r_), mult))
                    did(ds, "8", v.tensor_reduce(so[:, 0, :], vk(tmp), AX.X, add))
                    col = lambda x: bc(x, 2, 16)
                    did(ds, "9", T_(kv(tmp), col(vecB[:, 1, :]), bc(vv[:, 1, :], 1, HD), mult))
                    did(ds, "10", STT(SS[1], SS[1], cc("gam"), tmp, mult, add))
                    did(ds, "11", T_(kv(tmp), kv(SS[1]), col(vecB[:, 0, :]), mult))
                    did(ds, "12", v.tensor_reduce(so[:, 1, :], kvT(tmp), AX.X, add))
                    did(ds, "13", S_(SS[2], SS[2], vecB[:, 7, 0:1], None, mult))
                    did(ds, "14", T_(kv(tmp), kv(SS[2]), col(vecB[:, 4, :]), mult))
                    did(ds, "15", v.tensor_reduce(sa[:, 1, :], kvT(tmp), AX.X, add))
                    did(ds, "16", T_(sa[:, 1, :], vv[:, 2, :], sa[:, 1, :], sub))
                    did(ds, "17", S_(sa[:, 1, :], sa[:, 1, :], vecB[:, 6, 0:1], None, mult))
                    did(ds, "18", T_(kv(tmp), col(vecB[:, 4, :]), bc(sa[:, 1, :], 1, HD), mult))
                    did(ds, "19", T_(SS[2], SS[2], tmp, add))
                    did(ds, "20", T_(kv(tmp), kv(SS[2]), col(vecB[:, 3, :]), mult))
                    v.tensor_reduce(so[:, 2, :], kvT(tmp), AX.X, add).then_inc(*ds.step("so"))
                    dve.wait_ge(*TR["pe_s"].at("oT"))
                    oT = psB[:, 2, 0:48].rearrange("p (i n b) -> p i n b", i=2, n=3)
                    outs3 = (RA[:, 2:4, :], RB[:, 4:6, :], RD[:, 4:6, :])
                    for n in range(3):
                        last = v.tensor_copy(outs3[n][:, :, SEQ:TT], oT[:, :, n, :])
                    did(ds, "oT", last)

                    pm, am, dm = TR["pe_m"], TR["act_m"], TR["dve_m"]
                    dve.wait_ge(*pm.at("mean"))
                    dve.wait_ge(s_out, layer * (16 * N_OUTPUTS) + 16 * N_OUTPUTS)
                    did(dm, "cen", STT(q4(outs3[0]), psB[:, :, 0:HALF], -1.0 / HD, q4(outs3[0]), mult, add))
                    dve.wait_ge(*am.at("rn"))
                    for n in range(3):
                        last = T_(outs3[n], outs3[n], ws[:, 2 * n:2 * n + 2, :], mult)
                    did(dm, "normed", last)
                    for i in range(2):
                        S_(outs3[0][:, i, :], outs3[0][:, i, :], par("ln_g", i), par("ln_b", i), mult, add)
                    did(dm, "gains", S_(outs3[2], outs3[2], par("gdn_g"), None, mult))
                    did(dm, "bonus", T_(outs3[0], outs3[0], RA[:, 0:2, :], add))
                    outs4 = (outs3[0], outs3[1], RC[:, 0:2, :], outs3[2])
                    zs = (RA[:, 7:9, :], RB[:, 6:8, :], RC[:, 2:4, :], RD[:, 6:8, :])
                    for n in range(4):
                        dve.wait_ge(*am.at("tz", n))
                        sz = ws[:, 6 + 2 * n:8 + 2 * n, :]
                        did(dm, "siluz", STT(sz, sz, 1.0, zs[n], add, mult), n)
                        did(dm, "gated", STT(outs4[n], outs4[n], 0.5, sz, mult, mult), n)
                    for idx in range(N_GATE):
                        b, jd, n = 2 * (idx % 2), idx // 4, idx % 4
                        dve.wait_ge(*pm.at("gate", idx))
                        dve.wait_ge(*am.at("th", idx))
                        th = half(ws[:, 8 + idx % 2, :])
                        up = psB[:, b:b + 2, 0:HALF]
                        if n == 0:
                            did(dm, "mul", STT(half(ws[:, jd, :]), th, 1.0, up, add, mult), idx)
                            v.tensor_copy(der[:, 36:37], der[:, 12:13]).then_inc(*dm.step("mg"))
                        else:
                            did(dm, "mul", STT(half(ws[:, 10, :]), th, 1.0, up, add, mult), idx)
                            did(dm, "mg", T_(ws[:, jd, :], ws[:, jd, :], ws[:, 10, :], add), idx)
                        dve.wait_ge(*dm.at("mg", idx))
                    for e in range(KT):
                        b = 2 * (e % 2)
                        dve.wait_ge(*pm.at("out", e))
                        gate = modT[:, 16 + e, :]
                        n1 = SEQ - HALF
                        STT(xT[:, e, 0:HALF], psA[:, b, 0:HALF], gate[:, 8:9], xT[:, e, 0:HALF], mult, add)
                        STT(xT[:, e, HALF:SEQ], psA[:, b + 1, 0:n1], gate[:, 8:9], xT[:, e, HALF:SEQ], mult, add)
                        did(dm, "xs", T_(der[:, 32:40], psA[:, b + 1, n1:HALF], gate[:, 0:8], mult), e)
                        did(dm, "x", T_(xT[:, e, SEQ:TT], xT[:, e, SEQ:TT], der[:, 32:40], add), e)

            nc.all_engine_barrier()
            nc.gpsimd.sem_clear(range(s_const.num, TR["dve_m"].sem.num + 1))
            nc.all_engine_barrier()

        with nc.Block() as block:
            pe9, act9, dve9 = TR["pe9"], TR["act9"], TR["dve9"]

            @block.scalar
            def _(act):
                A = nc.scalar.activation
                for d in range(KT):
                    A(ws[:, 10 + d, :], xT[:, d, :], ACT.Square).then_inc(*act9.step("sq"))
                act.wait_ge(*pe9.at("ss"))
                A(rs[:].rearrange("p (h c) -> p h c", h=2), psB[:, 2:4, 0:HALF], ACT.Ln, bias=cc("eps"), scale=1.0 / D_MODEL).then_inc(*act9.step("ln"))
                act.wait_ge(*act9.at("ln"))
                A(rs[:], rs[:], ACT.Exp, scale=-0.5).then_inc(*act9.step("rs"))
                for t in range(4):
                    act.wait_ge(*pe9.at("y", t))
                    ps = psA if t % 2 == 0 else psB
                    nc.scalar.copy(ws[:, 2 * t:2 * t + 2, 0:512], ps[:, 0:2, :]).then_inc(*act9.step("y"))

            @block.tensor
            def _(pe):
                for d in range(KT):
                    pe.wait_ge(*act9.at("sq", d))
                    for hf in range(2):
                        last = nc.tensor.matmul(psB[:, 2 + hf, 0:HALF], ones, ws[:, 10 + d, hf * HALF:(hf + 1) * HALF], start=(d == 0), stop=(d == KT - 1))
                last.then_inc(*pe9.step("ss"))
                pe.wait_ge(*dve9.at("y"))
                for t in range(4):
                    ps = psA if t % 2 == 0 else psB
                    if t >= 2:
                        pe.wait_ge(*act9.at("y", t - 2))
                    for d in range(KT):
                        last = nc.tensor.transpose(ps[:, d // 4, (d % 4) * P:(d % 4 + 1) * P], hT[:, d, t * P:(t + 1) * P], ident)
                    last.then_inc(*pe9.step("y"))
                for d in range(KT):
                    last = nc.tensor.transpose(psA[0:8, 2 + d // 4, (d % 4) * P:(d % 4 + 1) * P], hT[:, d, SEQ:TT], ident)
                last.then_inc(*pe9.step("ys"))

            @block.vector
            def _(dve):
                dve.wait_ge(*act9.at("rs"))
                for d in range(KT):
                    last = nc.vector.scalar_tensor_tensor(hT[:, d, :], xT[:, d, :], par("final_g", d), rs[:], mult, mult)
                last.then_inc(*dve9.step("y"))
                dve.wait_ge(*pe9.at("ys"))
                nc.vector.tensor_copy(ws[0:8, 8:10, 0:512], psA[0:8, 2:4, :]).then_inc(*dve9.step("ys"))

            @block.sync
            def _(sp):
                for t in range(4):
                    sp.wait_ge(*act9.at("y", t))
                    sp.dma_start(o["y_prompt"][0, t * P:(t + 1) * P, :].rearrange("p (a c) -> p a c", a=2), ws[:, 2 * t:2 * t + 2, 0:512]).then_inc(s_y, 16)
                sp.wait_ge(*dve9.at("ys"))
                sp.dma_start(o["y_sample"][:, 0, :].rearrange("p (a c) -> p a c", a=2), ws[0:8, 8:10, 0:512]).then_inc(s_y, 16)
                sp.wait_ge(s_y, 16 * 5)
    return {n: t.made for n, t in tracks.items()}


STEPS = {
    'pe0': 'xs c x x x x x x x x'.split(),
    'act0': 'tanh_c x x x x x x x x'.split(),
    'dve0': 'tmask silu_c xs c'.split(),
    'pe_f': 'par st ada ada ada ada ada ada ada ada ada ada ada ada ada ada ada ada ada ada ada ada ada ada ada ada ss mod proj proj proj proj proj proj proj proj proj proj proj proj proj proj proj proj proj proj proj proj proj proj proj proj proj proj proj proj proj proj'.split(),
    'act_f': 'sq sq sq sq sq sq sq sq modrow modrow modrow modrow modrow modrow lnx rs lam_abs lam_z expA proj proj proj proj proj proj proj proj proj proj proj proj proj proj proj proj proj proj proj proj proj proj proj proj proj proj proj proj proj proj'.split(),
    'dve_f': 'zero parT der stT lam1 lam2 lam3 lam4 lam5 lamm13 lama13 lamm11 lama11 lamm9 lama9 lamm7 lama7 lamm5 lama5 lamm3 lama3 lamm1 lama1 lam6 lam_y lam_sp modT G xn hg hs'.split(),
    'pe_a': 'crow lora lora kks bsum gram tr z y z y z y z y z y z y z x1 u o gram tr z y z y z y z y z y z y z x1 u o gram tr z y z y z y z y z y z y z x1 u o gram tr z y z y z y z y z y z y z x1 u o mt'.split(),
    'act_a': 'crow twd thw tha kk2 kf lnk rn decay exps rows y y y y y y x1 o rows y y y y y y x1 o rows y y y y y y x1 o rows y y y y y y x1 o mrow'.split(),
    'dve_a': 'diff pm kk lw1 scan mid lrel lex kkn bv pend bt prep gr t t t t t t t u sum st gr t t t t t t t u sum st gr t t t t t t t u sum st gr t t t t t t t u sum st'.split(),
    'pe_d': 'qs ks bcast bcast gb gram tr z y z y z y z y z y z y z x1 u o gb gram tr z y z y z y z y z y z y z x1 u o gb gram tr z y z y z y z y z y z y z x1 u o gb gram tr z y z y z y z y z y z y z x1 u o'.split(),
    'act_d': 'cv0 gabs gz ths sq lnq lnk rn egc col dexp y y y y y y u o col dexp y y y y y y u o col dexp y y y y y y u o col dexp y y y y y y u o'.split(),
    'dve_d': 'cvt cvt cvt cs1 cs2 cs3 cv g1 g2 g3 g4 g5 gm13 ga13 gm11 ga11 gm9 ga9 gm7 ga7 gm5 ga5 gm3 ga3 gm1 ga1 g6 gmax gsp gneg gc silu2 qk ar kbe prep dm gr rows t t t t t t t x1 st dm gr rows t t t t t t t x1 st dm gr rows t t t t t t t x1 st dm gr rows t t t t t t t x1 st'.split(),
    'pe_b': 'rot rot gram tr o gram tr o gram tr o gram tr o'.split(),
    'act_b': 'o o o o'.split(),
    'dve_b': 'rot rope rot rope sv prep gr rows st gr rows st gr rows st gr rows st'.split(),
    'pe_c': 'gates gates hrow'.split(),
    'act_c': 'cv0 thr thi au lnu root hrow'.split(),
    'dve_c': 'cvt cvt cvt cs1 cs2 cs3 xc u2 ix lndiff b h'.split(),
    'pe_s': 'rows oT'.split(),
    'act_s': 'rows'.split(),
    'dve_s': '1 2 3 4 5 6 7 8 9 10 11 12 13 14 15 16 17 18 19 20 so oT'.split(),
    'pool': ''.split(),
    'pe_m': 'mean var var var gl gate gl gate gl gate gl gate gl gate gl gate gl gate gl gate gl gate gl gate gl gate gl gate gl gate gl gate gl gate gl gate gl gate gl gate gl gate gl gate gl gate gl gate gl gate gl gate gl gate gl gate gl gate gl gate gl gate gl gate gl gate gl gate out out out out out out out out'.split(),
    'act_m': 'sq sq sq ln ln ln rn tz tz tz tz th th th th th th th th th th th th th th th th th th th th th th th th th th th th th th th th'.split(),
    'dve_m': 'cen normed gains bonus siluz gated siluz gated siluz gated siluz gated mul mg mul mg mul mg mul mg mul mg mul mg mul mg mul mg mul mg mul mg mul mg mul mg mul mg mul mg mul mg mul mg mul mg mul mg mul mg mul mg mul mg mul mg mul mg mul mg mul mg mul mg mul mg mul mg mul mg mul mg mul mg mul mg xs x xs x xs x xs x xs x xs x xs x xs x'.split(),
    'pe9': 'ss y y y y ys'.split(),
    'act9': 'sq sq sq sq sq sq sq sq ln rs y y y y'.split(),
    'dve9': 'y ys'.split(),
}


_INS = ['x_prompt', 'x_sample', 'c_prompt', 'c_sample', 'state_rwkv_wkv', 'state_rwkv_shift', 'state_ret', 'state_lru_h',
        'state_lru_conv', 'state_gdn', 'state_gdn_conv', 'ada_w', 'ada_b', 'norm_g', 'w_in', 'rwkv_mu', 'rwkv_w0', 'rwkv_w2',
        'rwkv_a0', 'rwkv_a2', 'rwkv_k_k', 'rwkv_k_a', 'rwkv_r_k', 'rwkv_ln_g', 'rwkv_ln_b', 'lru_conv_w', 'lru_conv_b',
        'lru_gate_w', 'lru_gate_b', 'lru_lambda', 'gdn_conv_w', 'gdn_A_log', 'gdn_dt_bias', 'gdn_norm_g', 'w_up', 'w_out',
        'final_g']
_STATES = [('wkv', (HEADS, HD, HD)), ('shift', (A_SHIFT,)), ('ret', (HEADS, HD, HD)), ('lru_h', (W,)),
           ('lru_conv', (CONV - 1, W)), ('gdn', (HEADS, HD, HD)), ('gdn_conv', (CONV - 1, QKV))]
_OUTS = ([('y_prompt', (1, SEQ, D_MODEL)), ('y_sample', (NB, 1, D_MODEL))]
         + [('p_' + n, (DEPTH, 1) + s) for n, s in _STATES] + [('s_' + n, (DEPTH, NB) + s) for n, s in _STATES])
PAST_LEN = 4096


def constants():
    import numpy as np
    f = np.float32
    cst = np.zeros((P, CONST_N), f)

    def put(name, value, p0=0):
        lo, hi = CONST_COLS[name]
        value = np.asarray(value, f)
        cst[p0:p0 + value.shape[0], lo:hi] = value.reshape(value.shape[0], -1)

    p, t = np.arange(P), np.arange(C)
    put("ident", np.eye(P))
    put("bones", p[:, None] // HD == p[None, :] // HD)
    put("ones", np.ones((P, P)))
    rot = np.zeros((P, P), f)
    for m in range(P):
        rot[m + 32 if m % HD < 32 else m - 32, m] = -1.0 if m % HD < 32 else 1.0
    put("rotp", rot)
    strict, incl = t[None, :] > p[:, None], t[None, :] >= p[:, None]
    put("rmask", np.stack([strict, incl, strict, incl], 1))
    put("negm", np.where(incl, 0.0, -1e30))
    lg = np.log(1.0 - 2.0 ** (-5.0 - np.arange(HEADS, dtype=np.float64)))
    rel = t[None, None, :] - p[:, None, None]
    put("rdec", np.where(rel >= 0, np.exp(lg[None, :, None] * np.maximum(rel, 0)), 0.0))
    head = 2 * np.arange(2)[None, :] + (p[:, None] // HD)
    put("qdec", np.exp(lg[head][:, :, None] * (t + 1.0)))
    put("kdec", np.exp(lg[None, :] * (C - 1.0 - p[:, None])))
    put("gc", np.exp(lg[head] * C))
    put("gam", np.exp(lg[p % HEADS])[:, None])
    pos = np.concatenate([np.arange(SEQ), np.full(NB, PAST_LEN)]).astype(f)
    inv = (f(10000.0) ** (-np.arange(32, dtype=f) / f(32))).astype(f)
    ang = (pos[None, :] * inv[p % 32][:, None]).astype(f)
    put("cos", np.cos(ang.astype(np.float64)))
    put("sin", np.sin(ang.astype(np.float64)))
    reset = np.ones(TT)
    reset[0:SEQ:C] = 0.0
    reset[SEQ:] = 0.0
    put("reset", np.tile(reset, (P, 1)))
    for base in (0, 32):
        put("sel4", (np.arange(HEADS)[:, None, None] == np.arange(HEADS)[None, :, None]) * np.ones((1, 1, P)), base)
        put("sel2", np.arange(HEADS)[:, None, None] == head.T[None, :, :], base)
    put("eps", np.full((P, 1), 1e-6))
    put("epsgn", np.full((P, 1), 64e-5))
    masks = np.zeros((P, 14, P), f)
    for lv in range(7):
        b = 1 << lv
        m = (p[:, None] // (2 * b) == p[None, :] // (2 * b)) & (p[:, None] // b % 2 == 1) & (p[None, :] // b % 2 == 0)
        masks[:, lv], masks[:, 7 + lv] = m, m.T
    return cst, masks.reshape(P, -1)


def kernel(**inputs):
    import numpy as _np
    import concourse.bacc as _bacc
    from concourse import mybir as _mybir
    from concourse.bass_utils import run_bass_kernel_spmd as _run

    nc = _bacc.Bacc("TRN2", target_bir_lowering=False, num_devices=1)
    arrays, ins, outs = {}, {}, {}
    given = {name: _np.ascontiguousarray(inputs[name]) for name in _INS}
    given["consts"], given["tree_masks"] = constants()
    for name, x in given.items():
        arrays[f"in_{name}"] = x
        ins[name] = nc.dram_tensor(f"in_{name}", x.shape, _mybir.dt.from_np(x.dtype), kind="ExternalInput").ap()
    for name, shape in _OUTS:
        outs[name] = nc.dram_tensor(f"out_{name}", shape, _mybir.dt.float32, kind="ExternalOutput").ap()
    build_program(nc, ins, outs, STEPS)
    r = _run(nc, [arrays], core_ids=[0])
    return tuple(r.results[0][f"out_{name}"] for name, _ in _OUTS)
```

```python
import concourse.bass as bass
from concourse import mybir
from contextlib import ExitStack

D_MODEL, SEQ, DEPTH, NB = 1024, 512, 2, 8
HEADS, HD = 4, 64
W = HEADS * HD
LORA = 64
CONV = 4
A_SHIFT = 3 * W + 2 * LORA
QKV = 3 * W
OFF_B = A_SHIFT + W
OFF_C = OFF_B + 4 * W
OFF_D = OFF_C + 2 * W
OFF_BA = OFF_D + QKV
OFF_DZ = OFF_BA + 2 * HEADS
OFF_G = OFF_DZ + W
IN_W = OFF_G + 4 * D_MODEL
P = 128
KT = D_MODEL // P
TT = SEQ + NB
HALF = TT // 2
C = 128
NC = SEQ // C
RING = 4
W_DECAY = -0.5 * 0.6065306597126334
LRU_C = 8.0

CONST_COLS = {}
_at = 0
for _name, _n in (("ident", 128), ("bones", 128), ("ones", 128), ("rotp", 128), ("rmask", 512), ("negm", 128),
                  ("rdec", 512), ("qdec", 256), ("cos", TT), ("sin", TT), ("reset", TT), ("sel4", 512),
                  ("sel2", 256), ("kdec", 4), ("gc", 2), ("gam", 1), ("eps", 1), ("epsgn", 1)):
    CONST_COLS[_name] = (_at, _at + _n)
    _at += _n
CONST_N = _at

PARAM_ROWS = {}
_at = 0
for _name, _n in (("ada_b", 24), ("norm_g", 8), ("mu", 7), ("w0", 2), ("a0", 2), ("k_k", 2), ("k_a", 2), ("r_k", 2),
                  ("ln_g", 2), ("ln_b", 2), ("lru_w", 8), ("lru_b", 2), ("gate_b", 4), ("lam", 2), ("gdn_w", 24),
                  ("gdn_g", 1), ("final_g", 8)):
    PARAM_ROWS[_name] = _at
    _at += _n
PARAM_N = _at


class Track:

    def __init__(self, sem, order):
        self.sem, self.order, self.n, self.where = sem, order, 0, {}
        for i, name in enumerate(order or []):
            self.where.setdefault(name, []).append(i + 1)
        self.made = []

    def step(self, name):
        self.n += 1
        self.made.append(name)
        if self.order is not None:
            assert self.order[self.n - 1] == name, (name, self.n, self.order[self.n - 1])
        return self.sem, 1

    def at(self, name, i=0):
        if self.order is None:
            return self.sem, 1
        return self.sem, self.where[name][i]


def build_program(nc, a, o, order):
    F32, U8 = mybir.dt.float32, mybir.dt.uint8
    ALU, ACT, AX = mybir.AluOpType, mybir.ActivationFunctionType, mybir.AxisListType
    mult, add, sub = ALU.mult, ALU.add, ALU.subtract
    ctx = ExitStack()
    tracks = {}
    with ctx:
        def sb(name, shape, dt=F32):
            return ctx.enter_context(nc.sbuf_tensor(name, shape, dt))

        def sem(name):
            return ctx.enter_context(nc.semaphore(name))

        def track(name):
            tracks[name] = Track(sem(name), order.get(name) if order else None)
            return tracks[name]

        cst = sb("cst", [P, CONST_N])
        tmask = sb("tmask", [P, 14, P], U8)
        xT = sb("xT", [P, KT, TT])
        hT = sb("hT", [P, KT, TT])
        RA = sb("RA", [P, 9, TT])
        RB = sb("RB", [P, 8, TT])
        RC = sb("RC", [P, 4, TT])
        RD = sb("RD", [P, 8, TT])
        ws = sb("ws", [P, 18, TT])
        bg = sb("bg", [36, TT])
        ring = sb("ring", [P, RING, KT, P])
        upw = sb("upw", [P, RING, 2, P])
        rs = sb("rs", [P, TT])
        parT = sb("parT", [P, P])
        prow = sb("prow", [P, P])
        der = sb("der", [P, 40])
        stT = sb("stT", [P, 7, 64])
        srow = ws[0:64, 0:2, :].rearrange("p a b -> p (a b)")[:, 0:A_SHIFT]
        modT = sb("modT", [P, 24, 9])
        G = sb("G", [P, KT, 9])
        cT = sb("cT", [P, KT, 9])
        w2 = sb("w2", [P, W])
        gw = sb("gw", [P, 4, P])
        crow = sb("crow", [11, 15 * P])
        hrow = sb("hrow", [9, W])
        mg5 = sb("mg", [P, 5, TT])
        mg = [RA[:, 0], RA[:, 1], RA[:, 8]] + [mg5[:, k] for k in range(5)]
        tg = sb("tg", [P, 2, TT])
        svA = sb("svA", [P, 6, NB, 2])
        svB = sb("svB", [P, 8, NB, 2])
        rowA = prow
        vecA = vecB = sb("vec", [P, 8, HD])
        vv = sb("vv", [P, 3, 16])
        so = sb("so", [P, 3, 16])
        sa = sb("sa", [P, 2, 16])
        orow = sb("orow", [NB, W])
        Mst = [sb(f"M{n}", [P, 2, HD]) for n in range(3)]
        mid = sb("mid", [P, 2, NC])
        pc = sb("pc", [P, 4, 2, NC])
        gp = sb("gp", [36, 4])
        colbg = sb("colbg", [P, 36])
        kdl = sb("kdl", [P, 8])
        mrow = sb("mrow", [HD, 2, P])
        psA = ctx.enter_context(nc.psum_tensor("psA", [P, 4, 512], F32))
        psB = ctx.enter_context(nc.psum_tensor("psB", [P, 4, 512], F32))
        scrA = nc.dram_tensor("scr_a", (6, NB, W), F32).ap()
        scrB = nc.dram_tensor("scr_b", (8, NB, W), F32).ap()
        scrO = nc.dram_tensor("scr_o", (3, NB, W), F32).ap()

        def cc(name, p0=0, p1=P):
            lo, hi = CONST_COLS[name]
            return cst[p0:p1, lo:hi]

        def par(name, j=0, n=1):
            r = PARAM_ROWS[name] + j
            return parT[:, r:r + n]

        def bc(ap, axis, n):
            ap = ap.unsqueeze(axis)
            s = list(ap.shape)
            s[axis] = n
            return ap.broadcast_to(s)

        ident, bones, ones = cc("ident"), cc("bones"), cc("ones")
        wf = ws[:, :, :].rearrange("p a b -> p (a b)")
        wfC = RC[:, :, :].rearrange("p a b -> p (a b)")
        wfA = RA[:, 4:8, :].rearrange("p a b -> p (a b)")

        def wv(tile, n):
            return wf[:, tile * TT:tile * TT + n]

        q4 = lambda ap: ap.rearrange("p i (h c) -> p (i h) c", h=2)

        s_out, s_so, s_scr, s_vec, s_ss, s_oread, s_y = (sem(n) for n in (
            "outputs_written", "decode_states_written", "scratch_written", "decode_vectors_in", "decode_states_in",
            "decode_rows_in", "y_written"))
        N_OUTPUTS = 14
        s_const, s_x, s_par, s_st, s_w2 = (sem(n) for n in ("const_in", "x_in", "params_in", "states_in", "small_weights_in"))
        s_w = [sem(f"ring_in{i}") for i in range(RING)]
        s_zero = sem("zeroed")
        s_seen = sem("register_wait_passed")
        TR = {n: track(n) for n in ("pe0", "act0", "dve0", "pe_f", "act_f", "dve_f", "pe_a", "act_a", "dve_a", "pe_d", "act_d",
                                    "dve_d", "pe_b", "act_b", "dve_b", "pe_c", "act_c", "dve_c", "pe_s", "act_s", "dve_s",
                                    "pe_p", "act_p", "pe_n", "act_n", "dve_n", "pe_m", "act_m", "dve_m", "pe9", "act9", "dve9")}
        pe0, act0, dve0 = TR["pe0"], TR["act0"], TR["dve0"]

        PROJ = ([(j * P, "A", j) for j in range(9)] + [(OFF_D + j * P, "D", j) for j in range(6)] + [(OFF_BA, "ba", 0)]
                + [(OFF_DZ + j * P, "D", 6 + j) for j in range(2)] + [(OFF_B + j * P, "B", j) for j in range(8)]
                + [(OFF_C + j * P, "C", j) for j in range(4)])
        N_ADA, N_PROJ, P_D, P_B, P_C = 24, 30, 9, 18, 26
        MERGE = [(n, j) for n in (0, 3, 1, 2) for j in range(KT)]
        RINGSEQ = ([("ada", n) for n in range(16)] + [("proj", n) for n in range(P_D)] + [("ada", n) for n in range(16, N_ADA)]
                   + [("proj", n) for n in range(P_D, P_C)] + [("gate", n) for n in range(8)]
                   + [("proj", n) for n in range(P_C, N_PROJ)] + [("gate", n) for n in range(8, 32)] + [("out", n) for n in range(KT)])
        PLACE = {x: r for r, x in enumerate(RINGSEQ)}
        RAW = {"A": RA, "B": RB, "C": RC, "D": RD}

        def ring_slot(kind, n):
            r = PLACE[kind, n]
            loads = 0
            for q in range(r % RING, r + 1, RING):
                k, m = RINGSEQ[q]
                loads += 2 if k == "gate" or (k == "proj" and PROJ[m][1] == "ba") else 1
            return r % RING, (s_w[r % RING], 16 * loads)

        with nc.Block() as block:
            @block.sync
            def _(sp):
                sp.dma_start(cst[:], a["consts"]).then_inc(s_const, 16)
                sp.dma_start(wv(10, 14 * P), a["tree_masks"]).then_inc(s_const, 16)
                for t in range(4):
                    sp.dma_start(hT[:, 2 * t:2 * t + 2, 0:512], a["x_prompt"][0, t * P:(t + 1) * P, :].rearrange("p (a c) -> p a c", a=2)).then_inc(s_x, 16)
                sp.dma_start(ws[0:8, 0:2, 0:512], a["x_sample"][:, 0, :].rearrange("p (a c) -> p a c", a=2)).then_inc(s_x, 16)
                sp.dma_start(ws[0:8, 2:4, 0:512], a["c_sample"].rearrange("p (a c) -> p a c", a=2)).then_inc(s_x, 16)
                sp.dma_start(ws[8:9, 2:4, 0:512], a["c_prompt"].rearrange("p (a c) -> p a c", a=2)).then_inc(s_x, 16)

            @block.gpsimd
            def _(pool):
                nc.gpsimd.memset(gw[:], 0.0).then_inc(s_zero, 1)
                nc.gpsimd.memset(bg[:], 0.0).then_inc(s_zero, 1)
                pool.wait_ge(s_zero, 2)

            @block.scalar
            def _(act):
                act.wait_ge(s_x, 16 * 7)
                nc.scalar.activation(ws[0:9, 4:6, 0:512], ws[0:9, 2:4, 0:512], ACT.Tanh, scale=0.5).then_inc(*act0.step("tanh_c"))
                for d in range(KT):
                    act.wait_ge(*pe0.at("x", d))
                    nc.scalar.copy(xT[:, d, 0:SEQ], psA[:, d % 4, :]).then_inc(*act0.step("x"))

            @block.vector
            def _(dve):
                dve.wait_ge(s_const, 32)
                nc.vector.tensor_copy(tmask[:], wv(10, 14 * P).rearrange("p (m t) -> p m t", m=14)).then_inc(*dve0.step("tmask"))
                dve.wait_ge(*act0.at("tanh_c"))
                nc.vector.scalar_tensor_tensor(ws[0:9, 4:6, 0:512], ws[0:9, 4:6, 0:512], 1.0, ws[0:9, 2:4, 0:512], add, mult).then_inc(*dve0.step("silu_c"))
                dve.wait_ge(*pe0.at("xs"))
                nc.vector.tensor_copy(xT[:, :, SEQ:TT], psB[:, 0, 0:64].rearrange("p (d b) -> p d b", d=KT)).then_inc(*dve0.step("xs"))
                dve.wait_ge(*pe0.at("c"))
                nc.vector.tensor_scalar(cT[:], psB[:, 1, 0:72].rearrange("p (d b) -> p d b", d=KT), 0.5, None, mult).then_inc(*dve0.step("c"))
                dve.wait_ge(*dve0.at("c"))

            @block.tensor
            def _(pe):
                pe.wait_ge(s_const, 32)
                pe.wait_ge(s_x, 16 * 7)
                for d in range(KT):
                    last = nc.tensor.transpose(psB[:, 0, 8 * d:8 * d + 8], ws[0:8, d // 4, (d % 4) * P:(d % 4 + 1) * P], ident[0:8, 0:8])
                last.then_inc(*pe0.step("xs"))
                pe.wait_ge(*dve0.at("silu_c"))
                for d in range(KT):
                    last = nc.tensor.transpose(psB[:, 1, 9 * d:9 * d + 9], ws[0:9, 4 + d // 4, (d % 4) * P:(d % 4 + 1) * P], ident[0:9, 0:9])
                last.then_inc(*pe0.step("c"))
                for d in range(KT):
                    if d >= 4:
                        pe.wait_ge(*act0.at("x", d - 4))
                    for t in range(4):
                        last = nc.tensor.transpose(psA[:, d % 4, t * P:(t + 1) * P], hT[:, 2 * t + d // 4, (d % 4) * P:(d % 4 + 1) * P], ident)
                    last.then_inc(*pe0.step("x"))

        nc.all_engine_barrier()

        with nc.Fori(0, DEPTH) as layer:
            with nc.Block() as block:
                pe_f, act_f, dve_f = TR["pe_f"], TR["act_f"], TR["dve_f"]
                pp, ap = TR["pe_p"], TR["act_p"]
                pn, an, dn = TR["pe_n"], TR["act_n"], TR["dve_n"]
                pm, am, dm = TR["pe_m"], TR["act_m"], TR["dve_m"]
                ps_, as_, ds = TR["pe_s"], TR["act_s"], TR["dve_s"]
                def merged_at(idx):
                    return dm.at("mul", idx) if idx < KT else dm.at("mg", idx - KT)

                def ring_done(r):
                    kind, n = RINGSEQ[r]
                    return {"ada": pe_f, "proj": pp, "gate": pm, "out": pm}[kind].at(kind, n)

                @block.sync
                def _(sp):
                    for r, (kind, n) in enumerate(RINGSEQ):
                        s, (arrived, _) = ring_slot(kind, n)
                        if r >= RING:
                            sp.wait_ge(*ring_done(r - RING))
                        if kind == "ada":
                            src = a["ada_w"][layer, :, n * P:(n + 1) * P]
                        elif kind == "proj":
                            col, name, _ = PROJ[n]
                            if name == "ba":
                                for e in range(2):
                                    sp.dma_start(ring[:, s, :, 32 * e:32 * e + HEADS],
                                                 a["w_in"][layer, :, col + HEADS * e:col + HEADS * (e + 1)]
                                                 .rearrange("(k p) c -> p k c", p=P)).then_inc(arrived, 16)
                                continue
                            src = a["w_in"][layer, :, col:col + P]
                        elif kind == "gate":
                            br, j = MERGE[n]
                            src = a["w_in"][layer, :, OFF_G + br * D_MODEL + j * P:OFF_G + br * D_MODEL + (j + 1) * P]
                            sp.dma_start(upw[:, s, :, :], a["w_up"][layer, br, :, j * P:(j + 1) * P]
                                         .rearrange("(i p) c -> p i c", p=P)).then_inc(arrived, 16)
                        else:
                            src = a["w_out"][layer, :, n * P:(n + 1) * P]
                        sp.dma_start(ring[:, s, :, :], src.rearrange("(k p) c -> p k c", p=P)).then_inc(arrived, 16)

                N_PAR, N_ST, N_W2 = 1, 1, 8

                DEC = (("state_rwkv_wkv", "s_wkv", 0, wfC, 3), ("state_gdn", "s_gdn", 3, wfA, 5), ("state_ret", "s_ret", 0, wfA, 2))
                in_layer = lambda base, per, n: layer * (16 * per) + 16 * n

                @block.gpsimd
                def _(pool):
                    def seen():
                        pool.sem_inc(s_seen, 1)

                    def decode_state(n):
                        key, _, _, mem, _ = DEC[n]
                        for q in range(4):
                            pr = slice(32 * q, 32 * q + 32)
                            if n == 0:
                                pool.dma_start(mem[pr, 0:1024], a[key][layer].rearrange("b h (q v) k -> q (b h) (v k)", q=4)[q]).then_inc(s_ss, 16)
                            else:
                                pool.dma_start(mem[pr, 0:1024].rearrange("p (k v) -> p k v", v=16),
                                               a[key][layer].rearrange("b h k (q v) -> q (b h) k v", q=4)[q]).then_inc(s_ss, 16)

                    def decode_vectors(n):
                        lo, num = (0, 6) if n == 0 else ((3, 5) if n == 1 else (0, 3))
                        scr, vec = (scrA, vecA) if n == 0 else (scrB, vecB)
                        pool.wait_ge(*as_.at("rows", n))
                        pool.dma_start(scr[lo:lo + num].rearrange("n b (i c) -> (n b i) c", i=2), rowA[0:16 * num, :]).then_inc(s_scr, 16)
                        pool.wait_ge(s_scr, in_layer(0, 15, 5 * n + 1))
                        seen()
                        for q in range(4):
                            pr = slice(32 * q, 32 * q + 32)
                            pool.dma_start(vec[pr, lo:lo + num, :], scr[lo:lo + num].rearrange("n b (h d) -> (b h) n d", h=HEADS)).then_inc(s_vec, 16)
                            pool.dma_start(vv[pr, n, :], scr[(3, 5, 2)[n]].rearrange("b (h q v) -> q (b h) v", h=HEADS, q=4)[q]).then_inc(s_vec, 16)

                    def decode_results(n):
                        _, key, _, mem, _ = DEC[n]
                        pool.wait_ge(*ds.at("so", n))
                        for q in range(4):
                            pr = slice(32 * q, 32 * q + 32)
                            pool.dma_start(scrO[n].rearrange("b (h q v) -> q (b h) v", h=HEADS, q=4)[q], so[pr, n, :]).then_inc(s_scr, 16)
                        pool.wait_ge(s_scr, in_layer(0, 15, 5 * n + 5))
                        seen()
                        if n:
                            pool.wait_ge(*ps_.at("oT", n - 1))
                        pool.dma_start(orow[:], scrO[n]).then_inc(s_oread, 16)
                        for q in range(4):
                            pr = slice(32 * q, 32 * q + 32)
                            if n == 0:
                                pool.dma_start(o[key][layer].rearrange("b h (q v) k -> q (b h) (v k)", q=4)[q], mem[pr, 0:1024]).then_inc(s_so, 16)
                            else:
                                pool.dma_start(o[key][layer].rearrange("b h k (q v) -> q (b h) k v", q=4)[q],
                                               mem[pr, 0:1024].rearrange("p (k v) -> p k v", v=16)).then_inc(s_so, 16)

                    decode_state(0)
                    pool.wait_ge(*TR["act_a"].at("crow"))
                    pool.dma_start(o["p_shift"][layer], crow[2:3, 0:A_SHIFT]).then_inc(s_out, 16)
                    pool.dma_start(o["s_shift"][layer], crow[3:11, 0:A_SHIFT]).then_inc(s_out, 16)
                    pool.dma_start(o["s_lru_conv"][layer, :, 0:2, :], a["state_lru_conv"][layer, :, 1:3, :]).then_inc(s_out, 16)
                    pool.dma_start(o["s_gdn_conv"][layer, :, 0:2, :], a["state_gdn_conv"][layer, :, 1:3, :]).then_inc(s_out, 16)
                    decode_vectors(0)
                    decode_results(0)
                    pool.wait_ge(*TR["act_d"].at("crow"))
                    pool.dma_start(o["p_gdn_conv"][layer, 0], crow[0:3, 9 * P:15 * P]).then_inc(s_out, 16)
                    pool.dma_start(o["s_gdn_conv"][layer, :, 2, :], crow[3:11, 9 * P:15 * P]).then_inc(s_out, 16)
                    pool.wait_ge(*TR["act_a"].at("mrow"))
                    for i in range(2):
                        pool.dma_start(o["p_wkv"][layer, 0, 2 * i:2 * i + 2].rearrange("g v k -> v g k"),
                                       mrow[:, i, :].rearrange("v (g k) -> v g k", g=2)).then_inc(s_out, 16)
                    pool.wait_ge(*dn.at("gated", 0))
                    decode_state(1)
                    decode_vectors(1)
                    decode_results(1)
                    pool.wait_ge(s_so, in_layer(0, 12, 8))
                    seen()
                    decode_state(2)
                    pool.wait_ge(*TR["dve_d"].at("st", NC - 1))
                    pool.dma_start(o["p_gdn"][layer, 0].rearrange("(i g) k v -> (g k) i v", g=2), Mst[2][:]).then_inc(s_out, 16)
                    decode_vectors(2)
                    decode_results(2)
                    pool.wait_ge(*TR["act_c"].at("crow"))
                    pool.dma_start(o["p_lru_conv"][layer, 0], crow[0:3, 7 * P:9 * P]).then_inc(s_out, 16)
                    pool.dma_start(o["s_lru_conv"][layer, :, 2, :], crow[3:11, 7 * P:9 * P]).then_inc(s_out, 16)
                    pool.wait_ge(*TR["dve_b"].at("st", NC - 1))
                    pool.dma_start(o["p_ret"][layer, 0].rearrange("(i g) k v -> (g k) i v", g=2), Mst[1][:]).then_inc(s_out, 16)
                    pool.wait_ge(*TR["act_c"].at("hrow"))
                    pool.dma_start(o["p_lru_h"][layer], hrow[0:1, :]).then_inc(s_out, 16)
                    pool.dma_start(o["s_lru_h"][layer], hrow[1:9, :]).then_inc(s_out, 16)
                    pool.wait_ge(s_out, in_layer(0, N_OUTPUTS, N_OUTPUTS))
                    pool.wait_ge(s_so, in_layer(0, 12, 12))

                def headsum(src):
                    s4 = q4(src)
                    for k in range(4):
                        last = nc.tensor.matmul(psB[:, k, 0:HALF], bones, s4[:, k, :], start=True, stop=True)
                    return last

                def slot(h):
                    return 2 * (h % 2) + h // 2

                def hp(h):
                    return slice(HD * (h % 2), HD * (h % 2) + HD)

                def mats(base, sizes):
                    out, at = [], base
                    for n in sizes:
                        out.append(wf[:, at:at + n])
                        at += n
                    return out
                GRa, Ta, Va, Ya, rowsa, X1a, Ua = mats(0, (2048, 512, 512, 512, 768, 256, 256))
                Dd, GRd, Td, Vd, Yd, rowsd, X1d, Ud = mats(10 * TT, (512, 1024, 512, 512, 512, 512, 256, 256))
                h4 = lambda ap: ap.rearrange("p (h t) -> p h t", h=HEADS)
                GRa4, GRd4 = h4(GRa), h4(GRd)
                AtA, AtD = GRa4[:, :, 0:P], GRd4[:, :, 0:P]
                ARa = wv(10, 2048).rearrange("p (i c x t) -> p i c x t", i=2, c=NC, x=2)
                ARd = RD[:, 0:4, :].rearrange("p a b -> p (a b)")[:, 0:2048].rearrange("p (i c x t) -> p i c x t", i=2, c=NC, x=2)
                ch = lambda c: slice(c * C, (c + 1) * C)
                G1b, krb, vrb = mats(4 * TT, (512, 256, 256))

                def pe_tree(pe, tp, td, ta, At, T, V, Y, c):
                    T4, V4, Y4 = h4(T), h4(V), h4(Y)
                    for g in range(2):
                        for n in range(2):
                            last = nc.tensor.matmul(psB[:, 2 + g, n * P:(n + 1) * P], At[:, 2 * g + n, :], ident, start=True, stop=True)
                        last.then_inc(*tp.step("z"))
                    for lv in range(1, 7):
                        for g in range(2):
                            pe.wait_ge(*td.at("t", 14 * c + 2 * (lv - 1) + g))
                            for n in range(2):
                                h = 2 * g + n
                                last = nc.tensor.matmul(psB[:, 2 + g, n * P:(n + 1) * P], At[:, h, :], T4[:, h, :], start=True, stop=True)
                            last.then_inc(*tp.step("y"))
                        for g in range(2):
                            pe.wait_ge(*ta.at("y", 12 * c + 2 * (lv - 1) + g))
                            for n in range(2):
                                h = 2 * g + n
                                if lv < 6:
                                    nc.tensor.matmul(psB[:, 2 + g, n * P:(n + 1) * P], V4[:, h, :], Y4[:, h, :], start=True, stop=True)
                                last = nc.tensor.matmul(psB[:, 2 + g, 256 + n * P:256 + (n + 1) * P], Y4[:, h, :], V4[:, h, :], start=True, stop=True)
                            last.then_inc(*tp.step("z"))

                def act_tree(act, tp, ta, Y, c):
                    for lv in range(1, 7):
                        for g in range(2):
                            act.wait_ge(*tp.at("y", 12 * c + 2 * (lv - 1) + g))
                            nc.scalar.copy(Y[:, 256 * g:256 * g + 256], psB[:, 2 + g, 0:256]).then_inc(*ta.step("y"))

                def dve_tree(dve, tp, td, At, T, V, c):
                    T4, V4 = h4(T), h4(V)
                    two = lambda ap: ap.rearrange("p (h t) -> p h t", h=2)
                    for lv in range(7):
                        for g in range(2):
                            dve.wait_ge(*tp.at("z", 14 * c + 2 * lv + g))
                            if lv:
                                dve.wait_ge(*td.at("t", 14 * c + 2 * (lv - 1) + g))
                            hs = slice(2 * g, 2 * g + 2)
                            zt = At[:, hs, :] if lv == 0 else two(psB[:, 2 + g, 256:512])
                            if lv < 6:
                                nc.vector.copy_predicated(T4[:, hs, :], bc(tmask[:, lv, :], 1, 2), two(psB[:, 2 + g, 0:256]))
                            nc.vector.copy_predicated(V4[:, hs, :], bc(tmask[:, 7 + lv, :], 1, 2), zt).then_inc(*td.step("t"))

                @block.tensor
                def _(pe):
                    pa, pd, pb, pcc = (TR[n] for n in ("pe_a", "pe_d", "pe_b", "pe_c"))
                    aa, da, ad, dd, ab, db, ac, dc = (TR[n] for n in ("act_a", "dve_a", "act_d", "dve_d", "act_b", "dve_b", "act_c", "dve_c"))

                    def proj(idx, hf=None):
                        s, arrived = ring_slot("proj", idx)
                        m = P if PROJ[idx][1] != "ba" else 36
                        if hf != 1:
                            pe.wait_ge(*arrived)
                            if idx == P_C:
                                pe.wait_ge(*am.at("th", 7))
                            elif idx == P_C + 1:
                                pe.wait_ge(*dm.at("mul", 7))
                            elif idx >= 2:
                                pe.wait_ge(*ap.at("proj", idx - 2))
                            if idx == P_D:
                                pe.wait_ge(*act_f.at("modrow", 4))
                        for k in range(KT):
                            if idx == 0:
                                pe.wait_ge(*dve_f.at("hs", k))
                            for x in ((0, 1) if hf is None else (hf,)):
                                last = nc.tensor.matmul(psA[0:m, 2 * (idx % 2) + x, 0:HALF], ring[:, s, k, 0:m], hT[:, k, x * HALF:(x + 1) * HALF],
                                                        start=(k == 0), stop=(k == KT - 1))
                        if hf != 0:
                            last.then_inc(*pp.step("proj"))

                    outs = (RA[:, 2:4, :], RB[:, 4:6, :], RC[:, 0:2, :], RD[:, 4:6, :])

                    def merge(idx):
                        s, arrived = ring_slot("gate", idx)
                        pe.wait_ge(*arrived)
                        if idx == 0:
                            pe.wait_ge(*ap.at("proj", P_C - 1))
                            pe.wait_ge(*dn.at("gated", 0))
                        elif idx == 8:
                            pe.wait_ge(*ap.at("proj", N_PROJ - 1))
                            pe.wait_ge(*dn.at("gated", 1))
                        else:
                            pe.wait_ge(*am.at("th", idx - 1))
                        for k in range(KT):
                            for hf in range(2):
                                last = nc.tensor.matmul(psA[:, hf, 0:HALF], ring[:, s, k, :], hT[:, k, hf * HALF:(hf + 1) * HALF],
                                                        start=(k == 0), stop=(k == KT - 1))
                        last.then_inc(*pm.step("gl"))
                        if idx in (16, 24):
                            pe.wait_ge(*dn.at("gated", idx // 8))
                        if idx not in (0, 8):
                            pe.wait_ge(*dm.at("mul", idx - 1))
                        for i in range(2):
                            for hf in range(2):
                                last = nc.tensor.matmul(psA[:, 2 + hf, 0:HALF], upw[:, s, i, :], outs[MERGE[idx][0]][:, i, hf * HALF:(hf + 1) * HALF],
                                                        start=(i == 0), stop=(i == 1))
                        last.then_inc(*pm.step("gate"))

                    def crow_rows(tiles, at, b, step):
                        for n, t in enumerate(tiles):
                            last = nc.tensor.transpose(psB[0:11, b + n // 4, (n % 4) * P:(n % 4 + 1) * P], t[:, SEQ - 3:TT], ident)
                        last.then_inc(*step)

                    for d in range(KT):
                        pe.wait_ge(*act_f.at("sq", d))
                        for hf in range(2):
                            last = nc.tensor.matmul(psB[:, 2 + hf, 0:HALF], ones, ws[:, 10 + d, hf * HALF:(hf + 1) * HALF],
                                                    start=(d == 0), stop=(d == KT - 1))
                    last.then_inc(*pe_f.step("ss"))

                    def ada(n, out):
                        s, arrived = ring_slot("ada", n)
                        pe.wait_ge(*arrived)
                        for k in range(KT):
                            last = nc.tensor.matmul(out, cT[:, k, :], ring[:, s, k, :], start=(k == 0), stop=(k == KT - 1))
                        last.then_inc(*pe_f.step("ada"))

                    for r in range(16):
                        ada(r, psA[0:9, r // 4, (r % 4) * P:(r % 4 + 1) * P])
                        if r == 7:
                            pe.wait_ge(s_par, 16 * N_PAR)
                            nc.tensor.transpose(psB[:, 0, 0:PARAM_N], prow[0:PARAM_N, :], ident[0:PARAM_N, 0:PARAM_N]).then_inc(*pe_f.step("par"))
                            pe.wait_ge(s_st, 16 * N_ST)
                            for j in range(7):
                                last = nc.tensor.transpose(psB[:, 1, 64 * j:64 * j + 64], srow[:, j * P:(j + 1) * P], ident[0:64, 0:64])
                            last.then_inc(*pe_f.step("st"))
                    pe.wait_ge(*act_f.at("modrow", 3))
                    pe.wait_ge(*dve_f.at("stT"))
                    for r in range(16):
                        last = nc.tensor.transpose(psB[:, 1, 9 * r:9 * r + 9], ws[0:9, 4 + r // 4, (r % 4) * P:(r % 4 + 1) * P], ident[0:9, 0:9])
                    last.then_inc(*pe_f.step("mod"))
                    for idx in range(P_D):
                        proj(idx)

                    pe.wait_ge(*ap.at("proj", 7))
                    for r in range(16, N_ADA):
                        ada(r, psA[0:9, r // 4 - 2, (r % 4) * P:(r % 4 + 1) * P])
                    pe.wait_ge(*ap.at("proj", 8))
                    crow_rows([RA[:, j] for j in range(7)], 0, 0, pa.step("crow"))
                    pe.wait_ge(*act_f.at("modrow", 4))
                    for r in range(8):
                        last = nc.tensor.transpose(psB[:, 2, 9 * r:9 * r + 9], mg5[0:9, r // 4, (r % 4) * P:(r % 4 + 1) * P], ident[0:9, 0:9])
                    last.then_inc(*pe_f.step("mod"))
                    proj(9)
                    proj(10)
                    pe.wait_ge(*aa.at("twd"))
                    pe.wait_ge(*aa.at("crow"))
                    pe.wait_ge(*dve_f.at("modT", 1))
                    pe.wait_ge(s_w2, 16 * N_W2)
                    for g in range(2):
                        gr = slice(64 * g, 64 * g + 64)
                        if g:
                            pe.wait_ge(*aa.at("thw"))
                        for i in range(2):
                            for hf in range(2):
                                last = nc.tensor.matmul(psB[:, 2 * i + hf, 0:HALF], w2[gr, i * P:(i + 1) * P], RA[gr, 6, hf * HALF:(hf + 1) * HALF],
                                                        start=True, stop=True)
                        last.then_inc(*pa.step("lora"))
                        proj(11 + g)
                    pe.wait_ge(*aa.at("kk2"))
                    pe.wait_ge(*aa.at("tha"))
                    headsum(ws[:, 10:12, :]).then_inc(*pa.step("kks"))
                    for idx in range(13, 17):
                        proj(idx)
                    pe.wait_ge(*da.at("bt"))
                    pe.wait_ge(*aa.at("lnk"))
                    headsum(ws[:, 6:8, :]).then_inc(*pa.step("bsum"))
                    proj(17)
                    pe.wait_ge(*da.at("prep"))
                    nc.tensor.transpose(psB[0:96, 0, 0:P], svA[:].rearrange("p n b i -> p (n b i)"), ident).then_inc(*ps_.step("rows"))
                    pe.wait_ge(*as_.at("rows", 0))
                    Ma = Mst[0]
                    for c in range(NC):
                        if c:
                            pe.wait_ge(*da.at("st", c - 1))
                            pe.wait_ge(*aa.at("o", c - 1))
                        for h in range(HEADS):
                            i = h // 2
                            for x, t in enumerate((14, 16)):
                                last = nc.tensor.matmul(psB[:, h, 256 * x:256 * x + 256], ws[hp(h), t + i, ch(c)], ARa[hp(h), i, c, :, :],
                                                        start=True, stop=True)
                        last.then_inc(*pa.step("gram"))
                        if c < 3:
                            proj(P_B + 2 * c, 0)
                        pe.wait_ge(*da.at("gr", 2 * c + 1))
                        for n, src in enumerate((ws[:, 14], ws[:, 15], ws[:, 16], ws[:, 17], RA[:, 4], RA[:, 5])):
                            last = nc.tensor.transpose(psB[:, n // 4, (n % 4) * P:(n % 4 + 1) * P], src[:, ch(c)], ident)
                        last.then_inc(*pa.step("tr"))
                        pe.wait_ge(*aa.at("rows", c))
                        pe_tree(pe, pa, da, aa, AtA, Ta, Va, Ya, c)
                        pe.wait_ge(*da.at("t", 14 * c + 13))
                        V4 = h4(Va)
                        for h in range(HEADS):
                            out = psB[:, h % 2, (h // 2) * HD:(h // 2 + 1) * HD]
                            nc.tensor.matmul(out, ARa[hp(h), h // 2, c, 0, :], Ma[hp(h), h // 2, :], start=True, stop=False)
                            last = nc.tensor.matmul(out, GRa4[:, h, 256:384], rowsa[:, 512 + h * HD:512 + (h + 1) * HD], start=False, stop=True)
                        last.then_inc(*pa.step("x1"))
                        if c < 3:
                            proj(P_B + 2 * c, 1)
                        pe.wait_ge(*aa.at("x1", c))
                        for h in range(HEADS):
                            last = nc.tensor.matmul(psB[:, 2, h * HD:(h + 1) * HD], V4[:, h, :], X1a[:, h * HD:(h + 1) * HD], start=True, stop=True)
                        last.then_inc(*pa.step("u"))
                        pe.wait_ge(*da.at("u", c))
                        for h in range(HEADS):
                            out = psB[hp(h), h % 2, (h // 2) * P:(h // 2 + 1) * P]
                            nc.tensor.matmul(out, Ma[hp(h), h // 2, :], ARa[hp(h), h // 2, c, 1, :], start=True, stop=False)
                            nc.tensor.matmul(out, Ua[:, h * HD:(h + 1) * HD], GRa4[:, h, 128:256], start=False, stop=False)
                            nc.tensor.matmul(out, rowsa[:, 512 + h * HD:512 + (h + 1) * HD], GRa4[:, h, 384:512], start=False, stop=True)
                        for i in range(2):
                            s2 = slice(i * P, (i + 1) * P)
                            nc.tensor.matmul(psB[:, 3, s2], rowsa[:, i * P:(i + 1) * P], Ua[:, s2], start=True, stop=False)
                            last = nc.tensor.matmul(psB[:, 3, s2], rowsa[:, 256 + i * P:256 + (i + 1) * P], rowsa[:, 512 + i * P:512 + (i + 1) * P], start=False, stop=True)
                        last.then_inc(*pa.step("o"))
                        if c < 3:
                            proj(P_B + 2 * c + 1)
                    pe.wait_ge(*da.at("st", NC - 1))
                    pe.wait_ge(*aa.at("o", NC - 1))
                    for i in range(2):
                        last = nc.tensor.transpose(psB[0:HD, 0, i * P:(i + 1) * P], Ma[:, i, :], ident)
                    last.then_inc(*pa.step("mt"))
                    pe.wait_ge(*aa.at("mrow"))


                    def oT_rows(n):
                        pe.wait_ge(s_oread, in_layer(0, 3, n + 1))
                        pe.sem_inc(s_seen, 1)
                        for i in range(2):
                            last = nc.tensor.transpose(psB[:, 1, NB * i:NB * i + NB], orow[:, i * P:(i + 1) * P], ident[0:NB, 0:NB])
                        last.then_inc(*ps_.step("oT"))

                    def norm_sums(n, src):
                        pe.wait_ge(*ds.at("oT", n))
                        if n == 0:
                            headsum(src).then_inc(*pn.step("mean"))
                            proj(P_C - 2)
                        pe.wait_ge(*an.at("sq", n))
                        headsum(ws[:, 0:2, :]).then_inc(*pn.step("var"))

                    oT_rows(0)
                    norm_sums(0, RA[:, 2:4, :])
                    proj(P_C - 1)
                    pe.wait_ge(*an.at("ln", 0))
                    crow_rows([RD[:, j] for j in range(6)], 9, 0, pd.step("crow"))
                    for idx in range(4):
                        merge(idx)
                    pe.wait_ge(*ad.at("crow"))
                    pe.wait_ge(*ad.at("sq"))
                    headsum(RD[:, 0:2, :]).then_inc(*pd.step("qs"))
                    merge(4)
                    pe.wait_ge(*ad.at("lnq"))
                    headsum(RD[:, 2:4, :]).then_inc(*pd.step("ks"))
                    merge(5)
                    pe.wait_ge(*ad.at("lnk"))
                    pe.wait_ge(*dd.at("gc"))
                    sel2 = cc("sel2").rearrange("p (i t) -> p i t", i=2)
                    for g in range(2):
                        gr = slice(32 * g, 32 * g + HEADS)
                        if g:
                            merge(6)
                            pe.wait_ge(*dd.at("ar"))
                        for i in range(2):
                            nc.tensor.matmul(psB[:, i, :], sel2[gr, i, :], bg[gr, 0:SEQ], start=True, stop=True)
                        for i in range(2):
                            last = nc.tensor.matmul(psB[:, 2, 8 * i:8 * i + 8], sel2[gr, i, :], bg[gr, SEQ:TT], start=True, stop=True)
                        last.then_inc(*pd.step("bcast"))
                    merge(7)
                    pe.wait_ge(*dd.at("prep"))
                    nc.tensor.transpose(psB[0:80, 3, 0:P], svB[:, 3:8].rearrange("p n b i -> p (n b i)"), ident).then_inc(*ps_.step("rows"))
                    pe.wait_ge(*as_.at("rows", 1))
                    Md = Mst[2]
                    sel4 = h4(cc("sel4"))
                    rd4 = h4(GRd)
                    for c in range(NC):
                        if c:
                            pe.wait_ge(*dd.at("st", c - 1))
                            pe.wait_ge(*ad.at("o", c - 1))
                        for h in range(HEADS):
                            nc.tensor.matmul(psB[:, 0, h * P:(h + 1) * P], sel4[32:36, h, :], bg[32:36, ch(c)], start=True, stop=True)
                        nc.tensor.transpose(psB[:, 1, 0:36], bg[:, ch(c)], ident[0:36, 0:36]).then_inc(*pd.step("gb"))
                        for h in range(HEADS):
                            last = nc.tensor.matmul(psB[:, 2 + h % 2, (h // 2) * 256:(h // 2) * 256 + 256], ws[hp(h), 2 + h // 2, ch(c)],
                                                    ARd[hp(h), h // 2, c, :, :], start=True, stop=True)
                        last.then_inc(*pd.step("gram"))
                        proj(P_C + c, 0)
                        pe.wait_ge(*dd.at("dm", c))
                        for n in range(4):
                            last = nc.tensor.transpose(psB[:, 0, n * P:(n + 1) * P], ws[:, 2 + n, ch(c)], ident)
                        last.then_inc(*pd.step("tr"))
                        pe.wait_ge(*dd.at("gr", 2 * c + 1))
                        pe.wait_ge(*ad.at("col", c))
                        pe_tree(pe, pd, dd, ad, AtD, Td, Vd, Yd, c)
                        pe.wait_ge(*dd.at("rows", c))
                        pe.wait_ge(*dd.at("t", 14 * c + 13))
                        for h in range(HEADS):
                            last = nc.tensor.matmul(psB[:, h % 2, (h // 2) * HD:(h // 2 + 1) * HD], RD[hp(h), 4 + h // 2, ch(c)], Md[hp(h), h // 2, :], start=True, stop=True)
                        last.then_inc(*pd.step("x1"))
                        proj(P_C + c, 1)
                        pe.wait_ge(*dd.at("x1", c))
                        for h in range(HEADS):
                            last = nc.tensor.matmul(psB[:, 2, h * HD:(h + 1) * HD], h4(Vd)[:, slot(h), :], X1d[:, h * HD:(h + 1) * HD], start=True, stop=True)
                        last.then_inc(*pd.step("u"))
                        pe.wait_ge(*ad.at("u", c))
                        for h in range(HEADS):
                            out = psB[hp(h), h % 2, (h // 2) * P:(h // 2 + 1) * P]
                            nc.tensor.matmul(out, Md[hp(h), h // 2, :], ws[hp(h), 6 + h // 2, ch(c)], start=True, stop=False)
                            nc.tensor.matmul(out, Ud[:, h * HD:(h + 1) * HD], rd4[:, slot(h), 128:256], start=False, stop=True)
                        for i in range(2):
                            s2 = slice(i * P, (i + 1) * P)
                            last = nc.tensor.matmul(psB[:, 3, s2], rowsd[:, s2], Ud[:, s2], start=True, stop=True)
                        last.then_inc(*pd.step("o"))

                    pe.wait_ge(*dd.at("st", NC - 1))
                    pe.wait_ge(*ad.at("o", NC - 1))
                    oT_rows(1)
                    norm_sums(1, None)
                    pe.wait_ge(*an.at("ln", 1))
                    for n in range(2):
                        if n:
                            pe.wait_ge(*db.at("rot", 0))
                        s4 = q4(RB[:, 2 * n:2 * n + 2, :])
                        for k in range(4):
                            last = nc.tensor.matmul(psB[:, k, 0:HALF], cc("rotp"), s4[:, k, :], start=True, stop=True)
                        last.then_inc(*pb.step("rot"))
                        merge(8 + n)
                    pe.wait_ge(*db.at("prep"))
                    nc.tensor.transpose(psB[0:48, 3, 0:P], svB[:, 0:3].rearrange("p n b i -> p (n b i)"), ident).then_inc(*ps_.step("rows"))
                    pe.wait_ge(*as_.at("rows", 2))
                    Mb = Mst[1]
                    for c in range(NC):
                        if c:
                            pe.wait_ge(*db.at("st", c - 1))
                            pe.wait_ge(*ab.at("o", c - 1))
                        for h in range(HEADS):
                            last = nc.tensor.matmul(psB[:, h % 2, (h // 2) * P:(h // 2 + 1) * P], RB[hp(h), 2 + h // 2, ch(c)], RB[hp(h), h // 2, ch(c)], start=True, stop=True)
                        last.then_inc(*pb.step("gram"))
                        for n in range(4):
                            last = nc.tensor.transpose(psB[:, 2, n * P:(n + 1) * P], RB[:, 2 + n, ch(c)], ident)
                        last.then_inc(*pb.step("tr"))
                        pe.wait_ge(*db.at("gr", c))
                        pe.wait_ge(*db.at("rows", c))
                        for h in range(HEADS):
                            out = psB[hp(h), h % 2, (h // 2) * P:(h // 2 + 1) * P]
                            nc.tensor.matmul(out, Mb[hp(h), h // 2, :], ws[hp(h), 2 + h // 2, ch(c)], start=True, stop=False)
                            nc.tensor.matmul(out, vrb[:, h * HD:(h + 1) * HD], h4(G1b)[:, h, :], start=False, stop=True)
                        for i in range(2):
                            s2 = slice(i * P, (i + 1) * P)
                            last = nc.tensor.matmul(psB[:, 3, s2], krb[:, s2], vrb[:, s2], start=True, stop=True)
                        last.then_inc(*pb.step("o"))
                        merge(10 + c)

                    pe.wait_ge(*db.at("st", NC - 1))
                    pe.wait_ge(*ab.at("o", NC - 1))
                    crow_rows([RC[:, j] for j in range(2)], 7, 3, pcc.step("crow"))
                    merge(14)
                    oT_rows(2)
                    norm_sums(2, None)
                    merge(15)
                    pe.wait_ge(*an.at("ln", 2))
                    pe.wait_ge(*ac.at("crow"))
                    pe.wait_ge(*dc.at("xc"))
                    for g in range(2):
                        if g:
                            pe.wait_ge(*ac.at("thr"))
                        for i in range(2):
                            for hf in range(2):
                                last = nc.tensor.matmul(psB[:, 2 * i + hf, 0:HALF], gw[:, 2 * g + i, :], ws[:, i, hf * HALF:(hf + 1) * HALF], start=True, stop=True)
                        last.then_inc(*pcc.step("gates"))
                        merge(16 + g)
                    for idx in range(18, 22):
                        merge(idx)
                    pe.wait_ge(*ac.at("thi"))
                    pe.wait_ge(*dc.at("h"))
                    for i in range(2):
                        last = nc.tensor.transpose(psB[0:9, 0, i * P:(i + 1) * P], RC[:, i, SEQ - 1:TT], ident)
                    last.then_inc(*pcc.step("hrow"))
                    for idx in range(22, 32):
                        merge(idx)

                    pe.wait_ge(*merged_at(31))
                    for e in range(KT):
                        s, arrived = ring_slot("out", e)
                        b = 2 * (e % 2)
                        pe.wait_ge(*arrived)
                        if e >= 2:
                            pe.wait_ge(*dm.at("x", e - 2))
                        for k in range(KT):
                            for hf in range(2):
                                last = nc.tensor.matmul(psA[:, b + hf, 0:HALF], ring[:, s, k, :], mg[k][:, hf * HALF:(hf + 1) * HALF],
                                                        start=(k == 0), stop=(k == KT - 1))
                        last.then_inc(*pm.step("out"))

                @block.scalar
                def _(act):
                    A = nc.scalar.activation
                    eps = cc("eps")
                    half = lambda ap: ap.rearrange("p (h c) -> p h c", h=2)

                    def evac(*idxs):
                        for idx in idxs:
                            _, name, j = PROJ[idx]
                            b = 2 * (idx % 2)
                            act.wait_ge(*pp.at("proj", idx))
                            if idx == P_C:
                                act.wait_ge(s_so, in_layer(0, 12, 4))
                            if name == "ba":
                                A(half(bg[0:4, :]), psA[0:4, b:b + 2, 0:HALF], ACT.Tanh, scale=0.5)
                                A(half(bg[32:36, :]), psA[32:36, b:b + 2, 0:HALF], ACT.Identity, bias=gp[32:36, 1:2]).then_inc(*ap.step("proj"))
                            else:
                                nc.scalar.copy(half(RAW[name][:, j, :]), psA[:, b:b + 2, 0:HALF]).then_inc(*ap.step("proj"))

                    def gates(*idxs):
                        for idx in idxs:
                            act.wait_ge(*pm.at("gl", idx))
                            if idx >= 2:
                                act.wait_ge(*merged_at(idx - 2))
                            A(half(tg[:, idx % 2, :]), psA[:, 0:2, 0:HALF], ACT.Tanh, scale=0.5).then_inc(*am.step("th"))

                    def decode_rows(n, b):
                        act.wait_ge(*ps_.at("rows", n))
                        if n:
                            act.wait_ge(s_scr, in_layer(0, 15, 5 * n - 4))
                        rows = (96, 80, 48)[n]
                        nc.scalar.copy(rowA[0:rows, :], psB[0:rows, b, 0:P]).then_inc(*as_.step("rows"))

                    def norm(n, src, e):
                        act.wait_ge(*(dn.at("cen") if n == 0 else ds.at("oT", n)))
                        A(ws[:, 0:2, :], src, ACT.Square).then_inc(*an.step("sq"))
                        act.wait_ge(*pn.at("var", n))
                        A(q4(ws[:, 0:2, :]), psB[:, :, 0:HALF], ACT.Ln, bias=e, scale=1.0 / HD).then_inc(*an.step("ln"))
                        act.wait_ge(*an.at("ln", n))
                        A(ws[:, 0:2, :], ws[:, 0:2, :], ACT.Exp, scale=-0.5).then_inc(*an.step("rn"))

                    def gate(n, z):
                        A(ws[:, 2:4, :], z, ACT.Tanh, scale=0.5).then_inc(*an.step("tz"))

                    def tree_start(T, V, td, tp, ta, c):
                        if c:
                            act.wait_ge(*tp.at("u", c - 1))
                        nc.scalar.copy(h4(T), bc(ident, 1, HEADS))
                        nc.scalar.copy(h4(V), bc(ident, 1, HEADS)).then_inc(*ta.step("ti"))

                    for d in range(KT):
                        A(ws[:, 10 + d, :], xT[:, d, :], ACT.Square).then_inc(*act_f.step("sq"))
                    act.dma_start(prow[0:PARAM_N, :], a["param_rows"][layer]).then_inc(s_par, 16)
                    act.dma_start(srow[:, :], a["state_rows"][layer]).then_inc(s_st, 16)
                    act.dma_start(w2[0:64, :], a["rwkv_w2"][layer]).then_inc(s_w2, 16)
                    act.dma_start(w2[64:128, :], a["rwkv_a2"][layer]).then_inc(s_w2, 16)
                    for g in range(2):
                        for hf in range(2):
                            act.dma_start(gw[hf * HD:(hf + 1) * HD, 2 * g:2 * g + 2, hf * HD:(hf + 1) * HD],
                                          a["lru_gate_w"][layer, g].rearrange("(i f) d e -> f d i e", f=2)[hf]).then_inc(s_w2, 16)
                    act.dma_start(gp[32:36, 0:1], a["gdn_A_log"][layer].unsqueeze(1)).then_inc(s_w2, 16)
                    act.dma_start(gp[32:36, 1:2], a["gdn_dt_bias"][layer].unsqueeze(1)).then_inc(s_w2, 16)
                    act.wait_ge(*pe_f.at("ss"))
                    A(half(rs[:]), psB[:, 2:4, 0:HALF], ACT.Ln, bias=eps, scale=1.0 / D_MODEL).then_inc(*act_f.step("lnx"))
                    act.wait_ge(*act_f.at("lnx"))
                    A(rs[:], rs[:], ACT.Exp, scale=-0.5).then_inc(*act_f.step("rs"))
                    for g in range(4):
                        act.wait_ge(*pe_f.at("ada", 4 * g + 3))
                        nc.scalar.copy(ws[0:9, 4 + g, 0:512], psA[0:9, g, :]).then_inc(*act_f.step("modrow"))
                    act.wait_ge(*dve_f.at("der"))
                    A(der[:, 20:22], par("lam", 0, 2), ACT.Abs).then_inc(*act_f.step("lam_abs"))
                    act.wait_ge(*act_f.at("lam_abs"))
                    A(der[:, 22:24], der[:, 20:22], ACT.Exp, scale=-1.0).then_inc(*act_f.step("lam_z"))
                    act.wait_ge(s_w2, 16 * N_W2)
                    A(gp[32:36, 2:3], gp[32:36, 0:1], ACT.Exp).then_inc(*act_f.step("expA"))
                    evac(*range(9))

                    pa, aa, da = TR["pe_a"], TR["act_a"], TR["dve_a"]
                    act.wait_ge(*pe_f.at("ada", 23))
                    nc.scalar.copy(mg5[0:9, 0:2, 0:512], psA[0:9, 2:4, :]).then_inc(*act_f.step("modrow"))
                    act.wait_ge(*pa.at("crow"))
                    nc.scalar.copy(crow[:, 0:512], psB[0:11, 0, :])
                    nc.scalar.copy(crow[:, 512:7 * P], psB[0:11, 1, 0:3 * P]).then_inc(*aa.step("crow"))
                    evac(9)
                    act.wait_ge(*da.at("pm"))
                    A(RA[0:64, 6, :], RA[0:64, 6, :], ACT.Tanh).then_inc(*aa.step("twd"))
                    for g, (nm, hb, t) in enumerate((("thw", 0, 0), ("tha", 2, 8))):
                        act.wait_ge(*pa.at("lora", g))
                        for i in range(2):
                            last = A(half(ws[:, t + i, :]), psB[:, 2 * i:2 * i + 2, 0:HALF], ACT.Tanh, bias=der[:, hb + i:hb + i + 1], scale=0.5)
                        last.then_inc(*aa.step(nm))
                        evac(10 + g)
                    act.wait_ge(*da.at("kk"))
                    A(ws[:, 10:12, :], ws[:, 6:8, :], ACT.Square).then_inc(*aa.step("kk2"))
                    evac(12)
                    act.wait_ge(*aa.at("tha"))
                    for i in range(2):
                        last = A(ws[:, 12 + i, :], ws[:, 8 + i, :], ACT.Identity, bias=der[:, 6 + i:7 + i], scale=der[:, 4 + i:5 + i])
                    last.then_inc(*aa.step("kf"))
                    act.wait_ge(*pa.at("kks"))
                    A(q4(ws[:, 10:12, :]), psB[:, :, 0:HALF], ACT.Ln, bias=eps).then_inc(*aa.step("lnk"))
                    act.wait_ge(*aa.at("lnk"))
                    A(ws[:, 10:12, :], ws[:, 10:12, :], ACT.Exp, scale=-0.5).then_inc(*aa.step("rn"))
                    evac(13)
                    act.wait_ge(*da.at("lex"))
                    A(ws[:, 4:6, :], ws[:, 2:4, :], ACT.Exp, scale=W_DECAY)
                    A(pc[:, 0], mid[:], ACT.Exp, scale=W_DECAY)
                    A(ws[:, 0:2, 0:SEQ], ws[:, 0:2, 0:SEQ], ACT.Exp, scale=W_DECAY).then_inc(*aa.step("decay"))
                    act.wait_ge(*aa.at("decay"))
                    A(ws[:, 2:4, 0:SEQ], ws[:, 2:4, 0:SEQ], ACT.Exp, scale=-W_DECAY).then_inc(*aa.step("exps"))
                    evac(14, 15, 16, 17)
                    decode_rows(0, 0)
                    for c in range(NC):
                        tree_start(Ta, Va, da, pa, aa, c)
                        act.wait_ge(*pa.at("tr", c))
                        nc.scalar.copy(rowsa[:, 0:512], psB[:, 0, :])
                        nc.scalar.copy(rowsa[:, 512:768], psB[:, 1, 0:256]).then_inc(*aa.step("rows"))
                        act_tree(act, pa, aa, Ya, c)
                        act.wait_ge(*pa.at("x1", c))
                        nc.scalar.copy(X1a.rearrange("p (i g v) -> p i g v", i=2, g=2), psB[:, 0:2, 0:P].rearrange("p g (i v) -> p i g v", i=2)).then_inc(*aa.step("x1"))
                        act.wait_ge(*pa.at("o", c))
                        for g in range(2):
                            pr = slice(g * HD, (g + 1) * HD)
                            last = nc.scalar.copy(RA[pr, 2:4, ch(c)], psB[pr, g, 0:256].rearrange("p (i t) -> p i t", i=2))
                        last.then_inc(*aa.step("o"))
                        if c < 3:
                            evac(P_B + 2 * c, P_B + 2 * c + 1)
                    act.wait_ge(*pa.at("mt"))
                    nc.scalar.copy(mrow[:], psB[0:HD, 0, 0:256].rearrange("p (i t) -> p i t", i=2)).then_inc(*aa.step("mrow"))

                    norm(0, RA[:, 2:4, :], cc("epsgn"))
                    evac(P_C - 2)
                    gate(0, RA[:, 7:9, :])
                    evac(P_C - 1)

                    pd, ad, dd = TR["pe_d"], TR["act_d"], TR["dve_d"]
                    act.wait_ge(*dn.at("gated", 0))
                    act.wait_ge(*pd.at("crow"))
                    nc.scalar.copy(crow[:, 9 * P:13 * P], psB[0:11, 0, :])
                    nc.scalar.copy(crow[:, 13 * P:15 * P], psB[0:11, 1, 0:2 * P]).then_inc(*ad.step("crow"))
                    for t in range(6):
                        last = A(ws[:, t, 0:SEQ], RD[:, t, 0:SEQ], ACT.Identity, scale=par("gdn_w", 18 + t))
                    last.then_inc(*ad.step("cv0"))
                    A(ws[32:36, 10, :], bg[32:36, :], ACT.Abs).then_inc(*ad.step("gabs"))
                    act.wait_ge(*ad.at("gabs"))
                    A(ws[32:36, 11, :], ws[32:36, 10, :], ACT.Exp, scale=-1.0).then_inc(*ad.step("gz"))
                    gates(0, 1, 2)
                    act.wait_ge(*dd.at("cv"))
                    A(RD[:, 0:6, :], ws[:, 0:6, :], ACT.Tanh, scale=0.5).then_inc(*ad.step("ths"))
                    gates(3)
                    act.wait_ge(*dd.at("silu2"))
                    A(RD[:, 0:4, :], ws[:, 0:4, :], ACT.Square).then_inc(*ad.step("sq"))
                    act.wait_ge(*pd.at("qs"))
                    A(q4(RD[:, 0:2, :]), psB[:, :, 0:HALF], ACT.Ln, bias=eps, scale=0.25).then_inc(*ad.step("lnq"))
                    gates(4)
                    act.wait_ge(*pd.at("ks"))
                    A(q4(RD[:, 2:4, :]), psB[:, :, 0:HALF], ACT.Ln, bias=eps, scale=0.25).then_inc(*ad.step("lnk"))
                    act.wait_ge(*ad.at("lnk"))
                    A(RD[:, 0:4, :], RD[:, 0:4, :], ACT.Exp, scale=-0.5).then_inc(*ad.step("rn"))
                    gates(5, 6)
                    act.wait_ge(*pd.at("bcast", 1))
                    A(ws[:, 6:8, 0:SEQ], psB[:, 0:2, :], ACT.Exp)
                    A(ws[:, 6:8, SEQ:TT], psB[:, 2, 0:16].rearrange("p (i b) -> p i b", i=2), ACT.Exp).then_inc(*ad.step("egc"))
                    gates(7)
                    decode_rows(1, 3)
                    for c in range(NC):
                        tree_start(Td, Vd, dd, pd, ad, c)
                        act.wait_ge(*pd.at("gb", c))
                        nc.scalar.copy(colbg[:], psB[:, 1, 0:36]).then_inc(*ad.step("col"))
                        act.wait_ge(*dd.at("dm", c))
                        A(Dd, Dd, ACT.Exp)
                        A(kdl[:], kdl[:], ACT.Exp).then_inc(*ad.step("dexp"))
                        act_tree(act, pd, ad, Yd, c)
                        act.wait_ge(*pd.at("u", c))
                        nc.scalar.copy(Ud, psB[:, 2, 0:256]).then_inc(*ad.step("u"))
                        act.wait_ge(*pd.at("o", c))
                        for g in range(2):
                            pr = slice(g * HD, (g + 1) * HD)
                            last = nc.scalar.copy(RD[pr, 4:6, ch(c)], psB[pr, g, 0:256].rearrange("p (i t) -> p i t", i=2))
                        last.then_inc(*ad.step("o"))
                        evac(P_C + c)
                    norm(1, RD[:, 4:6, :], eps)
                    gate(1, RD[:, 6:8, :])

                    pb, ab, db = TR["pe_b"], TR["act_b"], TR["dve_b"]
                    gates(8, 9)
                    decode_rows(2, 3)
                    for c in range(NC):
                        act.wait_ge(*pb.at("o", c))
                        for g in range(2):
                            pr = slice(g * HD, (g + 1) * HD)
                            last = nc.scalar.copy(RB[pr, 4:6, ch(c)], psB[pr, g, 0:256].rearrange("p (i t) -> p i t", i=2))
                        last.then_inc(*ab.step("o"))
                        gates(10 + c)

                    pcc, ac, dc = TR["pe_c"], TR["act_c"], TR["dve_c"]
                    act.wait_ge(*pcc.at("crow"))
                    nc.scalar.copy(crow[:, 7 * P:9 * P], psB[0:11, 3, 0:2 * P]).then_inc(*ac.step("crow"))
                    gates(14)
                    norm(2, RB[:, 4:6, :], eps)
                    gate(2, RB[:, 6:8, :])
                    gates(15)
                    act.wait_ge(*dn.at("gated", 2))
                    for i in range(2):
                        last = A(ws[:, i, 0:SEQ], RC[:, i, 0:SEQ], ACT.Identity, bias=par("lru_b", i), scale=par("lru_w", 6 + i))
                    last.then_inc(*ac.step("cv0"))
                    for g, (nm, t) in enumerate((("thr", 2), ("thi", 4))):
                        act.wait_ge(*pcc.at("gates", g))
                        for i in range(2):
                            last = A(half(ws[:, t + i, :]), psB[:, 2 * i:2 * i + 2, 0:HALF], ACT.Tanh, bias=der[:, 8 + 2 * g + i:9 + 2 * g + i], scale=0.5)
                        last.then_inc(*ac.step(nm))
                        gates(16 + g)
                    act.wait_ge(*ac.at("thr"))
                    for i in range(2):
                        A(ws[:, 6 + i, :], ws[:, 2 + i, :], ACT.Exp, bias=der[:, 14 + i:15 + i], scale=der[:, 14 + i:15 + i])
                        last = A(ws[:, 8 + i, :], ws[:, 2 + i, :], ACT.Tanh, bias=der[:, 12 + i:13 + i], scale=der[:, 12 + i:13 + i])
                    last.then_inc(*ac.step("au"))
                    gates(18)
                    act.wait_ge(*dc.at("u2"))
                    A(ws[:, 10:12, :], ws[:, 10:12, :], ACT.Ln)
                    A(ws[:, 12:14, :], ws[:, 8:10, :], ACT.Ln, bias=cc("ones")[:, 0:1]).then_inc(*ac.step("lnu"))
                    gates(19)
                    act.wait_ge(*dc.at("lndiff"))
                    A(ws[:, 10:12, :], ws[:, 10:12, :], ACT.Exp, scale=0.5).then_inc(*ac.step("root"))
                    gates(20)
                    act.wait_ge(*dc.at("h"))
                    gate(3, RC[:, 2:4, :])
                    gates(21)
                    act.wait_ge(*pcc.at("hrow"))
                    nc.scalar.copy(hrow[:], psB[0:9, 0, 0:W]).then_inc(*ac.step("hrow"))
                    gates(*range(22, 32))

                @block.vector
                def _(dve):
                    v = nc.vector
                    T_, S_, STT = v.tensor_tensor, v.tensor_scalar, v.scalar_tensor_tensor

                    def did(track_, name, ins, i=0):
                        ins.then_inc(*track_.step(name))
                        dve.wait_ge(*track_.at(name, i))

                    half = lambda ap: ap.rearrange("p (h c) -> p h c", h=2)
                    for m in Mst:
                        last = v.memset(m[:], 0.0)
                    last.then_inc(*dve_f.step("zero"))
                    dve.wait_ge(*pe_f.at("par"))
                    did(dve_f, "parT", v.tensor_copy(parT[:, 0:PARAM_N], psB[:, 0, 0:PARAM_N]))
                    S_(der[:, 0:2], par("w0", 0, 2), 0.5, None, mult)
                    S_(der[:, 2:4], par("a0", 0, 2), 0.5, None, mult)
                    S_(der[:, 4:6], par("k_a", 0, 2), 0.5, None, mult)
                    S_(der[:, 6:8], par("k_a", 0, 2), -0.5, 1.0, mult, add)
                    did(dve_f, "der", S_(der[:, 8:12], par("gate_b", 0, 4), 0.5, None, mult))
                    dve.wait_ge(*pe_f.at("st"))
                    did(dve_f, "stT", v.tensor_copy(stT[:], psB[:, 1, 0:448].rearrange("p (j r) -> p j r", j=7)))

                    def log1p(tr, pre, z, t, t2, acc):
                        did(tr, pre + "1", S_(t, z, 2.0, None, add))
                        did(tr, pre + "2", v.reciprocal(t2, t))
                        did(tr, pre + "3", T_(t, z, t2, mult))
                        did(tr, pre + "4", T_(t2, t, t, mult))
                        did(tr, pre + "5", S_(acc, t2, 2.0 / 17, 2.0 / 15, mult, add))
                        for n in (13, 11, 9, 7, 5, 3, 1):
                            did(tr, pre + f"m{n}", T_(acc, acc, t2, mult))
                            did(tr, pre + f"a{n}", S_(acc, acc, 2.0 / n, None, add))
                        did(tr, pre + "6", T_(acc, acc, t, mult))

                    dve.wait_ge(*act_f.at("rs"))
                    for d in range(KT):
                        last = T_(hT[:, d, :], xT[:, d, :], rs[:], mult)
                    did(dve_f, "xn", last)
                    dve.wait_ge(*pe_f.at("mod", 0))
                    did(dve_f, "modT", T_(modT[:, 0:16, :], psB[:, 1, 0:144].rearrange("p (r s) -> p r s", r=16), bc(par("ada_b", 0, 16), 2, 9), add))
                    did(dve_f, "G", STT(G[:], modT[:, 8:16, :], 1.0, bc(par("norm_g", 0, 8), 2, 9), add, mult))
                    did(dve_f, "hg", T_(hT[:, :, SEQ:TT], hT[:, :, SEQ:TT], G[:, :, 0:8], mult))
                    did(dve_f, "hd", T_(hT[:, :, SEQ:TT], hT[:, :, SEQ:TT], modT[:, 0:8, 0:8], add))
                    for d in range(KT):
                        S_(hT[:, d, 0:SEQ], hT[:, d, 0:SEQ], G[:, d, 8:9], modT[:, d, 8:9], mult, add).then_inc(*dve_f.step("hs"))
                    dve.wait_ge(*act_f.at("lam_z"))
                    log1p(dve_f, "lam", der[:, 22:24], der[:, 24:26], der[:, 26:28], der[:, 28:30])
                    did(dve_f, "lam_y", S_(der[:, 30:32], par("lam", 0, 2), -1.0, 0.0, mult, ALU.max))
                    did(dve_f, "lam_sp", T_(der[:, 30:32], der[:, 30:32], der[:, 28:30], add))
                    S_(der[:, 12:14], der[:, 30:32], LRU_C / 2, None, mult)
                    S_(der[:, 14:16], der[:, 30:32], -LRU_C / 2, None, mult)
                    pa, aa, da = TR["pe_a"], TR["act_a"], TR["dve_a"]
                    outs3 = (RA[:, 2:4, :], RD[:, 4:6, :], RB[:, 4:6, :])
                    row = lambda x: bc(x, 1, 16)
                    col = lambda x: bc(x, 2, 16)
                    vk = lambda x: x.rearrange("p (v k) -> p v k", v=16)
                    kv = lambda x: x.rearrange("p (k v) -> p k v", v=16)
                    kvT = lambda x: x.rearrange("p (k v) -> p v k", v=16)

                    def merged(*idxs):
                        for idx in idxs:
                            j = MERGE[idx][1]
                            dve.wait_ge(*pm.at("gate", idx))
                            dve.wait_ge(*am.at("th", idx))
                            th, up = half(tg[:, idx % 2, :]), psA[:, 2:4, 0:HALF]
                            if idx < KT:
                                STT(half(mg[j]), th, 1.0, up, add, mult).then_inc(*dm.step("mul"))
                            else:
                                did(dm, "mul", STT(th, th, 1.0, up, add, mult), idx)
                                T_(mg[j], mg[j], tg[:, idx % 2, :], add).then_inc(*dm.step("mg"))

                    def decode_in(n):
                        dve.wait_ge(s_vec, in_layer(0, 24, 8 * n + 8))
                        dve.wait_ge(s_ss, in_layer(0, 12, 4 * n + 4))

                    def decode_out(n):
                        dve.wait_ge(*ps_.at("oT", n))
                        did(ds, "oT", v.tensor_copy(outs3[n][:, :, SEQ:TT], psB[:, 1, 0:2 * NB].rearrange("p (i b) -> p i b", i=2)), n)

                    def gated(n, out, z):
                        dve.wait_ge(*an.at("tz", n))
                        did(dn, "siluz", STT(ws[:, 2:4, :], ws[:, 2:4, :], 1.0, z, add, mult), n)
                        did(dn, "gated", STT(out, out, 0.5, ws[:, 2:4, :], mult, mult), n)

                    dve.wait_ge(*ap.at("proj", 8))
                    T_(ws[:, 0:7, 1:SEQ], RA[:, 0:7, 0:SEQ - 1], RA[:, 0:7, 1:SEQ], sub)
                    S_(ws[:, 0:7, 0:1], RA[:, 0:7, 0:1], -1.0, None, mult)
                    did(da, "diff", T_(ws[:, 0:7, SEQ:TT], stT[:, :, 0:8], RA[:, 0:7, SEQ:TT], sub))
                    dve.wait_ge(*pa.at("crow"))
                    for j in range(7):
                        last = STT(RA[:, j, :], ws[:, j, :], par("mu", j), RA[:, j, :], mult, add)
                    did(da, "pm", last)
                    dve.wait_ge(*pe_f.at("mod", 1))
                    did(dve_f, "modT", T_(modT[:, 16:24, :], psB[:, 2, 0:72].rearrange("p (r s) -> p r s", r=8), bc(par("ada_b", 16, 8), 2, 9), add), 1)
                    did(dve_f, "gate", S_(modT[:, 16:24, :], modT[:, 16:24, :], 0.5, None, mult))
                    for i in range(2):
                        last = S_(ws[:, 6 + i, :], RA[:, 2 + i, :], par("k_k", i), None, mult)
                    did(da, "kk", last)
                    dve.wait_ge(*aa.at("thw"))
                    did(da, "lw1", S_(ws[:, 0:2, :], ws[:, 0:2, :], 1.0, None, add))
                    for i in range(2):
                        last = v.tensor_tensor_scan(ws[:, 2 + i, :], cc("reset"), ws[:, i, :], 0.0, mult, add)
                    did(da, "scan", last)
                    L4 = ws[:, 2:4, 0:SEQ].rearrange("p i (c t) -> p i c t", c=NC)
                    did(da, "mid", v.tensor_copy(mid[:], L4[:, :, :, C // 2 - 1]))
                    did(da, "lrel", T_(L4, L4, bc(mid[:], 3, C), sub))
                    did(da, "lex", T_(ws[:, 0:2, 0:SEQ], ws[:, 2:4, 0:SEQ], ws[:, 0:2, 0:SEQ], sub))
                    dve.wait_ge(*aa.at("kf"))
                    S_(ws[:, 8:10, :], ws[:, 8:10, :], 0.5, 0.5, mult, add)
                    T_(RA[:, 2:4, :], RA[:, 2:4, :], ws[:, 12:14, :], mult)
                    dve.wait_ge(*aa.at("rn"))
                    did(da, "kkn", T_(ws[:, 6:8, :], ws[:, 6:8, :], ws[:, 10:12, :], mult))
                    did(da, "bv", T_(ws[:, 8:10, :], ws[:, 8:10, :], ws[:, 6:8, :], mult))
                    dve.wait_ge(*aa.at("exps"))
                    svt = lambda sv, n: sv[:, n].rearrange("p b i -> p i b")
                    for n, src in ((0, RA[:, 0:2]), (1, ws[:, 4:6]), (2, RA[:, 2:4]), (3, RA[:, 4:6]), (5, ws[:, 8:10])):
                        v.tensor_copy(svt(svA, n), src[:, :, SEQ:TT])
                    S_(svt(svA, 4), ws[:, 6:8, SEQ:TT], -1.0, None, mult)
                    s4 = lambda t: ws[:, t, 0:SEQ].rearrange("p (c t) -> p c t", c=NC)
                    for i in range(2):
                        STT(ARa[:, i, :, 0, :], s4(6 + i), -1.0, s4(i), mult, mult)
                        T_(ARa[:, i, :, 1, :], RA[:, i, 0:SEQ].rearrange("p (c t) -> p c t", c=NC), s4(4 + i), mult)
                    T_(ws[:, 14:16, 0:SEQ], ws[:, 8:10, 0:SEQ], ws[:, 2:4, 0:SEQ], mult)
                    T_(ws[:, 16:18, 0:SEQ], RA[:, 2:4, 0:SEQ], ws[:, 2:4, 0:SEQ], mult)
                    E4 = ws[:, 4:6, 0:SEQ].rearrange("p i (c t) -> p i c t", c=NC)
                    did(da, "pend", v.tensor_copy(pc[:, 1], E4[:, :, :, C - 1]))
                    T_(pc[:, 2, :, 0:NC - 1], pc[:, 1, :, 0:NC - 1], pc[:, 0, :, 1:NC], mult)
                    v.tensor_copy(pc[:, 2, :, NC - 1:NC], pc[:, 1, :, NC - 1:NC])
                    for i in range(2):
                        last = STT(ws[:, 6 + i, :], RA[:, i, :], par("r_k", i), RA[:, 2 + i, :], mult, mult)
                    did(da, "bt", last)
                    dve.wait_ge(*pa.at("bsum"))
                    did(da, "prep", T_(q4(RA[:, 0:2, :]), psB[:, :, 0:HALF], q4(RA[:, 4:6, :]), mult))
                    Ma = Mst[0]
                    for c in range(NC):
                        dve.wait_ge(*pa.at("gram", c))
                        for g in range(2):
                            T_(GRa4[:, 2 * g:2 * g + 2, :], psB[:, 2 * g:2 * g + 2, :], bc(cc("rmask"), 1, 2), mult).then_inc(*da.step("gr"))
                        dve.wait_ge(*da.at("gr", 2 * c + 1))
                        dve.wait_ge(*aa.at("ti", c))
                        dve_tree(dve, pa, da, AtA, Ta, Va, c)
                        dve.wait_ge(*pa.at("u", c))
                        v.tensor_copy(Ua, psB[:, 2, 0:256]).then_inc(*da.step("u"))
                        dve.wait_ge(*pa.at("o", c))
                        for g in range(2):
                            pr = slice(g * HD, (g + 1) * HD)
                            last = T_(Ma[pr], psB[pr, 3, 0:256].rearrange("p (i x) -> p i x", i=2)[:, :, g * HD:(g + 1) * HD], Ma[pr], add)
                        did(da, "sum", last, c)
                        did(da, "st", T_(Ma[:], Ma[:], bc(pc[:, 2, :, c], 2, HD), mult), c)
                        if c == 1:
                            decode_in(0)
                            S0, tmp = wfC[:, 0:1024], wfC[:, 1024:2048]
                            r_, w_, k_, a_, b_ = (vecA[:, n, :] for n in (0, 1, 2, 4, 5))
                            did(ds, "1", T_(vk(tmp), vk(S0), row(a_), mult))
                            v.tensor_reduce(sa[:, 0, :], vk(tmp), AX.X, add)
                            did(ds, "2", T_(vk(S0), vk(S0), row(w_), mult))
                            did(ds, "3", T_(vk(tmp), bc(sa[:, 0, :], 2, HD), row(b_), mult))
                            did(ds, "4", T_(S0, S0, tmp, add))
                            did(ds, "5", T_(vk(tmp), bc(vv[:, 0, :], 2, HD), row(k_), mult))
                            did(ds, "6", T_(S0, S0, tmp, add))
                            did(ds, "7", T_(vk(tmp), vk(S0), row(r_), mult))
                            v.tensor_reduce(so[:, 0, :], vk(tmp), AX.X, add).then_inc(*ds.step("so"))

                    pd, ad, dd = TR["pe_d"], TR["act_d"], TR["dve_d"]
                    decode_out(0)
                    dve.wait_ge(*pn.at("mean"))
                    did(dn, "cen", STT(q4(outs3[0]), psB[:, :, 0:HALF], -1.0 / HD, q4(outs3[0]), mult, add))
                    dve.wait_ge(*an.at("rn", 0))
                    did(dn, "normed", T_(outs3[0], outs3[0], ws[:, 0:2, :], mult), 0)
                    for i in range(2):
                        last = S_(outs3[0][:, i, :], outs3[0][:, i, :], par("ln_g", i), par("ln_b", i), mult, add)
                    did(dn, "gains", last)
                    did(dn, "bonus", T_(outs3[0], outs3[0], RA[:, 0:2, :], add))
                    gated(0, outs3[0], RA[:, 7:9, :])

                    def conv(tr, raw, n, wname, st0):
                        w0 = PARAM_ROWS[wname]
                        for tap in range(2, -1, -1):
                            sh = CONV - 1 - tap
                            for t in range(n):
                                last = STT(ws[:, t, sh:SEQ], raw[:, t, 0:SEQ - sh], par(wname, tap * n + t), ws[:, t, sh:SEQ], mult, add)
                            did(tr, "cvt", last, 2 - tap)
                        stc = stT[:, 0:n, st0:st0 + 24].rearrange("p i (b j) -> p i b j", j=3)
                        wt = parT[:, w0:w0 + 3 * n].rearrange("p (j i) -> p i j", i=n)
                        tmp = wv(14, n * 24).rearrange("p (i b j) -> p i b j", i=n, b=NB)
                        new = wv(15, n * NB).rearrange("p (i b) -> p i b", i=n)
                        did(tr, "cs1", T_(tmp, stc, bc(wt, 2, NB), mult))
                        v.tensor_reduce(ws[:, 0:n, SEQ:TT], tmp, AX.X, add)
                        did(tr, "cs2", T_(new, raw[:, 0:n, SEQ:TT], bc(parT[:, w0 + 3 * n:w0 + 4 * n], 2, NB), mult))
                        did(tr, "cs3", T_(ws[:, 0:n, SEQ:TT], ws[:, 0:n, SEQ:TT], new, add))

                    dve.wait_ge(*ad.at("cv0"))
                    conv(dd, RD, 6, "gdn_w", 40)
                    v.tensor_copy(colbg[:, 0:1], cc("eps")).then_inc(*dd.step("cv"))
                    merged(0)
                    dve.wait_ge(*ad.at("gz"))
                    g_ = lambda t: ws[32:36, t, :]
                    log1p(dd, "g", g_(11), g_(12), g_(13), g_(14))
                    merged(1, 2)
                    S_(gp[32:36, 3:4], gp[32:36, 2:3], -1.0, None, mult)
                    did(dd, "gmax", S_(g_(12), bg[32:36, :], 0.0, None, ALU.max))
                    did(dd, "gsp", T_(g_(12), g_(12), g_(14), add))
                    did(dd, "gneg", S_(g_(12), g_(12), gp[32:36, 3:4], None, mult))
                    S_(bg[0:4, :], bg[0:4, :], 0.5, 0.5, mult, add)
                    did(dd, "gc", v.tensor_tensor_scan(bg[32:36, :], cc("reset", 32, 36), g_(12), 0.0, mult, add))
                    dve.wait_ge(*ad.at("ths"))
                    did(dd, "silu2", STT(ws[:, 0:6, :], RD[:, 0:6, :], 1.0, ws[:, 0:6, :], add, mult))
                    merged(3, 4)
                    dve.wait_ge(*ad.at("rn"))
                    STT(ws[:, 0:2, :], ws[:, 0:2, :], 0.5 * HD ** -0.5, RD[:, 0:2, :], mult, mult)
                    did(dd, "qk", STT(ws[:, 2:4, :], ws[:, 2:4, :], 0.5, RD[:, 2:4, :], mult, mult))
                    merged(5)
                    dve.wait_ge(*pd.at("bcast", 0))
                    for i in range(2):
                        STT(ARd[:, i, :, 0, :], s4(2 + i), -1.0, psB[:, i, :].rearrange("p (c t) -> p c t", c=NC), mult, mult)
                        v.tensor_copy(ARd[:, i, :, 1, :], s4(i))
                    v.tensor_copy(svt(svB, 3), ws[:, 0:2, SEQ:TT])
                    v.tensor_copy(svt(svB, 4), ws[:, 2:4, SEQ:TT])
                    S_(svt(svB, 5), ws[:, 4:6, SEQ:TT], 0.5, None, mult)
                    did(dd, "ar", v.tensor_copy(svt(svB, 6), psB[:, 2, 0:16].rearrange("p (i b) -> p i b", i=2)))
                    merged(6)
                    dve.wait_ge(*ad.at("egc"))
                    v.tensor_copy(svt(svB, 7), ws[:, 6:8, SEQ:TT])
                    for i in range(2):
                        last = T_(RD[:, 4 + i, 0:SEQ].rearrange("p (c t) -> p c t", c=NC), ARd[:, i, :, 0, :], s4(6 + i), mult)
                    did(dd, "kbe", last)
                    did(dd, "prep", T_(ws[:, 6:8, 0:SEQ], ws[:, 0:2, 0:SEQ], ws[:, 6:8, 0:SEQ], mult))
                    merged(7)
                    Md = Mst[2]
                    D4 = h4(Dd)
                    for c in range(NC):
                        dve.wait_ge(*ad.at("col", c))
                        pg = h4(psB[:, 0, :])
                        for h in range(HEADS):
                            STT(D4[:, slot(h), :], pg[:, h, :], colbg[:, 32 + h:33 + h], cc("negm"), sub, add)
                        T_(kdl[:, 0:4], pg[:, :, C - 1], colbg[:, 32:36], sub)
                        v.tensor_copy(kdl[:, 4:8], pg[:, :, C - 1]).then_inc(*dd.step("dm"))
                        dve.wait_ge(*pd.at("gram", c))
                        dve.wait_ge(*ad.at("dexp", c))
                        for g in range(2):
                            T_(GRd[:, 512 * g:512 * g + 512].rearrange("p (h x t) -> p h x t", h=2, x=2),
                               psB[:, 2 + g, :].rearrange("p (h x t) -> p h x t", h=2, x=2), bc(D4[:, 2 * g:2 * g + 2, :], 2, 2), mult).then_inc(*dd.step("gr"))
                        dve.wait_ge(*dd.at("gr", 2 * c + 1))
                        dve.wait_ge(*ad.at("ti", c))
                        dve.wait_ge(*pd.at("tr", c))
                        T_(h4(rowsd[:, 0:256]), h4(psB[:, 0, 0:256]), bc(kdl[:, 0:4], 2, HD), mult)
                        STT(h4(rowsd[:, 256:512]), h4(psB[:, 0, 256:512]), 0.5, bc(colbg[:, 0:4], 2, HD), mult, mult).then_inc(*dd.step("rows"))
                        dve_tree(dve, pd, dd, AtD, Td, Vd, c)
                        dve.wait_ge(*pd.at("x1", c))
                        dve.wait_ge(*dd.at("rows", c))
                        T_(X1d.rearrange("p (i g v) -> p i g v", i=2, g=2), psB[:, 0:2, 0:P].rearrange("p g (i v) -> p i g v", i=2),
                           rowsd[:, 256:512].rearrange("p (i g v) -> p i g v", i=2, g=2), add).then_inc(*dd.step("x1"))
                        dve.wait_ge(*pd.at("o", c))
                        for h in range(HEADS):
                            i, g = h // 2, h % 2
                            last = STT(Md[hp(h), i, :], Md[hp(h), i, :], kdl[hp(h), 4 + h:5 + h], psB[hp(h), 3, i * P + g * HD:i * P + (g + 1) * HD], mult, add)
                        did(dd, "st", last, c)
                        if c == 1:
                            decode_in(1)
                            S0, tmp = wfA[:, 0:1024], wfA[:, 1024:2048]
                            did(ds, "11", S_(S0, S0, vecB[:, 7, 0:1], None, mult))
                            did(ds, "12", T_(kv(tmp), kv(S0), col(vecB[:, 4, :]), mult))
                            did(ds, "13", v.tensor_reduce(sa[:, 1, :], kvT(tmp), AX.X, add))
                            did(ds, "14", T_(sa[:, 1, :], vv[:, 1, :], sa[:, 1, :], sub))
                            did(ds, "15", S_(sa[:, 1, :], sa[:, 1, :], vecB[:, 6, 0:1], None, mult))
                            did(ds, "16", T_(kv(tmp), col(vecB[:, 4, :]), bc(sa[:, 1, :], 1, HD), mult))
                            did(ds, "17", T_(S0, S0, tmp, add))
                            did(ds, "18", T_(kv(tmp), kv(S0), col(vecB[:, 3, :]), mult))
                            v.tensor_reduce(so[:, 1, :], kvT(tmp), AX.X, add).then_inc(*ds.step("so"))
                    decode_out(1)
                    dve.wait_ge(*an.at("rn", 1))
                    did(dn, "normed", STT(outs3[1], outs3[1], par("gdn_g"), ws[:, 0:2, :], mult, mult), 1)
                    gated(1, outs3[1], RD[:, 6:8, :])

                    pb, ab, db = TR["pe_b"], TR["act_b"], TR["dve_b"]
                    rd = lambda n, hf_: RB[:, 2 * n:2 * n + 2, :]
                    for n, sc in ((0, 1.0), (1, HD ** -0.5)):
                        dve.wait_ge(*pb.at("rot", n))
                        for i in range(2):
                            STT(half(ws[:, i, :]), psB[:, 2 * i:2 * i + 2, 0:HALF], sc, half(cc("sin")), mult, mult)
                        for i in range(2):
                            last = STT(RB[:, 2 * n + i, :], RB[:, 2 * n + i, :], sc, cc("cos"), mult, mult)
                        did(db, "rot", last, n)
                        did(db, "rope", T_(RB[:, 2 * n:2 * n + 2, :], RB[:, 2 * n:2 * n + 2, :], ws[:, 0:2, :], add), n)
                        if n == 0:
                            merged(8)
                    for n in range(2):
                        v.tensor_copy(svt(svB, n), RB[:, 2 * n:2 * n + 2, SEQ:TT])
                    v.tensor_copy(svt(svB, 2), RB[:, 4:6, SEQ:TT]).then_inc(*db.step("sv"))
                    q_c = RB[:, 0:2, 0:SEQ].rearrange("p i (c t) -> p i c t", c=NC)
                    did(db, "prep", T_(ws[:, 2:4, 0:SEQ].rearrange("p i (c t) -> p i c t", c=NC), q_c,
                                       bc(cc("qdec").rearrange("p (i t) -> p i t", i=2), 2, NC), mult))
                    merged(9)
                    Mb = Mst[1]
                    for c in range(NC):
                        dve.wait_ge(*pb.at("gram", c))
                        T_(G1b.rearrange("p (i g t) -> p i g t", i=2, g=2), psB[:, 0:2, 0:256].rearrange("p g (i t) -> p i g t", i=2),
                           cc("rdec").rearrange("p (i g t) -> p i g t", i=2, g=2), mult).then_inc(*db.step("gr"))
                        dve.wait_ge(*pb.at("tr", c))
                        T_(h4(krb), h4(psB[:, 2, 0:256]), bc(cc("kdec"), 2, HD), mult)
                        v.tensor_copy(vrb, psB[:, 2, 256:512]).then_inc(*db.step("rows"))
                        dve.wait_ge(*pb.at("o", c))
                        for h in range(HEADS):
                            i, g = h // 2, h % 2
                            last = STT(Mb[hp(h), i, :], Mb[hp(h), i, :], cc("gc")[hp(h), i:i + 1], psB[hp(h), 3, i * P + g * HD:i * P + (g + 1) * HD], mult, add)
                        did(db, "st", last, c)
                        merged(10 + c)
                    decode_in(2)
                    S0, tmp = wfA[:, 0:1024], wfA[:, 1024:2048]
                    did(ds, "21", T_(kv(tmp), col(vecB[:, 1, :]), bc(vv[:, 2, :], 1, HD), mult))
                    did(ds, "22", STT(S0, S0, cc("gam"), tmp, mult, add))
                    did(ds, "23", T_(kv(tmp), kv(S0), col(vecB[:, 0, :]), mult))
                    v.tensor_reduce(so[:, 2, :], kvT(tmp), AX.X, add).then_inc(*ds.step("so"))
                    merged(14)
                    decode_out(2)
                    dve.wait_ge(*an.at("rn", 2))
                    did(dn, "normed", T_(outs3[2], outs3[2], ws[:, 0:2, :], mult), 2)
                    gated(2, outs3[2], RB[:, 6:8, :])
                    merged(15)

                    pcc, ac, dc = TR["pe_c"], TR["act_c"], TR["dve_c"]
                    dve.wait_ge(*ac.at("cv0"))
                    conv(dc, RC, 2, "lru_w", 16)
                    did(dc, "xc", T_(ws[:, 0:2, SEQ:TT], ws[:, 0:2, SEQ:TT], bc(par("lru_b", 0, 2), 2, NB), add))
                    merged(16, 17)
                    dve.wait_ge(*ac.at("au"))
                    S_(ws[:, 10:12, :], ws[:, 8:10, :], 2.0, 1e-18, mult, ALU.max).then_inc(*dc.step("u2"))
                    did(dc, "ix", STT(ws[:, 4:6, :], ws[:, 4:6, :], 1.0, ws[:, 0:2, :], add, mult))
                    merged(18)
                    dve.wait_ge(*ac.at("lnu"))
                    T_(ws[:, 10:12, :], ws[:, 10:12, :], ws[:, 12:14, :], sub).then_inc(*dc.step("lndiff"))
                    merged(19)
                    dve.wait_ge(*ac.at("root"))
                    T_(ws[:, 0:2, SEQ:TT], ws[:, 6:8, SEQ:TT], stT[:, 0:2, 8:16], mult)
                    did(dc, "b", STT(ws[:, 4:6, :], ws[:, 4:6, :], 0.5, ws[:, 10:12, :], mult, mult))
                    for i in range(2):
                        v.tensor_tensor_scan(RC[:, i, 0:SEQ], ws[:, 6 + i, 0:SEQ], ws[:, 4 + i, 0:SEQ], 0.0, mult, add)
                    did(dc, "h", T_(RC[:, 0:2, SEQ:TT], ws[:, 0:2, SEQ:TT], ws[:, 4:6, SEQ:TT], add))

                    merged(20)
                    dve.wait_ge(*an.at("tz", 3))
                    dve.wait_ge(*pcc.at("hrow"))
                    gated(3, RC[:, 0:2, :], RC[:, 2:4, :])
                    merged(*range(21, 32))
                    for e in range(KT):
                        b = 2 * (e % 2)
                        dve.wait_ge(*pm.at("out", e))
                        gate = modT[:, 16 + e, :]
                        n1 = SEQ - HALF
                        STT(xT[:, e, 0:HALF], psA[:, b, 0:HALF], gate[:, 8:9], xT[:, e, 0:HALF], mult, add)
                        STT(xT[:, e, HALF:SEQ], psA[:, b + 1, 0:n1], gate[:, 8:9], xT[:, e, HALF:SEQ], mult, add)
                        did(dm, "xs", T_(der[:, 32:40], psA[:, b + 1, n1:HALF], gate[:, 0:8], mult), e)
                        did(dm, "x", T_(xT[:, e, SEQ:TT], xT[:, e, SEQ:TT], der[:, 32:40], add), e)

            nc.all_engine_barrier()
            nc.gpsimd.sem_clear(range(s_const.num, TR["dve_m"].sem.num + 1))
            nc.all_engine_barrier()

        with nc.Block() as block:
            pe9, act9, dve9 = TR["pe9"], TR["act9"], TR["dve9"]

            @block.scalar
            def _(act):
                A = nc.scalar.activation
                for d in range(KT):
                    A(ws[:, 10 + d, :], xT[:, d, :], ACT.Square).then_inc(*act9.step("sq"))
                act.wait_ge(*pe9.at("ss"))
                A(rs[:].rearrange("p (h c) -> p h c", h=2), psB[:, 2:4, 0:HALF], ACT.Ln, bias=cc("eps"), scale=1.0 / D_MODEL).then_inc(*act9.step("ln"))
                act.wait_ge(*act9.at("ln"))
                A(rs[:], rs[:], ACT.Exp, scale=-0.5).then_inc(*act9.step("rs"))
                for t in range(4):
                    act.wait_ge(*pe9.at("y", t))
                    ps = psA if t % 2 == 0 else psB
                    nc.scalar.copy(ws[:, 2 * t:2 * t + 2, 0:512], ps[:, 0:2, :]).then_inc(*act9.step("y"))

            @block.tensor
            def _(pe):
                for d in range(KT):
                    pe.wait_ge(*act9.at("sq", d))
                    for hf in range(2):
                        last = nc.tensor.matmul(psB[:, 2 + hf, 0:HALF], ones, ws[:, 10 + d, hf * HALF:(hf + 1) * HALF], start=(d == 0), stop=(d == KT - 1))
                last.then_inc(*pe9.step("ss"))
                pe.wait_ge(*dve9.at("y"))
                for t in range(4):
                    ps = psA if t % 2 == 0 else psB
                    if t >= 2:
                        pe.wait_ge(*act9.at("y", t - 2))
                    for d in range(KT):
                        last = nc.tensor.transpose(ps[:, d // 4, (d % 4) * P:(d % 4 + 1) * P], hT[:, d, t * P:(t + 1) * P], ident)
                    last.then_inc(*pe9.step("y"))
                for d in range(KT):
                    last = nc.tensor.transpose(psA[0:8, 2 + d // 4, (d % 4) * P:(d % 4 + 1) * P], hT[:, d, SEQ:TT], ident)
                last.then_inc(*pe9.step("ys"))

            @block.vector
            def _(dve):
                dve.wait_ge(*act9.at("rs"))
                for d in range(KT):
                    last = nc.vector.scalar_tensor_tensor(hT[:, d, :], xT[:, d, :], par("final_g", d), rs[:], mult, mult)
                last.then_inc(*dve9.step("y"))
                dve.wait_ge(*pe9.at("ys"))
                nc.vector.tensor_copy(ws[0:8, 8:10, 0:512], psA[0:8, 2:4, :]).then_inc(*dve9.step("ys"))

            @block.sync
            def _(sp):
                for t in range(4):
                    sp.wait_ge(*act9.at("y", t))
                    sp.dma_start(o["y_prompt"][0, t * P:(t + 1) * P, :].rearrange("p (a c) -> p a c", a=2), ws[:, 2 * t:2 * t + 2, 0:512]).then_inc(s_y, 16)
                sp.wait_ge(*dve9.at("ys"))
                sp.dma_start(o["y_sample"][:, 0, :].rearrange("p (a c) -> p a c", a=2), ws[0:8, 8:10, 0:512]).then_inc(s_y, 16)
                sp.wait_ge(s_y, 16 * 5)
    return {n: t.made for n, t in tracks.items()}


STEPS = {
    'pe0': 'xs c x x x x x x x x'.split(),
    'act0': 'tanh_c x x x x x x x x'.split(),
    'dve0': 'tmask silu_c xs c'.split(),
    'pe_f': 'ss ada ada ada ada ada ada ada ada par st ada ada ada ada ada ada ada ada mod ada ada ada ada ada ada ada ada mod'.split(),
    'act_f': 'sq sq sq sq sq sq sq sq lnx rs modrow modrow modrow modrow lam_abs lam_z expA modrow'.split(),
    'dve_f': 'zero parT der stT xn modT G hg hd hs hs hs hs hs hs hs hs lam1 lam2 lam3 lam4 lam5 lamm13 lama13 lamm11 lama11 lamm9 lama9 lamm7 lama7 lamm5 lama5 lamm3 lama3 lamm1 lama1 lam6 lam_y lam_sp modT gate'.split(),
    'pe_a': 'crow lora lora kks bsum gram tr z z y y z z y y z z y y z z y y z z y y z z y y z z x1 u o gram tr z z y y z z y y z z y y z z y y z z y y z z y y z z x1 u o gram tr z z y y z z y y z z y y z z y y z z y y z z y y z z x1 u o gram tr z z y y z z y y z z y y z z y y z z y y z z y y z z x1 u o mt'.split(),
    'act_a': 'crow twd thw tha kk2 kf lnk rn decay exps ti rows y y y y y y y y y y y y x1 o ti rows y y y y y y y y y y y y x1 o ti rows y y y y y y y y y y y y x1 o ti rows y y y y y y y y y y y y x1 o mrow'.split(),
    'dve_a': 'diff pm kk lw1 scan mid lrel lex kkn bv pend bt prep gr gr t t t t t t t t t t t t t t u sum st gr gr t t t t t t t t t t t t t t u sum st gr gr t t t t t t t t t t t t t t u sum st gr gr t t t t t t t t t t t t t t u sum st'.split(),
    'pe_d': 'crow qs ks bcast bcast gb gram tr z z y y z z y y z z y y z z y y z z y y z z y y z z x1 u o gb gram tr z z y y z z y y z z y y z z y y z z y y z z y y z z x1 u o gb gram tr z z y y z z y y z z y y z z y y z z y y z z y y z z x1 u o gb gram tr z z y y z z y y z z y y z z y y z z y y z z y y z z x1 u o'.split(),
    'act_d': 'crow cv0 gabs gz ths sq lnq lnk rn egc ti col dexp y y y y y y y y y y y y u o ti col dexp y y y y y y y y y y y y u o ti col dexp y y y y y y y y y y y y u o ti col dexp y y y y y y y y y y y y u o'.split(),
    'dve_d': 'cvt cvt cvt cs1 cs2 cs3 cv g1 g2 g3 g4 g5 gm13 ga13 gm11 ga11 gm9 ga9 gm7 ga7 gm5 ga5 gm3 ga3 gm1 ga1 g6 gmax gsp gneg gc silu2 qk ar kbe prep dm gr gr rows t t t t t t t t t t t t t t x1 st dm gr gr rows t t t t t t t t t t t t t t x1 st dm gr gr rows t t t t t t t t t t t t t t x1 st dm gr gr rows t t t t t t t t t t t t t t x1 st'.split(),
    'pe_b': 'rot rot gram tr o gram tr o gram tr o gram tr o'.split(),
    'act_b': 'o o o o'.split(),
    'dve_b': 'rot rope rot rope sv prep gr rows st gr rows st gr rows st gr rows st'.split(),
    'pe_c': 'crow gates gates hrow'.split(),
    'act_c': 'crow cv0 thr thi au lnu root hrow'.split(),
    'dve_c': 'cvt cvt cvt cs1 cs2 cs3 xc u2 ix lndiff b h'.split(),
    'pe_s': 'rows oT rows oT rows oT'.split(),
    'act_s': 'rows rows rows'.split(),
    'dve_s': '1 2 3 4 5 6 7 so oT 11 12 13 14 15 16 17 18 so oT 21 22 23 so oT'.split(),
    'pe_p': 'proj proj proj proj proj proj proj proj proj proj proj proj proj proj proj proj proj proj proj proj proj proj proj proj proj proj proj proj proj proj'.split(),
    'act_p': 'proj proj proj proj proj proj proj proj proj proj proj proj proj proj proj proj proj proj proj proj proj proj proj proj proj proj proj proj proj proj'.split(),
    'pe_n': 'mean var var var'.split(),
    'act_n': 'sq ln rn tz sq ln rn tz sq ln rn tz tz'.split(),
    'dve_n': 'cen normed gains bonus siluz gated normed siluz gated normed siluz gated siluz gated'.split(),
    'pe_m': 'gl gate gl gate gl gate gl gate gl gate gl gate gl gate gl gate gl gate gl gate gl gate gl gate gl gate gl gate gl gate gl gate gl gate gl gate gl gate gl gate gl gate gl gate gl gate gl gate gl gate gl gate gl gate gl gate gl gate gl gate gl gate gl gate out out out out out out out out'.split(),
    'act_m': 'th th th th th th th th th th th th th th th th th th th th th th th th th th th th th th th th'.split(),
    'dve_m': 'mul mul mul mul mul mul mul mul mul mg mul mg mul mg mul mg mul mg mul mg mul mg mul mg mul mg mul mg mul mg mul mg mul mg mul mg mul mg mul mg mul mg mul mg mul mg mul mg mul mg mul mg mul mg mul mg xs x xs x xs x xs x xs x xs x xs x xs x'.split(),
    'pe9': 'ss y y y y ys'.split(),
    'act9': 'sq sq sq sq sq sq sq sq ln rs y y y y'.split(),
    'dve9': 'y ys'.split(),
}


_INS = ['x_prompt', 'x_sample', 'c_prompt', 'c_sample', 'state_rwkv_wkv', 'state_ret', 'state_lru_conv', 'state_gdn',
        'state_gdn_conv', 'ada_w', 'w_in', 'rwkv_w2', 'rwkv_a2', 'lru_gate_w', 'gdn_A_log', 'gdn_dt_bias', 'w_up', 'w_out']
_STATES = [('wkv', (HEADS, HD, HD)), ('shift', (A_SHIFT,)), ('ret', (HEADS, HD, HD)), ('lru_h', (W,)),
           ('lru_conv', (CONV - 1, W)), ('gdn', (HEADS, HD, HD)), ('gdn_conv', (CONV - 1, QKV))]
_OUTS = ([('y_prompt', (1, SEQ, D_MODEL)), ('y_sample', (NB, 1, D_MODEL))]
         + [('p_' + n, (DEPTH, 1) + s) for n, s in _STATES] + [('s_' + n, (DEPTH, NB) + s) for n, s in _STATES])
PAST_LEN = 4096


def constants():
    import numpy as np
    f = np.float32
    cst = np.zeros((P, CONST_N), f)

    def put(name, value, p0=0):
        lo, hi = CONST_COLS[name]
        value = np.asarray(value, f)
        cst[p0:p0 + value.shape[0], lo:hi] = value.reshape(value.shape[0], -1)

    p, t = np.arange(P), np.arange(C)
    put("ident", np.eye(P))
    put("bones", p[:, None] // HD == p[None, :] // HD)
    put("ones", np.ones((P, P)))
    rot = np.zeros((P, P), f)
    for m in range(P):
        rot[m + 32 if m % HD < 32 else m - 32, m] = -1.0 if m % HD < 32 else 1.0
    put("rotp", rot)
    strict, incl = t[None, :] > p[:, None], t[None, :] >= p[:, None]
    put("rmask", np.stack([strict, incl, strict, incl], 1))
    put("negm", np.where(incl, 0.0, -1e30))
    lg = np.log(1.0 - 2.0 ** (-5.0 - np.arange(HEADS, dtype=np.float64)))
    rel = t[None, None, :] - p[:, None, None]
    put("rdec", np.where(rel >= 0, np.exp(lg[None, :, None] * np.maximum(rel, 0)), 0.0))
    head = 2 * np.arange(2)[None, :] + (p[:, None] // HD)
    put("qdec", np.exp(lg[head][:, :, None] * (t + 1.0)))
    put("kdec", np.exp(lg[None, :] * (C - 1.0 - p[:, None])))
    put("gc", np.exp(lg[head] * C))
    put("gam", np.exp(lg[p % HEADS])[:, None])
    pos = np.concatenate([np.arange(SEQ), np.full(NB, PAST_LEN)]).astype(f)
    inv = (f(10000.0) ** (-np.arange(32, dtype=f) / f(32))).astype(f)
    ang = (pos[None, :] * inv[p % 32][:, None]).astype(f)
    put("cos", np.cos(ang.astype(np.float64)))
    put("sin", np.sin(ang.astype(np.float64)))
    reset = np.ones(TT)
    reset[0:SEQ:C] = 0.0
    reset[SEQ:] = 0.0
    put("reset", np.tile(reset, (P, 1)))
    for base in (0, 32):
        put("sel4", (np.arange(HEADS)[:, None, None] == np.arange(HEADS)[None, :, None]) * np.ones((1, 1, P)), base)
        put("sel2", np.arange(HEADS)[:, None, None] == head.T[None, :, :], base)
    put("eps", np.full((P, 1), 1e-6))
    put("epsgn", np.full((P, 1), 64e-5))
    masks = np.zeros((P, 14, P), f)
    for lv in range(7):
        b = 1 << lv
        m = (p[:, None] // (2 * b) == p[None, :] // (2 * b)) & (p[:, None] // b % 2 == 1) & (p[None, :] // b % 2 == 0)
        masks[:, lv], masks[:, 7 + lv] = m, m.T
    return cst, masks.reshape(P, -1)


def packed(inputs):
    import numpy as np
    rows = lambda name: np.reshape(inputs[name], (DEPTH, -1, P))
    order = ("ada_b", "norm_g", "rwkv_mu", "rwkv_w0", "rwkv_a0", "rwkv_k_k", "rwkv_k_a", "rwkv_r_k", "rwkv_ln_g", "rwkv_ln_b",
             "lru_conv_w", "lru_conv_b", "lru_gate_b", "lru_lambda", "gdn_conv_w")
    gdn_g = np.concatenate([inputs["gdn_norm_g"]] * 2, -1)[:, None, :]
    final_g = np.stack([np.reshape(inputs["final_g"], (KT, P))] * DEPTH)
    params = np.concatenate([rows(n) for n in order] + [gdn_g, final_g], 1)
    states = np.zeros((DEPTH, 64, A_SHIFT), params.dtype)
    states[:, 0:8] = inputs["state_rwkv_shift"]
    states[:, 8:16, 0:W] = inputs["state_lru_h"]
    states[:, 16:40, 0:W] = np.reshape(inputs["state_lru_conv"], (DEPTH, 24, W))
    states[:, 40:64, 0:QKV] = np.reshape(inputs["state_gdn_conv"], (DEPTH, 24, QKV))
    return np.ascontiguousarray(params), states


def kernel(**inputs):
    import numpy as _np
    import concourse.bacc as _bacc
    from concourse import mybir as _mybir
    from concourse.bass_utils import run_bass_kernel_spmd as _run

    nc = _bacc.Bacc("TRN2", target_bir_lowering=False, num_devices=1)
    arrays, ins, outs = {}, {}, {}
    given = {name: _np.ascontiguousarray(inputs[name]) for name in _INS}
    given["consts"], given["tree_masks"] = constants()
    given["param_rows"], given["state_rows"] = packed(inputs)
    for name, x in given.items():
        arrays[f"in_{name}"] = x
        ins[name] = nc.dram_tensor(f"in_{name}", x.shape, _mybir.dt.from_np(x.dtype), kind="ExternalInput").ap()
    for name, shape in _OUTS:
        outs[name] = nc.dram_tensor(f"out_{name}", shape, _mybir.dt.float32, kind="ExternalOutput").ap()
    build_program(nc, ins, outs, STEPS)
    r = _run(nc, [arrays], core_ids=[0])
    return tuple(r.results[0][f"out_{name}"] for name, _ in _OUTS)
```

```python
import concourse.bass as bass
from concourse import mybir
from contextlib import ExitStack

D_MODEL, SEQ, DEPTH, NB = 1024, 512, 2, 8
HEADS, HD = 4, 64
W = HEADS * HD
LORA = 64
CONV = 4
A_SHIFT = 3 * W + 2 * LORA
QKV = 3 * W
OFF_B = A_SHIFT + W
OFF_C = OFF_B + 4 * W
OFF_D = OFF_C + 2 * W
OFF_BA = OFF_D + QKV
OFF_DZ = OFF_BA + 2 * HEADS
OFF_G = OFF_DZ + W
IN_W = OFF_G + 4 * D_MODEL
P = 128
KT = D_MODEL // P
TT = SEQ + NB
HALF = TT // 2
C = 128
NC = SEQ // C
RING = 3
W_DECAY = -0.5 * 0.6065306597126334
LRU_C = 8.0

CONST_COLS = {}
_at = 0
for _name, _n in (("ident", 128), ("bones", 128), ("ones", 128), ("rotp", 128), ("rmask", 512), ("negm", 128),
                  ("rdec", 512), ("qdec", 256), ("cos", TT), ("sin", TT), ("reset", TT), ("sel4", 512),
                  ("sel2", 256), ("kdec", 4), ("gc", 2), ("gam", 1), ("eps", 1), ("epsgn", 1)):
    CONST_COLS[_name] = (_at, _at + _n)
    _at += _n
CONST_N = _at

PARAM_ROWS = {}
_at = 0
for _name, _n in (("ada_b", 24), ("norm_g", 8), ("mu", 7), ("w0", 2), ("a0", 2), ("k_k", 2), ("k_a", 2), ("r_k", 2),
                  ("ln_g", 2), ("ln_b", 2), ("lru_w", 8), ("lru_b", 2), ("gate_b", 4), ("lam", 2), ("gdn_w", 24),
                  ("gdn_g", 1), ("final_g", 8)):
    PARAM_ROWS[_name] = _at
    _at += _n
PARAM_N = _at


class Track:

    def __init__(self, sem, order):
        self.sem, self.order, self.n, self.where = sem, order, 0, {}
        for i, name in enumerate(order or []):
            self.where.setdefault(name, []).append(i + 1)
        self.made = []

    def step(self, name):
        self.n += 1
        self.made.append(name)
        if self.order is not None:
            assert self.order[self.n - 1] == name, (name, self.n, self.order[self.n - 1])
        return self.sem, 1

    def at(self, name, i=0):
        if self.order is None:
            return self.sem, 1
        return self.sem, self.where[name][i]


def build_program(nc, a, o, order):
    F32, F32R, U8 = mybir.dt.float32, mybir.dt.float32r, mybir.dt.uint8
    ALU, ACT, AX = mybir.AluOpType, mybir.ActivationFunctionType, mybir.AxisListType
    mult, add, sub = ALU.mult, ALU.add, ALU.subtract
    ctx = ExitStack()
    tracks = {}
    with ctx:
        def sb(name, shape, dt=F32):
            return ctx.enter_context(nc.sbuf_tensor(name, shape, dt))

        def sb_parts(name, parts_name, shape):
            with nc.sbuf_tensor(name, shape, F32) as whole:
                pass
            return whole, sb(parts_name, shape, F32R)

        def sem(name):
            return ctx.enter_context(nc.semaphore(name))

        def track(name):
            tracks[name] = Track(sem(name), order.get(name) if order else None)
            return tracks[name]

        cst = sb("cst", [P, CONST_N])
        tmask = sb("tmask", [P, 14, P], U8)
        xT, hhi = sb_parts("xT", "h_hi", [P, KT, TT])
        hT, hlo = sb_parts("hT", "h_lo", [P, KT, TT])
        RA, RAlo = sb_parts("RA", "ra_lo", [P, 9, TT])
        RB = sb("RB", [P, 8, TT])
        RC = sb("RC", [P, 4, TT])
        RD, mhi = sb_parts("RD", "merged_hi", [P, 8, TT])
        ws = sb("ws", [P, 18, TT])
        bg = sb("bg", [36, TT])
        ring, wlo = sb_parts("ring", "w_lo", [P, RING, KT, P])
        upw = sb("upw", [P, RING, 2, P])
        whi = sb("w_hi", [P, 2, KT, P], F32R)
        parT = sb("parT", [P, P])
        prow = sb("prow", [P, P])
        der = sb("der", [P, 40])
        stT = sb("stT", [P, 7, 64])
        srow = ws[0:64, 0:2, :].rearrange("p a b -> p (a b)")[:, 0:A_SHIFT]
        modT = sb("modT", [P, 24, 9])
        G = sb("G", [P, KT, 9])
        cT = sb("cT", [P, KT, 9])
        w2 = sb("w2", [P, W])
        gw = sb("gw", [P, 4, P])
        crow = sb("crow", [11, 8 * P])
        hrow = sb("hrow", [9, W])
        mg5, mg5lo = sb_parts("mg", "merged_lo", [P, 5, TT])
        mg = [RA[:, 0], RA[:, 1], RA[:, 8]] + [mg5[:, k] for k in range(5)]
        mlo = [RAlo[:, 0], RAlo[:, 1], RAlo[:, 8]] + [mg5lo[:, k] for k in range(5)]
        tg = sb("tg", [P, 2, TT])
        rs = tg[:, 0, :]
        crowA = mg5[0:11, 2:4, :].rearrange("p a b -> p (a b)")[:, 0:7 * P]
        svA = sb("svA", [P, 6, NB, 2])
        svB = sb("svB", [P, 8, NB, 2])
        rowA = prow
        vecA = vecB = sb("vec", [P, 8, HD])
        vv = sb("vv", [P, 3, 16])
        so = sb("so", [P, 3, 16])
        sa = sb("sa", [P, 2, 16])
        orow = sb("orow", [NB, W])
        Mst = [sb(f"M{n}", [P, 2, HD]) for n in range(3)]
        mid = sb("mid", [P, 2, NC])
        pc = sb("pc", [P, 4, 2, NC])
        gp = sb("gp", [36, 4])
        colbg = sb("colbg", [P, 36])
        kdl = sb("kdl", [P, 8])
        mrow = sb("mrow", [HD, 2, P])
        psA = ctx.enter_context(nc.psum_tensor("psA", [P, 4, 512], F32))
        psB = ctx.enter_context(nc.psum_tensor("psB", [P, 4, 512], F32))
        scrA = nc.dram_tensor("scr_a", (6, NB, W), F32).ap()
        scrB = nc.dram_tensor("scr_b", (8, NB, W), F32).ap()
        scrO = nc.dram_tensor("scr_o", (3, NB, W), F32).ap()
        scrX = nc.dram_tensor("scr_x", (P, KT, TT), F32).ap()

        def cc(name, p0=0, p1=P):
            lo, hi = CONST_COLS[name]
            return cst[p0:p1, lo:hi]

        def par(name, j=0, n=1):
            r = PARAM_ROWS[name] + j
            return parT[:, r:r + n]

        def bc(ap, axis, n):
            ap = ap.unsqueeze(axis)
            s = list(ap.shape)
            s[axis] = n
            return ap.broadcast_to(s)

        ident, bones, ones = cc("ident"), cc("bones"), cc("ones")
        wf = ws[:, :, :].rearrange("p a b -> p (a b)")
        wfC = RC[:, :, :].rearrange("p a b -> p (a b)")
        wfA = RA[:, 4:8, :].rearrange("p a b -> p (a b)")

        def wv(tile, n):
            return wf[:, tile * TT:tile * TT + n]

        q4 = lambda ap: ap.rearrange("p i (h c) -> p (i h) c", h=2)

        s_y = sem("y_written")
        N_OUTPUTS = 14
        s_const, s_x, s_par, s_st, s_w2 = (sem(n) for n in ("const_in", "x_in", "params_in", "states_in", "small_weights_in"))
        s_out, s_crow, s_so, s_scr, s_vec, s_ss, s_oread, s_xout, s_xin0, s_xin1 = (sem(n) for n in (
            "outputs_written", "shift_rows_written", "decode_states_written", "scratch_written", "decode_vectors_in",
            "decode_states_in", "decode_rows_in", "x_saved", "x_back0", "x_back1"))
        s_w = [sem(f"ring_in{i}") for i in range(RING)]
        s_zero = sem("zeroed")
        TR = {n: track(n) for n in ("pe0", "act0", "dve0", "pe_f", "act_f", "dve_f", "pe_a", "act_a", "dve_a", "pe_d", "act_d",
                                    "dve_d", "pe_b", "act_b", "dve_b", "pe_c", "act_c", "dve_c", "pe_s", "act_s", "dve_s",
                                    "pe_p", "act_p", "act_w", "pool_w", "pe_n", "act_n", "dve_n", "pe_m", "act_m", "dve_m", "pe9", "act9", "dve9")}
        pe0, act0, dve0 = TR["pe0"], TR["act0"], TR["dve0"]

        PROJ = ([(j * P, "A", j) for j in range(9)] + [(OFF_D + j * P, "D", j) for j in range(6)] + [(OFF_BA, "ba", 0)]
                + [(OFF_DZ + j * P, "D", 6 + j) for j in range(2)] + [(OFF_B + j * P, "B", j) for j in range(8)]
                + [(OFF_C + j * P, "C", j) for j in range(4)])
        N_ADA, N_PROJ, P_D, P_B, P_C = 24, 30, 9, 18, 26
        MERGE = [(n, j) for n in (0, 3, 1, 2) for j in range(KT)]
        RINGSEQ = ([("ada", n) for n in range(16)] + [("proj", n) for n in range(P_D)] + [("ada", n) for n in range(16, N_ADA)]
                   + [("proj", n) for n in range(P_D, P_C)] + [("gate", n) for n in range(8)]
                   + [("proj", n) for n in range(P_C, N_PROJ)] + [("gate", n) for n in range(8, 32)] + [("out", n) for n in range(KT)])
        PLACE = {x: r for r, x in enumerate(RINGSEQ)}
        SPLIT = [x for x in RINGSEQ if x[0] != "ada"]
        SPLACE = {x: q for q, x in enumerate(SPLIT)}
        RAW = {"A": RA, "B": RB, "C": RC, "D": RD}

        def ring_slot(kind, n):
            r = PLACE[kind, n]
            loads = 0
            for q in range(r % RING, r + 1, RING):
                k, m = RINGSEQ[q]
                loads += 2 if k == "gate" or (k == "proj" and PROJ[m][1] == "ba") else 1
            return r % RING, (s_w[r % RING], 16 * loads)

        with nc.Block() as block:
            @block.sync
            def _(sp):
                sp.dma_start(cst[:], a["consts"]).then_inc(s_const, 16)
                sp.dma_start(wv(10, 14 * P), a["tree_masks"]).then_inc(s_const, 16)
                for t in range(4):
                    sp.dma_start(hT[:, 2 * t:2 * t + 2, 0:512], a["x_prompt"][0, t * P:(t + 1) * P, :].rearrange("p (a c) -> p a c", a=2)).then_inc(s_x, 16)
                sp.dma_start(ws[0:8, 0:2, 0:512], a["x_sample"][:, 0, :].rearrange("p (a c) -> p a c", a=2)).then_inc(s_x, 16)
                sp.dma_start(ws[0:8, 2:4, 0:512], a["c_sample"].rearrange("p (a c) -> p a c", a=2)).then_inc(s_x, 16)
                sp.dma_start(ws[8:9, 2:4, 0:512], a["c_prompt"].rearrange("p (a c) -> p a c", a=2)).then_inc(s_x, 16)

            @block.gpsimd
            def _(pool):
                nc.gpsimd.memset(gw[:], 0.0).then_inc(s_zero, 1)
                nc.gpsimd.memset(bg[:], 0.0).then_inc(s_zero, 1)
                pool.wait_ge(s_zero, 2)

            @block.scalar
            def _(act):
                act.wait_ge(s_x, 16 * 7)
                nc.scalar.activation(ws[0:9, 4:6, 0:512], ws[0:9, 2:4, 0:512], ACT.Tanh, scale=0.5).then_inc(*act0.step("tanh_c"))
                for d in range(KT):
                    act.wait_ge(*pe0.at("x", d))
                    nc.scalar.copy(xT[:, d, 0:SEQ], psA[:, d % 4, :]).then_inc(*act0.step("x"))

            @block.vector
            def _(dve):
                dve.wait_ge(s_const, 32)
                nc.vector.tensor_copy(tmask[:], wv(10, 14 * P).rearrange("p (m t) -> p m t", m=14)).then_inc(*dve0.step("tmask"))
                dve.wait_ge(*act0.at("tanh_c"))
                nc.vector.scalar_tensor_tensor(ws[0:9, 4:6, 0:512], ws[0:9, 4:6, 0:512], 1.0, ws[0:9, 2:4, 0:512], add, mult).then_inc(*dve0.step("silu_c"))
                dve.wait_ge(*pe0.at("xs"))
                nc.vector.tensor_copy(xT[:, :, SEQ:TT], psB[:, 0, 0:64].rearrange("p (d b) -> p d b", d=KT)).then_inc(*dve0.step("xs"))
                dve.wait_ge(*pe0.at("c"))
                nc.vector.tensor_scalar(cT[:], psB[:, 1, 0:72].rearrange("p (d b) -> p d b", d=KT), 0.5, None, mult).then_inc(*dve0.step("c"))
                dve.wait_ge(*dve0.at("c"))

            @block.tensor
            def _(pe):
                pe.wait_ge(s_const, 32)
                pe.wait_ge(s_x, 16 * 7)
                for d in range(KT):
                    last = nc.tensor.transpose(psB[:, 0, 8 * d:8 * d + 8], ws[0:8, d // 4, (d % 4) * P:(d % 4 + 1) * P], ident[0:8, 0:8])
                last.then_inc(*pe0.step("xs"))
                pe.wait_ge(*dve0.at("silu_c"))
                for d in range(KT):
                    last = nc.tensor.transpose(psB[:, 1, 9 * d:9 * d + 9], ws[0:9, 4 + d // 4, (d % 4) * P:(d % 4 + 1) * P], ident[0:9, 0:9])
                last.then_inc(*pe0.step("c"))
                for d in range(KT):
                    if d >= 4:
                        pe.wait_ge(*act0.at("x", d - 4))
                    for t in range(4):
                        last = nc.tensor.transpose(psA[:, d % 4, t * P:(t + 1) * P], hT[:, 2 * t + d // 4, (d % 4) * P:(d % 4 + 1) * P], ident)
                    last.then_inc(*pe0.step("x"))

        nc.all_engine_barrier()

        with nc.Fori(0, DEPTH) as layer:
            with nc.Block() as block:
                pe_f, act_f, dve_f = TR["pe_f"], TR["act_f"], TR["dve_f"]
                pp, ap = TR["pe_p"], TR["act_p"]
                pn, an, dn = TR["pe_n"], TR["act_n"], TR["dve_n"]
                aw, pw = TR["act_w"], TR["pool_w"]
                pm, am, dm = TR["pe_m"], TR["act_m"], TR["dve_m"]
                ps_, as_, ds = TR["pe_s"], TR["act_s"], TR["dve_s"]
                def merged_at(idx):
                    return dm.at("mul", idx) if idx < KT else dm.at("mg", idx - KT)

                def tile_part(ap, x):
                    if x[0] == "proj" and PROJ[x[1]][1] == "ba":
                        return ap[:, :, 0:64].rearrange("p k (e c) -> p k e c", e=2)[:, :, :, 0:HEADS]
                    return ap

                def ring_done(r):
                    kind, n = RINGSEQ[r]
                    return {"ada": pe_f, "proj": pp, "gate": pm, "out": pm}[kind].at(kind, n)

                N_PAR, N_ST, N_W2 = 1, 1, 8

                DEC = (("state_rwkv_wkv", "s_wkv", 0, wfC, 3), ("state_gdn", "s_gdn", 3, wfA, 5), ("state_ret", "s_ret", 0, wfA, 2))
                @block.sync
                def _(sp):
                    def decode_state(n):
                        key, _, _, mem, _ = DEC[n]
                        for q in range(4):
                            pr = slice(32 * q, 32 * q + 32)
                            if n == 0:
                                sp.dma_start(mem[pr, 0:1024], a[key][layer].rearrange("b h (q v) k -> q (b h) (v k)", q=4)[q]).then_inc(s_ss, 16)
                            else:
                                sp.dma_start(mem[pr, 0:1024].rearrange("p (k v) -> p k v", v=16),
                                               a[key][layer].rearrange("b h k (q v) -> q (b h) k v", q=4)[q]).then_inc(s_ss, 16)

                    def decode_vectors(n):
                        lo, num = (0, 6) if n == 0 else ((3, 5) if n == 1 else (0, 3))
                        scr, vec = (scrA, vecA) if n == 0 else (scrB, vecB)
                        sp.wait_ge(*as_.at("rows", n))
                        sp.dma_start(scr[lo:lo + num].rearrange("n b (i c) -> (n b i) c", i=2), rowA[0:16 * num, :]).then_inc(s_scr, 16)
                        sp.wait_ge(s_scr, 16 * (5 * n + 1))
                        for q in range(4):
                            pr = slice(32 * q, 32 * q + 32)
                            sp.dma_start(vec[pr, lo:lo + num, :], scr[lo:lo + num].rearrange("n b (h d) -> (b h) n d", h=HEADS)).then_inc(s_vec, 16)
                            sp.dma_start(vv[pr, n, :], scr[(3, 5, 2)[n]].rearrange("b (h q v) -> q (b h) v", h=HEADS, q=4)[q]).then_inc(s_vec, 16)

                    def decode_results(n):
                        _, key, _, mem, _ = DEC[n]
                        sp.wait_ge(*ds.at("so", n))
                        for q in range(4):
                            pr = slice(32 * q, 32 * q + 32)
                            sp.dma_start(scrO[n].rearrange("b (h q v) -> q (b h) v", h=HEADS, q=4)[q], so[pr, n, :]).then_inc(s_scr, 16)
                        sp.wait_ge(s_scr, 16 * (5 * n + 5))
                        if n:
                            sp.wait_ge(*ps_.at("oT", n - 1))
                        sp.dma_start(orow[:], scrO[n]).then_inc(s_oread, 16)
                        for q in range(4):
                            pr = slice(32 * q, 32 * q + 32)
                            if n == 0:
                                sp.dma_start(o[key][layer].rearrange("b h (q v) k -> q (b h) (v k)", q=4)[q], mem[pr, 0:1024]).then_inc(s_so, 16)
                            else:
                                sp.dma_start(o[key][layer].rearrange("b h k (q v) -> q (b h) k v", q=4)[q],
                                               mem[pr, 0:1024].rearrange("p (k v) -> p k v", v=16)).then_inc(s_so, 16)

                    def before(kind, n):
                        if (kind, n) == RINGSEQ[RING]:
                            sp.dma_start(scrX, xT[:]).then_inc(s_xout, 16)
                            decode_state(0)
                            sp.dma_start(o["s_lru_conv"][layer, :, 0:2, :], a["state_lru_conv"][layer, :, 1:3, :]).then_inc(s_out, 16)
                            sp.dma_start(o["s_gdn_conv"][layer, :, 0:2, :], a["state_gdn_conv"][layer, :, 1:3, :]).then_inc(s_out, 16)
                        elif (kind, n) == ("proj", 13):
                            sp.wait_ge(*TR["act_a"].at("crow"))
                            sp.dma_start(o["p_shift"][layer], crowA[2:3, :]).then_inc(s_crow, 16)
                            sp.dma_start(o["s_shift"][layer], crowA[3:11, :]).then_inc(s_crow, 16)
                        elif (kind, n) == ("proj", 20):
                            decode_vectors(0)
                        elif (kind, n) == ("gate", 0):
                            decode_results(0)
                        elif (kind, n) == ("gate", 3):
                            sp.wait_ge(*TR["act_a"].at("mrow"))
                            for i in range(2):
                                sp.dma_start(o["p_wkv"][layer, 0, 2 * i:2 * i + 2].rearrange("g v k -> v g k"),
                                             mrow[:, i, :].rearrange("v (g k) -> v g k", g=2)).then_inc(s_out, 16)
                            sp.wait_ge(*dn.at("gated", 0))
                            decode_state(1)
                        elif (kind, n) == ("gate", 5):
                            sp.wait_ge(*TR["act_d"].at("crow"))
                            sp.dma_start(o["p_gdn_conv"][layer, 0], crow[0:3, 0:6 * P]).then_inc(s_out, 16)
                            sp.dma_start(o["s_gdn_conv"][layer, :, 2, :], crow[3:11, 0:6 * P]).then_inc(s_out, 16)
                        elif (kind, n) == ("proj", 28):
                            decode_vectors(1)
                        elif (kind, n) == ("gate", 9):
                            decode_results(1)
                        elif (kind, n) == ("gate", 10):
                            sp.wait_ge(s_so, 16 * 8)
                            decode_state(2)
                        elif (kind, n) == ("gate", 12):
                            sp.wait_ge(*TR["dve_d"].at("st", NC - 1))
                            sp.dma_start(o["p_gdn"][layer, 0].rearrange("(i g) k v -> (g k) i v", g=2), Mst[2][:]).then_inc(s_out, 16)
                            decode_vectors(2)
                        elif (kind, n) == ("gate", 17):
                            decode_results(2)
                        elif (kind, n) == ("gate", 19):
                            sp.wait_ge(*TR["act_c"].at("crow"))
                            sp.dma_start(o["p_lru_conv"][layer, 0], crow[0:3, 6 * P:8 * P]).then_inc(s_out, 16)
                            sp.dma_start(o["s_lru_conv"][layer, :, 2, :], crow[3:11, 6 * P:8 * P]).then_inc(s_out, 16)
                            sp.wait_ge(*TR["dve_b"].at("st", NC - 1))
                            sp.dma_start(o["p_ret"][layer, 0].rearrange("(i g) k v -> (g k) i v", g=2), Mst[1][:]).then_inc(s_out, 16)
                        elif (kind, n) == ("gate", 28):
                            sp.wait_ge(*TR["act_c"].at("hrow"))
                            sp.dma_start(o["p_lru_h"][layer], hrow[0:1, :]).then_inc(s_out, 16)
                            sp.dma_start(o["s_lru_h"][layer], hrow[1:9, :]).then_inc(s_out, 16)
                        elif (kind, n) == ("out", 3):
                            sp.wait_ge(*pm.at("gl", 31))
                            sp.dma_start(xT[:, 0:4, :], scrX[:, 0:4, :]).then_inc(s_xin0, 16)
                            sp.dma_start(xT[:, 4:8, :], scrX[:, 4:8, :]).then_inc(s_xin1, 16)

                    for r, (kind, n) in enumerate(RINGSEQ):
                        before(kind, n)
                        s, (arrived, _) = ring_slot(kind, n)
                        if r >= RING:
                            sp.wait_ge(*ring_done(r - RING))
                        if kind == "ada":
                            src = a["ada_w"][layer, :, n * P:(n + 1) * P]
                        elif kind == "proj":
                            col, name, _ = PROJ[n]
                            if name == "ba":
                                for e in range(2):
                                    sp.dma_start(ring[:, s, :, 32 * e:32 * e + HEADS],
                                                 a["w_in"][layer, :, col + HEADS * e:col + HEADS * (e + 1)]
                                                 .rearrange("(k p) c -> p k c", p=P)).then_inc(arrived, 16)
                                continue
                            src = a["w_in"][layer, :, col:col + P]
                        elif kind == "gate":
                            br, j = MERGE[n]
                            src = a["w_in"][layer, :, OFF_G + br * D_MODEL + j * P:OFF_G + br * D_MODEL + (j + 1) * P]
                            sp.dma_start(upw[:, s, :, :], a["w_up"][layer, br, :, j * P:(j + 1) * P]
                                         .rearrange("(i p) c -> p i c", p=P)).then_inc(arrived, 16)
                        else:
                            src = a["w_out"][layer, :, n * P:(n + 1) * P]
                        sp.dma_start(ring[:, s, :, :], src.rearrange("(k p) c -> p k c", p=P)).then_inc(arrived, 16)

                    sp.wait_ge(s_crow, 32)
                    sp.wait_ge(s_out, 16 * (N_OUTPUTS - 2))
                    sp.wait_ge(s_so, 16 * 12)

                @block.gpsimd
                def _(pool):
                    for q, (kind, n) in enumerate(SPLIT):
                        s, _ = ring_slot(kind, n)
                        pool.wait_ge(*aw.at("hi", q))
                        nc.gpsimd.tensor_tensor(tile_part(wlo[:, s], (kind, n)), tile_part(ring[:, s], (kind, n)), tile_part(whi[:, q % 2], (kind, n)), sub).then_inc(*pw.step("lo"))

                def headsum(src):
                    s4 = q4(src)
                    for k in range(4):
                        last = nc.tensor.matmul(psB[:, k, 0:HALF], bones, s4[:, k, :], start=True, stop=True)
                    return last

                def slot(h):
                    return 2 * (h % 2) + h // 2

                def hp(h):
                    return slice(HD * (h % 2), HD * (h % 2) + HD)

                def mats(base, sizes):
                    out, at = [], base
                    for n in sizes:
                        out.append(wf[:, at:at + n])
                        at += n
                    return out
                GRa, Ta, Va, Ya, rowsa, X1a, Ua = mats(0, (2048, 512, 512, 512, 768, 256, 256))
                Dd, GRd, Td, Vd, Yd, rowsd, X1d, Ud = mats(10 * TT, (512, 1024, 512, 512, 512, 512, 256, 256))
                h4 = lambda ap: ap.rearrange("p (h t) -> p h t", h=HEADS)
                norm_ws = lambda n: RD[:, 0:2, :] if n == 2 else ws[:, 0:2, :]
                gate_ws = lambda n: RD[:, 2:4, :] if n == 2 else ws[:, 2:4, :]
                GRa4, GRd4 = h4(GRa), h4(GRd)
                AtA, AtD = GRa4[:, :, 0:P], GRd4[:, :, 0:P]
                ARa = wv(10, 2048).rearrange("p (i c x t) -> p i c x t", i=2, c=NC, x=2)
                ARd = RD[:, 0:4, :].rearrange("p a b -> p (a b)")[:, 0:2048].rearrange("p (i c x t) -> p i c x t", i=2, c=NC, x=2)
                ch = lambda c: slice(c * C, (c + 1) * C)
                G1b, krb, vrb = mats(4 * TT, (512, 256, 256))

                two = lambda ap: ap.rearrange("p (h t) -> p h t", h=2)

                def meet(ap, lv, second):
                    if len(ap.shape) == 2:
                        return ap.rearrange("p (n s b) -> p n s b", s=2, b=1 << lv)[:, :, second, :]
                    return ap.rearrange("p h (n s b) -> p h n s b", s=2, b=1 << lv)[:, :, :, second, :]

                def pe_tree(pe, tp, td, ta, At, T, V, Y, c, part):
                    T4, V4, Y4 = h4(T), h4(V), h4(Y)
                    for g in range(2):
                        for n in range(2):
                            last = nc.tensor.matmul(psB[:, 2 + g, n * P:(n + 1) * P], At[:, 2 * g + n, :], ident, start=True, stop=True)
                        last.then_inc(*tp.step("z"))
                    for lv in range(1, 7):
                        for g in range(2):
                            pe.wait_ge(*td.at("t", 14 * c + 2 * (lv - 1) + g))
                            for n in range(2):
                                h = 2 * g + n
                                last = nc.tensor.matmul(psB[:, 2 + g, n * P:(n + 1) * P], At[:, h, :], T4[:, h, :], start=True, stop=True)
                            last.then_inc(*tp.step("y"))
                        part(2 * lv - 2)
                        for g in range(2):
                            pe.wait_ge(*ta.at("y", 12 * c + 2 * (lv - 1) + g))
                            for n in range(2):
                                h = 2 * g + n
                                if lv < 6:
                                    nc.tensor.matmul(psB[:, 2 + g, n * P:(n + 1) * P], V4[:, h, :], Y4[:, h, :], start=True, stop=True)
                                last = nc.tensor.matmul(psB[:, 2 + g, 256 + n * P:256 + (n + 1) * P], Y4[:, h, :], V4[:, h, :], start=True, stop=True)
                            last.then_inc(*tp.step("z"))
                        part(2 * lv - 1)

                def act_tree(act, tp, ta, Y, c):
                    for lv in range(1, 7):
                        for g in range(2):
                            act.wait_ge(*tp.at("y", 12 * c + 2 * (lv - 1) + g))
                            nc.scalar.copy(meet(two(Y[:, 256 * g:256 * g + 256]), lv, 0), meet(two(psB[:, 2 + g, 0:256]), lv, 0)).then_inc(*ta.step("y"))

                def dve_tree(dve, tp, td, At, T, V, c, between=None):
                    T4, V4 = h4(T), h4(V)
                    for lv in range(7):
                        for g in range(2):
                            dve.wait_ge(*tp.at("z", 14 * c + 2 * lv + g))
                            if lv:
                                dve.wait_ge(*td.at("t", 14 * c + 2 * (lv - 1) + g))
                            hs = slice(2 * g, 2 * g + 2)
                            zt = At[:, hs, :] if lv == 0 else two(psB[:, 2 + g, 256:512])
                            if lv < 6:
                                nc.vector.copy_predicated(meet(T4[:, hs, :], lv, 0), bc(meet(tmask[:, lv, :], lv, 0), 1, 2), meet(two(psB[:, 2 + g, 0:256]), lv, 0))
                            nc.vector.copy_predicated(meet(V4[:, hs, :], lv, 1), bc(meet(tmask[:, 7 + lv, :], lv, 1), 1, 2), meet(zt, lv, 1)).then_inc(*td.step("t"))
                        if between:
                            between(lv)

                @block.tensor
                def _(pe):
                    pa, pd, pb, pcc = (TR[n] for n in ("pe_a", "pe_d", "pe_b", "pe_c"))
                    aa, da, ad, dd, ab, db, ac, dc = (TR[n] for n in ("act_a", "dve_a", "act_d", "dve_d", "act_b", "dve_b", "act_c", "dve_c"))

                    PARTS = 12

                    def product(out, x, kind, n, hi, lo, m=P, wait=None, parts=range(PARTS)):
                        s, _ = ring_slot(kind, n)
                        q = SPLACE[kind, n]
                        cols = lambda ap, h: ap[:, h * HALF:(h + 1) * HALF]
                        for p in parts:
                            if p == 0:
                                pe.wait_ge(*aw.at("hi", q))
                            if p < KT:
                                if wait:
                                    pe.wait_ge(*wait(p))
                                for part in (hi, lo):
                                    for h in x:
                                        nc.tensor.matmul(out(h), whi[:, q % 2, p, 0:m], cols(part(p), h), start=(p == 0 and part is hi), stop=False)
                                continue
                            if p == KT:
                                pe.wait_ge(*pw.at("lo", q))
                            for k in (2 * (p - KT), 2 * (p - KT) + 1):
                                for h in x:
                                    last = nc.tensor.matmul(out(h), wlo[:, s, k, 0:m], cols(hi(k), h), start=False, stop=(k == KT - 1))
                        return last if parts[-1] == PARTS - 1 else None

                    h_hi, h_lo = (lambda k: hhi[:, k, :]), (lambda k: hlo[:, k, :])

                    def proj(idx, hf=None, part=None):
                        m = P if PROJ[idx][1] != "ba" else 36
                        if hf != 1 and not part:
                            if idx == P_C:
                                pe.wait_ge(*am.at("th", 7))
                            elif idx == P_C + 1:
                                pe.wait_ge(*dm.at("mul", 7))
                            elif idx >= 2:
                                pe.wait_ge(*ap.at("proj", idx - 2))
                            if idx == P_D:
                                pe.wait_ge(*act_f.at("modrow", 4))
                        last = product(lambda x: psA[0:m, 2 * (idx % 2) + x, 0:HALF], (0, 1) if hf is None else (hf,), "proj", idx,
                                       h_hi, h_lo, m, (lambda k: dve_f.at("hl", k)) if idx == 0 else None,
                                       range(PARTS) if part is None else (part,))
                        if last and hf != 0:
                            last.then_inc(*pp.step("proj"))

                    outs = (RA[:, 2:4, :], RB[:, 4:6, :], RC[:, 0:2, :], RD[:, 4:6, :])

                    def merge(idx):
                        merge_gate(idx)
                        merge_up(idx)

                    def merge_gate(idx):
                        s, arrived = ring_slot("gate", idx)
                        pe.wait_ge(*arrived)
                        if idx == 0:
                            pe.wait_ge(*ap.at("proj", P_C - 1))
                        elif idx == 8:
                            pe.wait_ge(*ap.at("proj", N_PROJ - 1))
                        else:
                            pe.wait_ge(*am.at("th", idx - 1))
                        product(lambda x: psA[:, x, 0:HALF], (0, 1), "gate", idx, h_hi, h_lo).then_inc(*pm.step("gl"))

                    def merge_up(idx):
                        s, _ = ring_slot("gate", idx)
                        if idx in (0, 8, 16, 24):
                            pe.wait_ge(*dn.at("gated", idx // 8))
                        if idx not in (0, 8):
                            pe.wait_ge(*dm.at("mul", idx - 1))
                        for i in range(2):
                            for hf in range(2):
                                last = nc.tensor.matmul(psA[:, 2 + hf, 0:HALF], upw[:, s, i, :], outs[MERGE[idx][0]][:, i, hf * HALF:(hf + 1) * HALF],
                                                        start=(i == 0), stop=(i == 1))
                        last.then_inc(*pm.step("gate"))

                    def crow_rows(tiles, at, b, step):
                        for n, t in enumerate(tiles):
                            last = nc.tensor.transpose(psB[0:11, b + n // 4, (n % 4) * P:(n % 4 + 1) * P], t[:, SEQ - 3:TT], ident)
                        last.then_inc(*step)

                    for d in range(KT):
                        pe.wait_ge(*act_f.at("sq", d))
                        for hf in range(2):
                            last = nc.tensor.matmul(psB[:, 2 + hf, 0:HALF], ones, ws[:, 10 + d, hf * HALF:(hf + 1) * HALF],
                                                    start=(d == 0), stop=(d == KT - 1))
                    last.then_inc(*pe_f.step("ss"))

                    def ada(n, out):
                        s, arrived = ring_slot("ada", n)
                        pe.wait_ge(*arrived)
                        for k in range(KT):
                            last = nc.tensor.matmul(out, cT[:, k, :], ring[:, s, k, :], start=(k == 0), stop=(k == KT - 1))
                        last.then_inc(*pe_f.step("ada"))

                    for r in range(16):
                        ada(r, psA[0:9, r // 4, (r % 4) * P:(r % 4 + 1) * P])
                        if r == 7:
                            pe.wait_ge(s_par, 16 * N_PAR)
                            nc.tensor.transpose(psB[:, 0, 0:PARAM_N], prow[0:PARAM_N, :], ident[0:PARAM_N, 0:PARAM_N]).then_inc(*pe_f.step("par"))
                            pe.wait_ge(s_st, 16 * N_ST)
                            for j in range(7):
                                last = nc.tensor.transpose(psB[:, 1, 64 * j:64 * j + 64], srow[:, j * P:(j + 1) * P], ident[0:64, 0:64])
                            last.then_inc(*pe_f.step("st"))
                    pe.wait_ge(*act_f.at("modrow", 3))
                    pe.wait_ge(*dve_f.at("stT"))
                    for r in range(16):
                        last = nc.tensor.transpose(psB[:, 1, 9 * r:9 * r + 9], ws[0:9, 4 + r // 4, (r % 4) * P:(r % 4 + 1) * P], ident[0:9, 0:9])
                    last.then_inc(*pe_f.step("mod"))
                    for idx in range(P_D):
                        proj(idx)

                    pe.wait_ge(*ap.at("proj", 7))
                    for r in range(16, N_ADA):
                        ada(r, psA[0:9, r // 4 - 2, (r % 4) * P:(r % 4 + 1) * P])
                    pe.wait_ge(*ap.at("proj", 8))
                    crow_rows([RA[:, j] for j in range(7)], 0, 0, pa.step("crow"))
                    pe.wait_ge(*act_f.at("modrow", 4))
                    for r in range(8):
                        last = nc.tensor.transpose(psB[:, 2, 9 * r:9 * r + 9], mg5[0:9, r // 4, (r % 4) * P:(r % 4 + 1) * P], ident[0:9, 0:9])
                    last.then_inc(*pe_f.step("mod"))
                    proj(9)
                    proj(10)
                    pe.wait_ge(*aa.at("twd"))
                    pe.wait_ge(*aa.at("crow"))
                    pe.wait_ge(*dve_f.at("modT", 1))
                    pe.wait_ge(s_w2, 16 * N_W2)
                    for g in range(2):
                        gr = slice(64 * g, 64 * g + 64)
                        if g:
                            pe.wait_ge(*aa.at("thw"))
                        for i in range(2):
                            for hf in range(2):
                                last = nc.tensor.matmul(psB[:, 2 * i + hf, 0:HALF], w2[gr, i * P:(i + 1) * P], RA[gr, 6, hf * HALF:(hf + 1) * HALF],
                                                        start=True, stop=True)
                        last.then_inc(*pa.step("lora"))
                        proj(11 + g)
                    pe.wait_ge(*aa.at("kk2"))
                    pe.wait_ge(*aa.at("tha"))
                    headsum(ws[:, 10:12, :]).then_inc(*pa.step("kks"))
                    for idx in range(13, 17):
                        proj(idx)
                    pe.wait_ge(*da.at("bt"))
                    pe.wait_ge(*aa.at("lnk"))
                    headsum(ws[:, 6:8, :]).then_inc(*pa.step("bsum"))
                    proj(17)
                    pe.wait_ge(*da.at("prep"))
                    nc.tensor.transpose(psB[0:96, 0, 0:P], svA[:].rearrange("p n b i -> p (n b i)"), ident).then_inc(*ps_.step("rows"))
                    pe.wait_ge(*as_.at("rows", 0))
                    Ma = Mst[0]
                    for c in range(NC):
                        if c:
                            pe.wait_ge(*da.at("st", c - 1))
                            pe.wait_ge(*aa.at("o", c - 1))
                        for h in range(HEADS):
                            i = h // 2
                            for x, t in enumerate((14, 16)):
                                last = nc.tensor.matmul(psB[:, h, 256 * x:256 * x + 256], ws[hp(h), t + i, ch(c)], ARa[hp(h), i, c, :, :],
                                                        start=True, stop=True)
                        last.then_inc(*pa.step("gram"))
                        if c < 3:
                            proj(P_B + 2 * c + 1, 0)
                        pe.wait_ge(*da.at("gr", 2 * c + 1))
                        for n, src in enumerate((ws[:, 14], ws[:, 15], ws[:, 16], ws[:, 17], RA[:, 4], RA[:, 5])):
                            last = nc.tensor.transpose(psB[:, n // 4, (n % 4) * P:(n % 4 + 1) * P], src[:, ch(c)], ident)
                        last.then_inc(*pa.step("tr"))
                        pe.wait_ge(*aa.at("rows", c))
                        pe_tree(pe, pa, da, aa, AtA, Ta, Va, Ya, c, lambda part: proj(P_B + 2 * c, part=part))
                        pe.wait_ge(*da.at("t", 14 * c + 13))
                        V4 = h4(Va)
                        for h in range(HEADS):
                            out = psB[:, h % 2, (h // 2) * HD:(h // 2 + 1) * HD]
                            nc.tensor.matmul(out, ARa[hp(h), h // 2, c, 0, :], Ma[hp(h), h // 2, :], start=True, stop=False)
                            last = nc.tensor.matmul(out, GRa4[:, h, 256:384], rowsa[:, 512 + h * HD:512 + (h + 1) * HD], start=False, stop=True)
                        last.then_inc(*pa.step("x1"))
                        if c < 3:
                            proj(P_B + 2 * c + 1, 1)
                        pe.wait_ge(*aa.at("x1", c))
                        for h in range(HEADS):
                            last = nc.tensor.matmul(psB[:, 2, h * HD:(h + 1) * HD], V4[:, h, :], X1a[:, h * HD:(h + 1) * HD], start=True, stop=True)
                        last.then_inc(*pa.step("u"))
                        pe.wait_ge(*da.at("u", c))
                        for h in range(HEADS):
                            out = psB[hp(h), h % 2, (h // 2) * P:(h // 2 + 1) * P]
                            nc.tensor.matmul(out, Ma[hp(h), h // 2, :], ARa[hp(h), h // 2, c, 1, :], start=True, stop=False)
                            nc.tensor.matmul(out, Ua[:, h * HD:(h + 1) * HD], GRa4[:, h, 128:256], start=False, stop=False)
                            nc.tensor.matmul(out, rowsa[:, 512 + h * HD:512 + (h + 1) * HD], GRa4[:, h, 384:512], start=False, stop=True)
                        for i in range(2):
                            s2 = slice(i * P, (i + 1) * P)
                            nc.tensor.matmul(psB[:, 3, s2], rowsa[:, i * P:(i + 1) * P], Ua[:, s2], start=True, stop=False)
                            last = nc.tensor.matmul(psB[:, 3, s2], rowsa[:, 256 + i * P:256 + (i + 1) * P], rowsa[:, 512 + i * P:512 + (i + 1) * P], start=False, stop=True)
                        last.then_inc(*pa.step("o"))
                    pe.wait_ge(*da.at("st", NC - 1))
                    pe.wait_ge(*aa.at("o", NC - 1))
                    for i in range(2):
                        last = nc.tensor.transpose(psB[0:HD, 0, i * P:(i + 1) * P], Ma[:, i, :], ident)
                    last.then_inc(*pa.step("mt"))
                    pe.wait_ge(*aa.at("mrow"))


                    def oT_rows(n):
                        pe.wait_ge(s_oread, 16 * (n + 1))
                        for i in range(2):
                            last = nc.tensor.transpose(psB[:, 1, NB * i:NB * i + NB], orow[:, i * P:(i + 1) * P], ident[0:NB, 0:NB])
                        last.then_inc(*ps_.step("oT"))

                    def norm_sums(n, src):
                        pe.wait_ge(*ds.at("oT", n))
                        if n == 0:
                            headsum(src).then_inc(*pn.step("mean"))
                            proj(P_C - 1)
                        pe.wait_ge(*an.at("sq", n))
                        headsum(norm_ws(n)).then_inc(*pn.step("var"))

                    oT_rows(0)
                    norm_sums(0, RA[:, 2:4, :])
                    pe.wait_ge(*an.at("ln", 0))
                    crow_rows([RD[:, j] for j in range(6)], 9, 0, pd.step("crow"))
                    for idx in range(4):
                        merge(idx)
                    pe.wait_ge(*ad.at("crow"))
                    pe.wait_ge(*ad.at("sq"))
                    headsum(RD[:, 0:2, :]).then_inc(*pd.step("qs"))
                    merge(4)
                    pe.wait_ge(*ad.at("lnq"))
                    headsum(RD[:, 2:4, :]).then_inc(*pd.step("ks"))
                    merge(5)
                    pe.wait_ge(*ad.at("lnk"))
                    pe.wait_ge(*dd.at("gc"))
                    sel2 = cc("sel2").rearrange("p (i t) -> p i t", i=2)
                    for g in range(2):
                        gr = slice(32 * g, 32 * g + HEADS)
                        if g:
                            merge(6)
                            pe.wait_ge(*dd.at("ar"))
                        for i in range(2):
                            nc.tensor.matmul(psB[:, i, :], sel2[gr, i, :], bg[gr, 0:SEQ], start=True, stop=True)
                        for i in range(2):
                            last = nc.tensor.matmul(psB[:, 2, 8 * i:8 * i + 8], sel2[gr, i, :], bg[gr, SEQ:TT], start=True, stop=True)
                        last.then_inc(*pd.step("bcast"))
                    merge(7)
                    pe.wait_ge(*dd.at("prep"))
                    nc.tensor.transpose(psB[0:80, 3, 0:P], svB[:, 3:8].rearrange("p n b i -> p (n b i)"), ident).then_inc(*ps_.step("rows"))
                    pe.wait_ge(*as_.at("rows", 1))
                    Md = Mst[2]
                    sel4 = h4(cc("sel4"))
                    rd4 = h4(GRd)
                    for c in range(NC):
                        if c:
                            pe.wait_ge(*dd.at("st", c - 1))
                            pe.wait_ge(*ad.at("o", c - 1))
                        for h in range(HEADS):
                            nc.tensor.matmul(psB[:, 0, h * P:(h + 1) * P], sel4[32:36, h, :], bg[32:36, ch(c)], start=True, stop=True)
                        nc.tensor.transpose(psB[:, 1, 0:36], bg[:, ch(c)], ident[0:36, 0:36]).then_inc(*pd.step("gb"))
                        for h in range(HEADS):
                            last = nc.tensor.matmul(psB[:, 2 + h % 2, (h // 2) * 256:(h // 2) * 256 + 256], ws[hp(h), 2 + h // 2, ch(c)],
                                                    ARd[hp(h), h // 2, c, :, :], start=True, stop=True)
                        last.then_inc(*pd.step("gram"))
                        pe.wait_ge(*dd.at("dm", c))
                        for n in range(4):
                            last = nc.tensor.transpose(psB[:, 0, n * P:(n + 1) * P], ws[:, 2 + n, ch(c)], ident)
                        last.then_inc(*pd.step("tr"))
                        pe.wait_ge(*dd.at("gr", 2 * c + 1))
                        pe.wait_ge(*ad.at("col", c))
                        pe_tree(pe, pd, dd, ad, AtD, Td, Vd, Yd, c, lambda part: proj(P_C + c, part=part))
                        pe.wait_ge(*dd.at("rows", c))
                        pe.wait_ge(*dd.at("t", 14 * c + 13))
                        for h in range(HEADS):
                            last = nc.tensor.matmul(psB[:, h % 2, (h // 2) * HD:(h // 2 + 1) * HD], RD[hp(h), 4 + h // 2, ch(c)], Md[hp(h), h // 2, :], start=True, stop=True)
                        last.then_inc(*pd.step("x1"))
                        pe.wait_ge(*dd.at("x1", c))
                        for h in range(HEADS):
                            last = nc.tensor.matmul(psB[:, 2, h * HD:(h + 1) * HD], h4(Vd)[:, slot(h), :], X1d[:, h * HD:(h + 1) * HD], start=True, stop=True)
                        last.then_inc(*pd.step("u"))
                        pe.wait_ge(*ad.at("u", c))
                        for h in range(HEADS):
                            out = psB[hp(h), h % 2, (h // 2) * P:(h // 2 + 1) * P]
                            nc.tensor.matmul(out, Md[hp(h), h // 2, :], ws[hp(h), 6 + h // 2, ch(c)], start=True, stop=False)
                            nc.tensor.matmul(out, Ud[:, h * HD:(h + 1) * HD], rd4[:, slot(h), 128:256], start=False, stop=True)
                        for i in range(2):
                            s2 = slice(i * P, (i + 1) * P)
                            last = nc.tensor.matmul(psB[:, 3, s2], rowsd[:, s2], Ud[:, s2], start=True, stop=True)
                        last.then_inc(*pd.step("o"))

                    pe.wait_ge(*dd.at("st", NC - 1))
                    pe.wait_ge(*ad.at("o", NC - 1))
                    oT_rows(1)
                    norm_sums(1, None)
                    pe.wait_ge(*an.at("ln", 1))
                    for n in range(2):
                        if n:
                            pe.wait_ge(*db.at("rot", 0))
                        s4 = q4(RB[:, 2 * n:2 * n + 2, :])
                        for k in range(4):
                            last = nc.tensor.matmul(psB[:, k, 0:HALF], cc("rotp"), s4[:, k, :], start=True, stop=True)
                        last.then_inc(*pb.step("rot"))
                        merge_gate(8 + n)
                    merge_up(8)
                    merge_up(9)
                    pe.wait_ge(*db.at("prep"))
                    nc.tensor.transpose(psB[0:48, 3, 0:P], svB[:, 0:3].rearrange("p n b i -> p (n b i)"), ident).then_inc(*ps_.step("rows"))
                    pe.wait_ge(*as_.at("rows", 2))
                    Mb = Mst[1]
                    for c in range(NC):
                        if c:
                            pe.wait_ge(*db.at("st", c - 1))
                            pe.wait_ge(*ab.at("o", c - 1))
                        for h in range(HEADS):
                            last = nc.tensor.matmul(psB[:, h % 2, (h // 2) * P:(h // 2 + 1) * P], RB[hp(h), 2 + h // 2, ch(c)], RB[hp(h), h // 2, ch(c)], start=True, stop=True)
                        last.then_inc(*pb.step("gram"))
                        for n in range(4):
                            last = nc.tensor.transpose(psB[:, 2, n * P:(n + 1) * P], RB[:, 2 + n, ch(c)], ident)
                        last.then_inc(*pb.step("tr"))
                        merge_gate(10 + c)
                        pe.wait_ge(*db.at("gr", c))
                        pe.wait_ge(*db.at("rows", c))
                        for h in range(HEADS):
                            out = psB[hp(h), h % 2, (h // 2) * P:(h // 2 + 1) * P]
                            nc.tensor.matmul(out, Mb[hp(h), h // 2, :], ws[hp(h), 2 + h // 2, ch(c)], start=True, stop=False)
                            nc.tensor.matmul(out, vrb[:, h * HD:(h + 1) * HD], h4(G1b)[:, h, :], start=False, stop=True)
                        for i in range(2):
                            s2 = slice(i * P, (i + 1) * P)
                            last = nc.tensor.matmul(psB[:, 3, s2], krb[:, s2], vrb[:, s2], start=True, stop=True)
                        last.then_inc(*pb.step("o"))
                        merge_up(10 + c)

                    pe.wait_ge(*db.at("st", NC - 1))
                    pe.wait_ge(*ab.at("o", NC - 1))
                    crow_rows([RC[:, j] for j in range(2)], 7, 3, pcc.step("crow"))
                    pe.wait_ge(*ac.at("crow"))
                    pe.wait_ge(*dc.at("xc"))
                    for g in range(2):
                        if g:
                            pe.wait_ge(*ac.at("thr"))
                        for i in range(2):
                            for hf in range(2):
                                last = nc.tensor.matmul(psB[:, 2 * i + hf, 0:HALF], gw[:, 2 * g + i, :], ws[:, i, hf * HALF:(hf + 1) * HALF], start=True, stop=True)
                        last.then_inc(*pcc.step("gates"))
                        merge(14 + g)
                    pe.wait_ge(*ac.at("thi"))
                    oT_rows(2)
                    merge_gate(16)
                    norm_sums(2, None)
                    merge_gate(17)
                    merge_up(16)
                    merge_up(17)
                    for idx in range(18, 20):
                        merge(idx)
                    pe.wait_ge(*an.at("ln", 2))
                    pe.wait_ge(*dc.at("h"))
                    for i in range(2):
                        last = nc.tensor.transpose(psB[0:9, 0, i * P:(i + 1) * P], RC[:, i, SEQ - 1:TT], ident)
                    last.then_inc(*pcc.step("hrow"))
                    for idx in range(20, 32):
                        merge(idx)

                    pe.wait_ge(*am.at("th", 31))
                    for e in range(KT):
                        b = 2 * (e % 2)
                        if e == 1:
                            pe.wait_ge(*merged_at(31))
                        elif e >= 2:
                            pe.wait_ge(*dm.at("x", e - 2))
                        product(lambda x: psA[:, b + x, 0:HALF], (0, 1), "out", e, lambda k: mhi[:, k, :], lambda k: mlo[k],
                                wait=(lambda k: dm.at("mlo", k)) if e == 0 else None).then_inc(*pm.step("out"))

                @block.scalar
                def _(act):
                    A = nc.scalar.activation
                    eps = cc("eps")
                    half = lambda ap: ap.rearrange("p (h c) -> p h c", h=2)

                    def split(q):
                        if q < len(SPLIT):
                            s, arrived = ring_slot(*SPLIT[q])
                            act.wait_ge(*arrived)
                            if q >= 2:
                                kind, n = SPLIT[q - 2]
                                act.wait_ge(*(pm.at("gl", n) if kind == "gate" else ring_done(PLACE[kind, n])))
                            nc.scalar.copy(tile_part(whi[:, q % 2], SPLIT[q]), tile_part(ring[:, s], SPLIT[q])).then_inc(*aw.step("hi"))

                    def evac(*idxs, ahead=True):
                        for idx in idxs:
                            _, name, j = PROJ[idx]
                            b = 2 * (idx % 2)
                            act.wait_ge(*pp.at("proj", idx))
                            if idx == P_C:
                                act.wait_ge(s_so, 16 * (4))
                            if name == "ba":
                                A(half(bg[0:4, :]), psA[0:4, b:b + 2, 0:HALF], ACT.Tanh, scale=0.5)
                                A(half(bg[32:36, :]), psA[32:36, b:b + 2, 0:HALF], ACT.Identity, bias=gp[32:36, 1:2]).then_inc(*ap.step("proj"))
                            else:
                                nc.scalar.copy(half(RAW[name][:, j, :]), psA[:, b:b + 2, 0:HALF]).then_inc(*ap.step("proj"))
                            if ahead:
                                split(SPLACE["proj", idx] + 2)

                    def gates(*idxs):
                        for idx in idxs:
                            act.wait_ge(*pm.at("gl", idx))
                            if idx >= 2:
                                act.wait_ge(*merged_at(idx - 2))
                            A(half(tg[:, idx % 2, :]), psA[:, 0:2, 0:HALF], ACT.Tanh, scale=0.5).then_inc(*am.step("th"))
                            split(SPLACE["gate", idx] + 2)

                    def decode_rows(n, b):
                        act.wait_ge(*ps_.at("rows", n))
                        if n:
                            act.wait_ge(s_scr, 16 * (5 * n - 4))
                        rows = (96, 80, 48)[n]
                        nc.scalar.copy(rowA[0:rows, :], psB[0:rows, b, 0:P]).then_inc(*as_.step("rows"))

                    def norm(n, src, e):
                        act.wait_ge(*(dn.at("cen") if n == 0 else ds.at("oT", n)))
                        A(norm_ws(n), src, ACT.Square).then_inc(*an.step("sq"))
                        act.wait_ge(*pn.at("var", n))
                        A(q4(norm_ws(n)), psB[:, :, 0:HALF], ACT.Ln, bias=e, scale=1.0 / HD).then_inc(*an.step("ln"))
                        act.wait_ge(*an.at("ln", n))
                        A(norm_ws(n), norm_ws(n), ACT.Exp, scale=-0.5).then_inc(*an.step("rn"))

                    def gate(n, z):
                        A(gate_ws(n), z, ACT.Tanh, scale=0.5).then_inc(*an.step("tz"))

                    def tree_start(T, V, td, tp, ta, c):
                        if c:
                            act.wait_ge(*tp.at("u", c - 1))
                        nc.scalar.copy(h4(T), bc(ident, 1, HEADS))
                        nc.scalar.copy(h4(V), bc(ident, 1, HEADS)).then_inc(*ta.step("ti"))

                    for d in range(KT):
                        A(ws[:, 10 + d, :], xT[:, d, :], ACT.Square).then_inc(*act_f.step("sq"))
                    act.dma_start(prow[0:PARAM_N, :], a["param_rows"][layer]).then_inc(s_par, 16)
                    act.dma_start(srow[:, :], a["state_rows"][layer]).then_inc(s_st, 16)
                    act.dma_start(w2[0:64, :], a["rwkv_w2"][layer]).then_inc(s_w2, 16)
                    act.dma_start(w2[64:128, :], a["rwkv_a2"][layer]).then_inc(s_w2, 16)
                    for g in range(2):
                        for hf in range(2):
                            act.dma_start(gw[hf * HD:(hf + 1) * HD, 2 * g:2 * g + 2, hf * HD:(hf + 1) * HD],
                                          a["lru_gate_w"][layer, g].rearrange("(i f) d e -> f d i e", f=2)[hf]).then_inc(s_w2, 16)
                    act.dma_start(gp[32:36, 0:1], a["gdn_A_log"][layer].unsqueeze(1)).then_inc(s_w2, 16)
                    act.dma_start(gp[32:36, 1:2], a["gdn_dt_bias"][layer].unsqueeze(1)).then_inc(s_w2, 16)
                    act.wait_ge(*pe_f.at("ss"))
                    A(half(rs[:]), psB[:, 2:4, 0:HALF], ACT.Ln, bias=eps, scale=1.0 / D_MODEL).then_inc(*act_f.step("lnx"))
                    act.wait_ge(*act_f.at("lnx"))
                    A(rs[:], rs[:], ACT.Exp, scale=-0.5).then_inc(*act_f.step("rs"))
                    for g in range(4):
                        act.wait_ge(*pe_f.at("ada", 4 * g + 3))
                        nc.scalar.copy(ws[0:9, 4 + g, 0:512], psA[0:9, g, :]).then_inc(*act_f.step("modrow"))
                    act.wait_ge(*dve_f.at("der"))
                    A(der[:, 20:22], par("lam", 0, 2), ACT.Abs).then_inc(*act_f.step("lam_abs"))
                    act.wait_ge(*act_f.at("lam_abs"))
                    A(der[:, 22:24], der[:, 20:22], ACT.Exp, scale=-1.0).then_inc(*act_f.step("lam_z"))
                    act.wait_ge(s_w2, 16 * N_W2)
                    A(gp[32:36, 2:3], gp[32:36, 0:1], ACT.Exp).then_inc(*act_f.step("expA"))
                    split(0)
                    act.wait_ge(s_xout, 16)
                    for d in range(KT):
                        act.wait_ge(*dve_f.at("hs", d))
                        nc.scalar.copy(hhi[:, d, :], hT[:, d, :]).then_inc(*act_f.step("hh"))
                    split(1)
                    evac(*range(7))
                    evac(7, 8, ahead=False)

                    pa, aa, da = TR["pe_a"], TR["act_a"], TR["dve_a"]
                    act.wait_ge(*pe_f.at("ada", 23))
                    nc.scalar.copy(mg5[0:9, 0:2, 0:512], psA[0:9, 2:4, :]).then_inc(*act_f.step("modrow"))
                    split(9)
                    split(10)
                    act.wait_ge(*pa.at("crow"))
                    nc.scalar.copy(crowA[:, 0:512], psB[0:11, 0, :])
                    nc.scalar.copy(crowA[:, 512:7 * P], psB[0:11, 1, 0:3 * P]).then_inc(*aa.step("crow"))
                    evac(9)
                    act.wait_ge(*da.at("pm"))
                    A(RA[0:64, 6, :], RA[0:64, 6, :], ACT.Tanh).then_inc(*aa.step("twd"))
                    for g, (nm, hb, t) in enumerate((("thw", 0, 0), ("tha", 2, 8))):
                        act.wait_ge(*pa.at("lora", g))
                        for i in range(2):
                            last = A(half(ws[:, t + i, :]), psB[:, 2 * i:2 * i + 2, 0:HALF], ACT.Tanh, bias=der[:, hb + i:hb + i + 1], scale=0.5)
                        last.then_inc(*aa.step(nm))
                        evac(10 + g)
                    act.wait_ge(*da.at("kk"))
                    A(ws[:, 10:12, :], ws[:, 6:8, :], ACT.Square).then_inc(*aa.step("kk2"))
                    evac(12)
                    act.wait_ge(*aa.at("tha"))
                    for i in range(2):
                        last = A(ws[:, 12 + i, :], ws[:, 8 + i, :], ACT.Identity, bias=der[:, 6 + i:7 + i], scale=der[:, 4 + i:5 + i])
                    last.then_inc(*aa.step("kf"))
                    act.wait_ge(*pa.at("kks"))
                    A(q4(ws[:, 10:12, :]), psB[:, :, 0:HALF], ACT.Ln, bias=eps).then_inc(*aa.step("lnk"))
                    act.wait_ge(*aa.at("lnk"))
                    A(ws[:, 10:12, :], ws[:, 10:12, :], ACT.Exp, scale=-0.5).then_inc(*aa.step("rn"))
                    evac(13)
                    act.wait_ge(*da.at("lex"))
                    A(ws[:, 4:6, :], ws[:, 2:4, :], ACT.Exp, scale=W_DECAY)
                    A(pc[:, 0], mid[:], ACT.Exp, scale=W_DECAY)
                    A(ws[:, 0:2, 0:SEQ], ws[:, 0:2, 0:SEQ], ACT.Exp, scale=W_DECAY).then_inc(*aa.step("decay"))
                    act.wait_ge(*aa.at("decay"))
                    A(ws[:, 2:4, 0:SEQ], ws[:, 2:4, 0:SEQ], ACT.Exp, scale=-W_DECAY).then_inc(*aa.step("exps"))
                    evac(14, 15, 16, 17)
                    decode_rows(0, 0)
                    for c in range(NC):
                        tree_start(Ta, Va, da, pa, aa, c)
                        act.wait_ge(*pa.at("tr", c))
                        nc.scalar.copy(rowsa[:, 0:512], psB[:, 0, :])
                        nc.scalar.copy(rowsa[:, 512:768], psB[:, 1, 0:256]).then_inc(*aa.step("rows"))
                        act_tree(act, pa, aa, Ya, c)
                        act.wait_ge(*pa.at("x1", c))
                        nc.scalar.copy(X1a.rearrange("p (i g v) -> p i g v", i=2, g=2), psB[:, 0:2, 0:P].rearrange("p g (i v) -> p i g v", i=2)).then_inc(*aa.step("x1"))
                        evac(P_B + 2 * c)
                        act.wait_ge(*pa.at("o", c))
                        for g in range(2):
                            pr = slice(g * HD, (g + 1) * HD)
                            last = nc.scalar.copy(RA[pr, 2:4, ch(c)], psB[pr, g, 0:256].rearrange("p (i t) -> p i t", i=2))
                        last.then_inc(*aa.step("o"))
                        if c < 3:
                            evac(P_B + 2 * c + 1)
                    act.wait_ge(*pa.at("mt"))
                    nc.scalar.copy(mrow[:], psB[0:HD, 0, 0:256].rearrange("p (i t) -> p i t", i=2)).then_inc(*aa.step("mrow"))

                    norm(0, RA[:, 2:4, :], cc("epsgn"))
                    evac(P_C - 1)
                    gate(0, RA[:, 7:9, :])
                    gates(0)

                    pd, ad, dd = TR["pe_d"], TR["act_d"], TR["dve_d"]
                    act.wait_ge(*dn.at("gated", 0))
                    act.wait_ge(*pd.at("crow"))
                    nc.scalar.copy(crow[:, 0:4 * P], psB[0:11, 0, :])
                    nc.scalar.copy(crow[:, 4 * P:6 * P], psB[0:11, 1, 0:2 * P]).then_inc(*ad.step("crow"))
                    for t in range(6):
                        last = A(ws[:, t, 0:SEQ], RD[:, t, 0:SEQ], ACT.Identity, scale=par("gdn_w", 18 + t))
                    last.then_inc(*ad.step("cv0"))
                    A(ws[32:36, 10, :], bg[32:36, :], ACT.Abs).then_inc(*ad.step("gabs"))
                    act.wait_ge(*ad.at("gabs"))
                    A(ws[32:36, 11, :], ws[32:36, 10, :], ACT.Exp, scale=-1.0).then_inc(*ad.step("gz"))
                    gates(1, 2)
                    act.wait_ge(*dd.at("cv"))
                    A(RD[:, 0:6, :], ws[:, 0:6, :], ACT.Tanh, scale=0.5).then_inc(*ad.step("ths"))
                    gates(3)
                    act.wait_ge(*dd.at("silu2"))
                    A(RD[:, 0:4, :], ws[:, 0:4, :], ACT.Square).then_inc(*ad.step("sq"))
                    act.wait_ge(*pd.at("qs"))
                    A(q4(RD[:, 0:2, :]), psB[:, :, 0:HALF], ACT.Ln, bias=eps, scale=0.25).then_inc(*ad.step("lnq"))
                    gates(4)
                    act.wait_ge(*pd.at("ks"))
                    A(q4(RD[:, 2:4, :]), psB[:, :, 0:HALF], ACT.Ln, bias=eps, scale=0.25).then_inc(*ad.step("lnk"))
                    act.wait_ge(*ad.at("lnk"))
                    A(RD[:, 0:4, :], RD[:, 0:4, :], ACT.Exp, scale=-0.5).then_inc(*ad.step("rn"))
                    gates(5, 6)
                    act.wait_ge(*pd.at("bcast", 1))
                    A(ws[:, 6:8, 0:SEQ], psB[:, 0:2, :], ACT.Exp)
                    A(ws[:, 6:8, SEQ:TT], psB[:, 2, 0:16].rearrange("p (i b) -> p i b", i=2), ACT.Exp).then_inc(*ad.step("egc"))
                    gates(7)
                    decode_rows(1, 3)
                    for c in range(NC):
                        tree_start(Td, Vd, dd, pd, ad, c)
                        act.wait_ge(*pd.at("gb", c))
                        nc.scalar.copy(colbg[:], psB[:, 1, 0:36]).then_inc(*ad.step("col"))
                        act.wait_ge(*dd.at("dm", c))
                        A(Dd, Dd, ACT.Exp)
                        A(kdl[:], kdl[:], ACT.Exp).then_inc(*ad.step("dexp"))
                        act_tree(act, pd, ad, Yd, c)
                        act.wait_ge(*pd.at("u", c))
                        nc.scalar.copy(Ud, psB[:, 2, 0:256]).then_inc(*ad.step("u"))
                        evac(P_C + c)
                        act.wait_ge(*pd.at("o", c))
                        for g in range(2):
                            pr = slice(g * HD, (g + 1) * HD)
                            last = nc.scalar.copy(RD[pr, 4:6, ch(c)], psB[pr, g, 0:256].rearrange("p (i t) -> p i t", i=2))
                        last.then_inc(*ad.step("o"))
                    norm(1, RD[:, 4:6, :], eps)
                    gate(1, RD[:, 6:8, :])

                    pb, ab, db = TR["pe_b"], TR["act_b"], TR["dve_b"]
                    gates(8, 9)
                    decode_rows(2, 3)
                    ac = TR["act_c"]
                    for i in range(2):
                        last = A(ws[:, i, 0:SEQ], RC[:, i, 0:SEQ], ACT.Identity, bias=par("lru_b", i), scale=par("lru_w", 6 + i))
                    last.then_inc(*ac.step("cv0"))
                    for c in range(NC):
                        act.wait_ge(*pb.at("o", c))
                        for g in range(2):
                            pr = slice(g * HD, (g + 1) * HD)
                            last = nc.scalar.copy(RB[pr, 4:6, ch(c)], psB[pr, g, 0:256].rearrange("p (i t) -> p i t", i=2))
                        last.then_inc(*ab.step("o"))
                        gates(10 + c)

                    pcc, ac, dc = TR["pe_c"], TR["act_c"], TR["dve_c"]
                    act.wait_ge(*pcc.at("crow"))
                    nc.scalar.copy(crow[:, 6 * P:8 * P], psB[0:11, 3, 0:2 * P]).then_inc(*ac.step("crow"))
                    for g, (nm, t) in enumerate((("thr", 2), ("thi", 4))):
                        act.wait_ge(*pcc.at("gates", g))
                        for i in range(2):
                            last = A(half(ws[:, t + i, :]), psB[:, 2 * i:2 * i + 2, 0:HALF], ACT.Tanh, bias=der[:, 8 + 2 * g + i:9 + 2 * g + i], scale=0.5)
                        last.then_inc(*ac.step(nm))
                        gates(14 + g)
                    for i in range(2):
                        A(ws[:, 6 + i, :], ws[:, 2 + i, :], ACT.Exp, bias=der[:, 14 + i:15 + i], scale=der[:, 14 + i:15 + i])
                        last = A(ws[:, 8 + i, :], ws[:, 2 + i, :], ACT.Tanh, bias=der[:, 12 + i:13 + i], scale=der[:, 12 + i:13 + i])
                    last.then_inc(*ac.step("au"))
                    gates(16)
                    norm(2, RB[:, 4:6, :], eps)
                    gate(2, RB[:, 6:8, :])
                    gates(17)
                    act.wait_ge(*dc.at("u2"))
                    A(ws[:, 10:12, :], ws[:, 10:12, :], ACT.Ln)
                    A(ws[:, 12:14, :], ws[:, 8:10, :], ACT.Ln, bias=cc("ones")[:, 0:1]).then_inc(*ac.step("lnu"))
                    act.wait_ge(*dc.at("lndiff"))
                    A(ws[:, 10:12, :], ws[:, 10:12, :], ACT.Exp, scale=0.5).then_inc(*ac.step("root"))
                    gates(18, 19)
                    act.wait_ge(*dc.at("h"))
                    gate(3, RC[:, 2:4, :])
                    act.wait_ge(*pcc.at("hrow"))
                    nc.scalar.copy(hrow[:], psB[0:9, 0, 0:256]).then_inc(*ac.step("hrow"))
                    gates(20, 21)
                    gates(*range(22, 24))
                    def m_hi(j):
                        act.wait_ge(*merged_at(24 + j))
                        nc.scalar.copy(mhi[:, j, :], mg[j]).then_inc(*am.step("mhi"))
                    for j in range(KT):
                        gates(24 + j)
                        if j:
                            m_hi(j - 1)
                    m_hi(KT - 1)
                    for e in range(2, KT):
                        split(SPLACE["out", e])

                @block.vector
                def _(dve):
                    v = nc.vector
                    T_, S_, STT = v.tensor_tensor, v.tensor_scalar, v.scalar_tensor_tensor

                    def did(track_, name, ins, i=0):
                        ins.then_inc(*track_.step(name))
                        dve.wait_ge(*track_.at(name, i))

                    half = lambda ap: ap.rearrange("p (h c) -> p h c", h=2)
                    for m in Mst:
                        last = v.memset(m[:], 0.0)
                    last.then_inc(*dve_f.step("zero"))
                    dve.wait_ge(*pe_f.at("par"))
                    did(dve_f, "parT", v.tensor_copy(parT[:, 0:PARAM_N], psB[:, 0, 0:PARAM_N]))
                    S_(der[:, 0:2], par("w0", 0, 2), 0.5, None, mult)
                    S_(der[:, 2:4], par("a0", 0, 2), 0.5, None, mult)
                    S_(der[:, 4:6], par("k_a", 0, 2), 0.5, None, mult)
                    S_(der[:, 6:8], par("k_a", 0, 2), -0.5, 1.0, mult, add)
                    did(dve_f, "der", S_(der[:, 8:12], par("gate_b", 0, 4), 0.5, None, mult))
                    dve.wait_ge(*pe_f.at("st"))
                    did(dve_f, "stT", v.tensor_copy(stT[:], psB[:, 1, 0:448].rearrange("p (j r) -> p j r", j=7)))

                    def log1p(tr, pre, z, t, t2, acc, between=None):
                        did(tr, pre + "1", S_(t, z, 2.0, None, add))
                        did(tr, pre + "2", v.reciprocal(t2, t))
                        did(tr, pre + "3", T_(t, z, t2, mult))
                        did(tr, pre + "4", T_(t2, t, t, mult))
                        did(tr, pre + "5", S_(acc, t2, 2.0 / 17, 2.0 / 15, mult, add))
                        for n in (13, 11, 9, 7, 5, 3, 1):
                            did(tr, pre + f"m{n}", T_(acc, acc, t2, mult))
                            did(tr, pre + f"a{n}", S_(acc, acc, 2.0 / n, None, add))
                            if n == 7 and between:
                                between()
                        did(tr, pre + "6", T_(acc, acc, t, mult))

                    dve.wait_ge(*act_f.at("rs"))
                    for d in range(KT):
                        last = T_(hT[:, d, :], xT[:, d, :], rs[:], mult)
                    did(dve_f, "xn", last)
                    dve.wait_ge(*pe_f.at("mod", 0))
                    did(dve_f, "modT", T_(modT[:, 0:16, :], psB[:, 1, 0:144].rearrange("p (r s) -> p r s", r=16), bc(par("ada_b", 0, 16), 2, 9), add))
                    did(dve_f, "G", STT(G[:], modT[:, 8:16, :], 1.0, bc(par("norm_g", 0, 8), 2, 9), add, mult))
                    did(dve_f, "hg", T_(hT[:, :, SEQ:TT], hT[:, :, SEQ:TT], G[:, :, 0:8], mult))
                    did(dve_f, "hd", T_(hT[:, :, SEQ:TT], hT[:, :, SEQ:TT], modT[:, 0:8, 0:8], add))
                    def h_lo(d):
                        dve.wait_ge(*act_f.at("hh", d))
                        T_(hlo[:, d, :], hT[:, d, :], hhi[:, d, :], sub).then_inc(*dve_f.step("hl"))

                    for d in range(KT):
                        S_(hT[:, d, 0:SEQ], hT[:, d, 0:SEQ], G[:, d, 8:9], modT[:, d, 8:9], mult, add).then_inc(*dve_f.step("hs"))
                        if d:
                            h_lo(d - 1)
                    h_lo(KT - 1)
                    dve.wait_ge(*act_f.at("lam_z"))
                    log1p(dve_f, "lam", der[:, 22:24], der[:, 24:26], der[:, 26:28], der[:, 28:30])
                    did(dve_f, "lam_y", S_(der[:, 30:32], par("lam", 0, 2), -1.0, 0.0, mult, ALU.max))
                    did(dve_f, "lam_sp", T_(der[:, 30:32], der[:, 30:32], der[:, 28:30], add))
                    S_(der[:, 12:14], der[:, 30:32], LRU_C / 2, None, mult)
                    S_(der[:, 14:16], der[:, 30:32], -LRU_C / 2, None, mult)
                    pa, aa, da = TR["pe_a"], TR["act_a"], TR["dve_a"]
                    outs3 = (RA[:, 2:4, :], RD[:, 4:6, :], RB[:, 4:6, :])
                    row = lambda x: bc(x, 1, 16)
                    col = lambda x: bc(x, 2, 16)
                    vk = lambda x: x.rearrange("p (v k) -> p v k", v=16)
                    kv = lambda x: x.rearrange("p (k v) -> p k v", v=16)
                    kvT = lambda x: x.rearrange("p (k v) -> p v k", v=16)

                    def m_lo(j):
                        dve.wait_ge(*am.at("mhi", j))
                        T_(mlo[j], mg[j], mhi[:, j, :], sub).then_inc(*dm.step("mlo"))

                    def merged(*idxs):
                        for idx in idxs:
                            j = MERGE[idx][1]
                            dve.wait_ge(*pm.at("gate", idx))
                            if idx == 5:
                                dve.wait_ge(s_crow, 32)
                            dve.wait_ge(*am.at("th", idx))
                            th, up = half(tg[:, idx % 2, :]), psA[:, 2:4, 0:HALF]
                            if idx < KT:
                                STT(half(mg[j]), th, 1.0, up, add, mult).then_inc(*dm.step("mul"))
                            else:
                                did(dm, "mul", STT(th, th, 1.0, up, add, mult), idx)
                                T_(mg[j], mg[j], tg[:, idx % 2, :], add).then_inc(*dm.step("mg"))
                            if idx > 24:
                                m_lo(j - 1)

                    def decode_in(n):
                        dve.wait_ge(s_vec, 16 * (8 * n + 8))
                        dve.wait_ge(s_ss, 16 * (4 * n + 4))

                    def decode_out(n):
                        dve.wait_ge(*ps_.at("oT", n))
                        did(ds, "oT", v.tensor_copy(outs3[n][:, :, SEQ:TT], psB[:, 1, 0:2 * NB].rearrange("p (i b) -> p i b", i=2)), n)

                    def gated(n, out, z):
                        dve.wait_ge(*an.at("tz", n))
                        did(dn, "siluz", STT(gate_ws(n), gate_ws(n), 1.0, z, add, mult), n)
                        did(dn, "gated", STT(out, out, 0.5, gate_ws(n), mult, mult), n)

                    dve.wait_ge(*ap.at("proj", 8))
                    T_(ws[:, 0:7, 1:SEQ], RA[:, 0:7, 0:SEQ - 1], RA[:, 0:7, 1:SEQ], sub)
                    S_(ws[:, 0:7, 0:1], RA[:, 0:7, 0:1], -1.0, None, mult)
                    did(da, "diff", T_(ws[:, 0:7, SEQ:TT], stT[:, :, 0:8], RA[:, 0:7, SEQ:TT], sub))
                    dve.wait_ge(*pa.at("crow"))
                    for j in range(7):
                        last = STT(RA[:, j, :], ws[:, j, :], par("mu", j), RA[:, j, :], mult, add)
                    did(da, "pm", last)
                    dve.wait_ge(*pe_f.at("mod", 1))
                    did(dve_f, "modT", T_(modT[:, 16:24, :], psB[:, 2, 0:72].rearrange("p (r s) -> p r s", r=8), bc(par("ada_b", 16, 8), 2, 9), add), 1)
                    did(dve_f, "gate", S_(modT[:, 16:24, :], modT[:, 16:24, :], 0.5, None, mult))
                    for i in range(2):
                        last = S_(ws[:, 6 + i, :], RA[:, 2 + i, :], par("k_k", i), None, mult)
                    did(da, "kk", last)
                    dve.wait_ge(*aa.at("thw"))
                    did(da, "lw1", S_(ws[:, 0:2, :], ws[:, 0:2, :], 1.0, None, add))
                    for i in range(2):
                        last = v.tensor_tensor_scan(ws[:, 2 + i, :], cc("reset"), ws[:, i, :], 0.0, mult, add)
                    did(da, "scan", last)
                    L4 = ws[:, 2:4, 0:SEQ].rearrange("p i (c t) -> p i c t", c=NC)
                    did(da, "mid", v.tensor_copy(mid[:], L4[:, :, :, C // 2 - 1]))
                    did(da, "lrel", T_(L4, L4, bc(mid[:], 3, C), sub))
                    did(da, "lex", T_(ws[:, 0:2, 0:SEQ], ws[:, 2:4, 0:SEQ], ws[:, 0:2, 0:SEQ], sub))
                    dve.wait_ge(*aa.at("kf"))
                    S_(ws[:, 8:10, :], ws[:, 8:10, :], 0.5, 0.5, mult, add)
                    T_(RA[:, 2:4, :], RA[:, 2:4, :], ws[:, 12:14, :], mult)
                    dve.wait_ge(*aa.at("rn"))
                    did(da, "kkn", T_(ws[:, 6:8, :], ws[:, 6:8, :], ws[:, 10:12, :], mult))
                    did(da, "bv", T_(ws[:, 8:10, :], ws[:, 8:10, :], ws[:, 6:8, :], mult))
                    dve.wait_ge(*aa.at("exps"))
                    svt = lambda sv, n: sv[:, n].rearrange("p b i -> p i b")
                    for n, src in ((0, RA[:, 0:2]), (1, ws[:, 4:6]), (2, RA[:, 2:4]), (3, RA[:, 4:6]), (5, ws[:, 8:10])):
                        v.tensor_copy(svt(svA, n), src[:, :, SEQ:TT])
                    S_(svt(svA, 4), ws[:, 6:8, SEQ:TT], -1.0, None, mult)
                    s4 = lambda t: ws[:, t, 0:SEQ].rearrange("p (c t) -> p c t", c=NC)
                    for i in range(2):
                        STT(ARa[:, i, :, 0, :], s4(6 + i), -1.0, s4(i), mult, mult)
                        T_(ARa[:, i, :, 1, :], RA[:, i, 0:SEQ].rearrange("p (c t) -> p c t", c=NC), s4(4 + i), mult)
                    T_(ws[:, 14:16, 0:SEQ], ws[:, 8:10, 0:SEQ], ws[:, 2:4, 0:SEQ], mult)
                    T_(ws[:, 16:18, 0:SEQ], RA[:, 2:4, 0:SEQ], ws[:, 2:4, 0:SEQ], mult)
                    E4 = ws[:, 4:6, 0:SEQ].rearrange("p i (c t) -> p i c t", c=NC)
                    did(da, "pend", v.tensor_copy(pc[:, 1], E4[:, :, :, C - 1]))
                    T_(pc[:, 2, :, 0:NC - 1], pc[:, 1, :, 0:NC - 1], pc[:, 0, :, 1:NC], mult)
                    v.tensor_copy(pc[:, 2, :, NC - 1:NC], pc[:, 1, :, NC - 1:NC])
                    for i in range(2):
                        last = STT(ws[:, 6 + i, :], RA[:, i, :], par("r_k", i), RA[:, 2 + i, :], mult, mult)
                    did(da, "bt", last)
                    dve.wait_ge(*pa.at("bsum"))
                    did(da, "prep", T_(q4(RA[:, 0:2, :]), psB[:, :, 0:HALF], q4(RA[:, 4:6, :]), mult))
                    def decode_a(part):
                        S0, tmp = wfC[:, 0:1024], wfC[:, 1024:2048]
                        r_, w_, k_, a_, b_ = (vecA[:, n, :] for n in (0, 1, 2, 4, 5))
                        if part == 0:
                            decode_in(0)
                            did(ds, "1", T_(vk(tmp), vk(S0), row(a_), mult))
                        elif part == 1:
                            v.tensor_reduce(sa[:, 0, :], vk(tmp), AX.X, add)
                            did(ds, "2", T_(vk(S0), vk(S0), row(w_), mult))
                        elif part == 2:
                            did(ds, "3", T_(vk(tmp), bc(sa[:, 0, :], 2, HD), row(b_), mult))
                        elif part == 3:
                            did(ds, "4", T_(S0, S0, tmp, add))
                        elif part == 4:
                            did(ds, "5", T_(vk(tmp), bc(vv[:, 0, :], 2, HD), row(k_), mult))
                        elif part == 5:
                            did(ds, "6", T_(S0, S0, tmp, add))
                        else:
                            did(ds, "7", T_(vk(tmp), vk(S0), row(r_), mult))
                            v.tensor_reduce(so[:, 0, :], vk(tmp), AX.X, add).then_inc(*ds.step("so"))

                    Ma = Mst[0]
                    for c in range(NC):
                        dve.wait_ge(*pa.at("gram", c))
                        for g in range(2):
                            T_(GRa4[:, 2 * g:2 * g + 2, :], psB[:, 2 * g:2 * g + 2, :], bc(cc("rmask"), 1, 2), mult).then_inc(*da.step("gr"))
                        dve.wait_ge(*da.at("gr", 2 * c + 1))
                        dve.wait_ge(*aa.at("ti", c))
                        dve_tree(dve, pa, da, AtA, Ta, Va, c, decode_a if c == 2 else None)
                        dve.wait_ge(*pa.at("u", c))
                        v.tensor_copy(Ua, psB[:, 2, 0:256]).then_inc(*da.step("u"))
                        dve.wait_ge(*pa.at("o", c))
                        for g in range(2):
                            pr = slice(g * HD, (g + 1) * HD)
                            last = T_(Ma[pr], psB[pr, 3, 0:256].rearrange("p (i x) -> p i x", i=2)[:, :, g * HD:(g + 1) * HD], Ma[pr], add)
                        did(da, "sum", last, c)
                        did(da, "st", T_(Ma[:], Ma[:], bc(pc[:, 2, :, c], 2, HD), mult), c)

                    pd, ad, dd = TR["pe_d"], TR["act_d"], TR["dve_d"]
                    decode_out(0)
                    dve.wait_ge(*pn.at("mean"))
                    did(dn, "cen", STT(q4(outs3[0]), psB[:, :, 0:HALF], -1.0 / HD, q4(outs3[0]), mult, add))
                    dve.wait_ge(*an.at("rn", 0))
                    did(dn, "normed", T_(outs3[0], outs3[0], ws[:, 0:2, :], mult), 0)
                    for i in range(2):
                        last = S_(outs3[0][:, i, :], outs3[0][:, i, :], par("ln_g", i), par("ln_b", i), mult, add)
                    did(dn, "gains", last)
                    did(dn, "bonus", T_(outs3[0], outs3[0], RA[:, 0:2, :], add))
                    gated(0, outs3[0], RA[:, 7:9, :])
                    merged(0)

                    def conv(tr, raw, n, wname, st0, between=None):
                        w0 = PARAM_ROWS[wname]
                        for tap in range(2, -1, -1):
                            sh = CONV - 1 - tap
                            for t in range(n):
                                last = STT(ws[:, t, sh:SEQ], raw[:, t, 0:SEQ - sh], par(wname, tap * n + t), ws[:, t, sh:SEQ], mult, add)
                            did(tr, "cvt", last, 2 - tap)
                            if tap == 2 and between:
                                between()
                        stc = stT[:, 0:n, st0:st0 + 24].rearrange("p i (b j) -> p i b j", j=3)
                        wt = parT[:, w0:w0 + 3 * n].rearrange("p (j i) -> p i j", i=n)
                        tmp = wv(14, n * 24).rearrange("p (i b j) -> p i b j", i=n, b=NB)
                        new = wv(15, n * NB).rearrange("p (i b) -> p i b", i=n)
                        did(tr, "cs1", T_(tmp, stc, bc(wt, 2, NB), mult))
                        v.tensor_reduce(ws[:, 0:n, SEQ:TT], tmp, AX.X, add)
                        did(tr, "cs2", T_(new, raw[:, 0:n, SEQ:TT], bc(parT[:, w0 + 3 * n:w0 + 4 * n], 2, NB), mult))
                        did(tr, "cs3", T_(ws[:, 0:n, SEQ:TT], ws[:, 0:n, SEQ:TT], new, add))

                    dve.wait_ge(*ad.at("cv0"))
                    conv(dd, RD, 6, "gdn_w", 40, lambda: merged(1))
                    v.tensor_copy(colbg[:, 0:1], cc("eps")).then_inc(*dd.step("cv"))
                    merged(2)
                    dve.wait_ge(*ad.at("ths"))
                    did(dd, "silu2", STT(ws[:, 0:6, :], RD[:, 0:6, :], 1.0, ws[:, 0:6, :], add, mult))
                    merged(3)
                    dve.wait_ge(*ad.at("gz"))
                    g_ = lambda t: ws[32:36, t, :]
                    log1p(dd, "g", g_(11), g_(12), g_(13), g_(14), lambda: merged(4))
                    S_(gp[32:36, 3:4], gp[32:36, 2:3], -1.0, None, mult)
                    did(dd, "gmax", S_(g_(12), bg[32:36, :], 0.0, None, ALU.max))
                    did(dd, "gsp", T_(g_(12), g_(12), g_(14), add))
                    did(dd, "gneg", S_(g_(12), g_(12), gp[32:36, 3:4], None, mult))
                    S_(bg[0:4, :], bg[0:4, :], 0.5, 0.5, mult, add)
                    did(dd, "gc", v.tensor_tensor_scan(bg[32:36, :], cc("reset", 32, 36), g_(12), 0.0, mult, add))
                    dve.wait_ge(*ad.at("rn"))
                    STT(ws[:, 0:2, :], ws[:, 0:2, :], 0.5 * HD ** -0.5, RD[:, 0:2, :], mult, mult)
                    did(dd, "qk", STT(ws[:, 2:4, :], ws[:, 2:4, :], 0.5, RD[:, 2:4, :], mult, mult))
                    merged(5)
                    dve.wait_ge(*pd.at("bcast", 0))
                    for i in range(2):
                        STT(ARd[:, i, :, 0, :], s4(2 + i), -1.0, psB[:, i, :].rearrange("p (c t) -> p c t", c=NC), mult, mult)
                        v.tensor_copy(ARd[:, i, :, 1, :], s4(i))
                    v.tensor_copy(svt(svB, 3), ws[:, 0:2, SEQ:TT])
                    v.tensor_copy(svt(svB, 4), ws[:, 2:4, SEQ:TT])
                    S_(svt(svB, 5), ws[:, 4:6, SEQ:TT], 0.5, None, mult)
                    did(dd, "ar", v.tensor_copy(svt(svB, 6), psB[:, 2, 0:16].rearrange("p (i b) -> p i b", i=2)))
                    merged(6)
                    dve.wait_ge(*ad.at("egc"))
                    v.tensor_copy(svt(svB, 7), ws[:, 6:8, SEQ:TT])
                    for i in range(2):
                        last = T_(RD[:, 4 + i, 0:SEQ].rearrange("p (c t) -> p c t", c=NC), ARd[:, i, :, 0, :], s4(6 + i), mult)
                    did(dd, "kbe", last)
                    did(dd, "prep", T_(ws[:, 6:8, 0:SEQ], ws[:, 0:2, 0:SEQ], ws[:, 6:8, 0:SEQ], mult))
                    merged(7)
                    def decode_d(part):
                        S0, tmp = wfA[:, 0:1024], wfA[:, 1024:2048]
                        if part == 0:
                            decode_in(1)
                            did(ds, "11", S_(S0, S0, vecB[:, 7, 0:1], None, mult))
                        elif part == 1:
                            did(ds, "12", T_(kv(tmp), kv(S0), col(vecB[:, 4, :]), mult))
                        elif part == 2:
                            did(ds, "13", v.tensor_reduce(sa[:, 1, :], kvT(tmp), AX.X, add))
                        elif part == 3:
                            did(ds, "14", T_(sa[:, 1, :], vv[:, 1, :], sa[:, 1, :], sub))
                            did(ds, "15", S_(sa[:, 1, :], sa[:, 1, :], vecB[:, 6, 0:1], None, mult))
                            did(ds, "16", T_(kv(tmp), col(vecB[:, 4, :]), bc(sa[:, 1, :], 1, HD), mult))
                        elif part == 4:
                            did(ds, "17", T_(S0, S0, tmp, add))
                        elif part == 5:
                            did(ds, "18", T_(kv(tmp), kv(S0), col(vecB[:, 3, :]), mult))
                        else:
                            v.tensor_reduce(so[:, 1, :], kvT(tmp), AX.X, add).then_inc(*ds.step("so"))

                    Md = Mst[2]
                    D4 = h4(Dd)
                    for c in range(NC):
                        dve.wait_ge(*ad.at("col", c))
                        pg = h4(psB[:, 0, :])
                        for h in range(HEADS):
                            STT(D4[:, slot(h), :], pg[:, h, :], colbg[:, 32 + h:33 + h], cc("negm"), sub, add)
                        T_(kdl[:, 0:4], pg[:, :, C - 1], colbg[:, 32:36], sub)
                        v.tensor_copy(kdl[:, 4:8], pg[:, :, C - 1]).then_inc(*dd.step("dm"))
                        dve.wait_ge(*pd.at("gram", c))
                        dve.wait_ge(*ad.at("dexp", c))
                        for g in range(2):
                            T_(GRd[:, 512 * g:512 * g + 512].rearrange("p (h x t) -> p h x t", h=2, x=2),
                               psB[:, 2 + g, :].rearrange("p (h x t) -> p h x t", h=2, x=2), bc(D4[:, 2 * g:2 * g + 2, :], 2, 2), mult).then_inc(*dd.step("gr"))
                        dve.wait_ge(*dd.at("gr", 2 * c + 1))
                        dve.wait_ge(*ad.at("ti", c))
                        dve.wait_ge(*pd.at("tr", c))
                        T_(h4(rowsd[:, 0:256]), h4(psB[:, 0, 0:256]), bc(kdl[:, 0:4], 2, HD), mult)
                        STT(h4(rowsd[:, 256:512]), h4(psB[:, 0, 256:512]), 0.5, bc(colbg[:, 0:4], 2, HD), mult, mult).then_inc(*dd.step("rows"))
                        dve_tree(dve, pd, dd, AtD, Td, Vd, c, decode_d if c == 2 else None)
                        dve.wait_ge(*pd.at("x1", c))
                        dve.wait_ge(*dd.at("rows", c))
                        T_(X1d.rearrange("p (i g v) -> p i g v", i=2, g=2), psB[:, 0:2, 0:P].rearrange("p g (i v) -> p i g v", i=2),
                           rowsd[:, 256:512].rearrange("p (i g v) -> p i g v", i=2, g=2), add).then_inc(*dd.step("x1"))
                        dve.wait_ge(*pd.at("o", c))
                        for h in range(HEADS):
                            i, g = h // 2, h % 2
                            last = STT(Md[hp(h), i, :], Md[hp(h), i, :], kdl[hp(h), 4 + h:5 + h], psB[hp(h), 3, i * P + g * HD:i * P + (g + 1) * HD], mult, add)
                        did(dd, "st", last, c)
                    decode_out(1)
                    dve.wait_ge(*an.at("rn", 1))
                    did(dn, "normed", STT(outs3[1], outs3[1], par("gdn_g"), ws[:, 0:2, :], mult, mult), 1)
                    gated(1, outs3[1], RD[:, 6:8, :])

                    pb, ab, db = TR["pe_b"], TR["act_b"], TR["dve_b"]
                    rd = lambda n, hf_: RB[:, 2 * n:2 * n + 2, :]
                    for n, sc in ((0, 1.0), (1, HD ** -0.5)):
                        dve.wait_ge(*pb.at("rot", n))
                        for i in range(2):
                            STT(half(ws[:, i, :]), psB[:, 2 * i:2 * i + 2, 0:HALF], sc, half(cc("sin")), mult, mult)
                        for i in range(2):
                            last = STT(RB[:, 2 * n + i, :], RB[:, 2 * n + i, :], sc, cc("cos"), mult, mult)
                        did(db, "rot", last, n)
                        did(db, "rope", T_(RB[:, 2 * n:2 * n + 2, :], RB[:, 2 * n:2 * n + 2, :], ws[:, 0:2, :], add), n)
                        if n == 0:
                            merged(8)
                    for n in range(2):
                        v.tensor_copy(svt(svB, n), RB[:, 2 * n:2 * n + 2, SEQ:TT])
                    v.tensor_copy(svt(svB, 2), RB[:, 4:6, SEQ:TT]).then_inc(*db.step("sv"))
                    q_c = RB[:, 0:2, 0:SEQ].rearrange("p i (c t) -> p i c t", c=NC)
                    did(db, "prep", T_(ws[:, 2:4, 0:SEQ].rearrange("p i (c t) -> p i c t", c=NC), q_c,
                                       bc(cc("qdec").rearrange("p (i t) -> p i t", i=2), 2, NC), mult))
                    merged(9)
                    Mb = Mst[1]
                    for c in range(NC):
                        dve.wait_ge(*pb.at("gram", c))
                        T_(G1b.rearrange("p (i g t) -> p i g t", i=2, g=2), psB[:, 0:2, 0:256].rearrange("p g (i t) -> p i g t", i=2),
                           cc("rdec").rearrange("p (i g t) -> p i g t", i=2, g=2), mult).then_inc(*db.step("gr"))
                        dve.wait_ge(*pb.at("tr", c))
                        T_(h4(krb), h4(psB[:, 2, 0:256]), bc(cc("kdec"), 2, HD), mult)
                        v.tensor_copy(vrb, psB[:, 2, 256:512]).then_inc(*db.step("rows"))
                        dve.wait_ge(*pb.at("o", c))
                        for h in range(HEADS):
                            i, g = h // 2, h % 2
                            last = STT(Mb[hp(h), i, :], Mb[hp(h), i, :], cc("gc")[hp(h), i:i + 1], psB[hp(h), 3, i * P + g * HD:i * P + (g + 1) * HD], mult, add)
                        did(db, "st", last, c)
                        merged(10 + c)
                        if c == 1:
                            ac, dc = TR["act_c"], TR["dve_c"]
                            dve.wait_ge(*ac.at("cv0"))
                            conv(dc, RC, 2, "lru_w", 16)
                            did(dc, "xc", T_(ws[:, 0:2, SEQ:TT], ws[:, 0:2, SEQ:TT], bc(par("lru_b", 0, 2), 2, NB), add))
                    decode_in(2)
                    S0, tmp = wfA[:, 0:1024], wfA[:, 1024:2048]
                    did(ds, "21", T_(kv(tmp), col(vecB[:, 1, :]), bc(vv[:, 2, :], 1, HD), mult))
                    did(ds, "22", STT(S0, S0, cc("gam"), tmp, mult, add))
                    did(ds, "23", T_(kv(tmp), kv(S0), col(vecB[:, 0, :]), mult))
                    v.tensor_reduce(so[:, 2, :], kvT(tmp), AX.X, add).then_inc(*ds.step("so"))
                    pcc, ac, dc = TR["pe_c"], TR["act_c"], TR["dve_c"]
                    merged(14, 15)
                    decode_out(2)
                    dve.wait_ge(*ac.at("au"))
                    S_(ws[:, 10:12, :], ws[:, 8:10, :], 2.0, 1e-18, mult, ALU.max).then_inc(*dc.step("u2"))
                    dve.wait_ge(*an.at("rn", 2))
                    did(dn, "normed", T_(outs3[2], outs3[2], norm_ws(2), mult), 2)
                    gated(2, outs3[2], RB[:, 6:8, :])
                    did(dc, "ix", STT(ws[:, 4:6, :], ws[:, 4:6, :], 1.0, ws[:, 0:2, :], add, mult))
                    merged(16)
                    dve.wait_ge(*ac.at("lnu"))
                    T_(ws[:, 10:12, :], ws[:, 10:12, :], ws[:, 12:14, :], sub).then_inc(*dc.step("lndiff"))
                    merged(17)
                    dve.wait_ge(*ac.at("root"))
                    T_(ws[:, 0:2, SEQ:TT], ws[:, 6:8, SEQ:TT], stT[:, 0:2, 8:16], mult)
                    did(dc, "b", STT(ws[:, 4:6, :], ws[:, 4:6, :], 0.5, ws[:, 10:12, :], mult, mult))
                    for i in range(2):
                        v.tensor_tensor_scan(RC[:, i, 0:SEQ], ws[:, 6 + i, 0:SEQ], ws[:, 4 + i, 0:SEQ], 0.0, mult, add)
                    did(dc, "h", T_(RC[:, 0:2, SEQ:TT], ws[:, 0:2, SEQ:TT], ws[:, 4:6, SEQ:TT], add))
                    merged(18, 19)
                    dve.wait_ge(*an.at("tz", 3))
                    dve.wait_ge(*pcc.at("hrow"))
                    gated(3, RC[:, 0:2, :], RC[:, 2:4, :])
                    merged(20)
                    merged(*range(21, 32))
                    m_lo(KT - 1)
                    for e in range(KT):
                        b = 2 * (e % 2)
                        dve.wait_ge(*pm.at("out", e))
                        if e % 4 == 0:
                            dve.wait_ge(s_xin1 if e else s_xin0, 16)
                        gate = modT[:, 16 + e, :]
                        n1 = SEQ - HALF
                        STT(xT[:, e, 0:HALF], psA[:, b, 0:HALF], gate[:, 8:9], xT[:, e, 0:HALF], mult, add)
                        STT(xT[:, e, HALF:SEQ], psA[:, b + 1, 0:n1], gate[:, 8:9], xT[:, e, HALF:SEQ], mult, add)
                        did(dm, "xs", T_(der[:, 32:40], psA[:, b + 1, n1:HALF], gate[:, 0:8], mult), e)
                        did(dm, "x", T_(xT[:, e, SEQ:TT], xT[:, e, SEQ:TT], der[:, 32:40], add), e)

            nc.all_engine_barrier()
            nc.gpsimd.sem_clear(range(s_const.num, TR["dve_m"].sem.num + 1))
            nc.all_engine_barrier()

        with nc.Block() as block:
            pe9, act9, dve9 = TR["pe9"], TR["act9"], TR["dve9"]

            @block.scalar
            def _(act):
                A = nc.scalar.activation
                for d in range(KT):
                    A(ws[:, 10 + d, :], xT[:, d, :], ACT.Square).then_inc(*act9.step("sq"))
                act.wait_ge(*pe9.at("ss"))
                A(rs[:].rearrange("p (h c) -> p h c", h=2), psB[:, 2:4, 0:HALF], ACT.Ln, bias=cc("eps"), scale=1.0 / D_MODEL).then_inc(*act9.step("ln"))
                act.wait_ge(*act9.at("ln"))
                A(rs[:], rs[:], ACT.Exp, scale=-0.5).then_inc(*act9.step("rs"))
                for t in range(4):
                    act.wait_ge(*pe9.at("y", t))
                    ps = psA if t % 2 == 0 else psB
                    nc.scalar.copy(ws[:, 2 * t:2 * t + 2, 0:512], ps[:, 0:2, :]).then_inc(*act9.step("y"))

            @block.tensor
            def _(pe):
                for d in range(KT):
                    pe.wait_ge(*act9.at("sq", d))
                    for hf in range(2):
                        last = nc.tensor.matmul(psB[:, 2 + hf, 0:HALF], ones, ws[:, 10 + d, hf * HALF:(hf + 1) * HALF], start=(d == 0), stop=(d == KT - 1))
                last.then_inc(*pe9.step("ss"))
                pe.wait_ge(*dve9.at("y"))
                for t in range(4):
                    ps = psA if t % 2 == 0 else psB
                    if t >= 2:
                        pe.wait_ge(*act9.at("y", t - 2))
                    for d in range(KT):
                        last = nc.tensor.transpose(ps[:, d // 4, (d % 4) * P:(d % 4 + 1) * P], hT[:, d, t * P:(t + 1) * P], ident)
                    last.then_inc(*pe9.step("y"))
                for d in range(KT):
                    last = nc.tensor.transpose(psA[0:8, 2 + d // 4, (d % 4) * P:(d % 4 + 1) * P], hT[:, d, SEQ:TT], ident)
                last.then_inc(*pe9.step("ys"))

            @block.vector
            def _(dve):
                dve.wait_ge(*act9.at("rs"))
                for d in range(KT):
                    last = nc.vector.scalar_tensor_tensor(hT[:, d, :], xT[:, d, :], par("final_g", d), rs[:], mult, mult)
                last.then_inc(*dve9.step("y"))
                dve.wait_ge(*pe9.at("ys"))
                nc.vector.tensor_copy(ws[0:8, 8:10, 0:512], psA[0:8, 2:4, :]).then_inc(*dve9.step("ys"))

            @block.sync
            def _(sp):
                for t in range(4):
                    sp.wait_ge(*act9.at("y", t))
                    sp.dma_start(o["y_prompt"][0, t * P:(t + 1) * P, :].rearrange("p (a c) -> p a c", a=2), ws[:, 2 * t:2 * t + 2, 0:512]).then_inc(s_y, 16)
                sp.wait_ge(*dve9.at("ys"))
                sp.dma_start(o["y_sample"][:, 0, :].rearrange("p (a c) -> p a c", a=2), ws[0:8, 8:10, 0:512]).then_inc(s_y, 16)
                sp.wait_ge(s_y, 16 * 5)
    return {n: t.made for n, t in tracks.items()}


STEPS = {
    'pe0': 'xs c x x x x x x x x'.split(),
    'act0': 'tanh_c x x x x x x x x'.split(),
    'dve0': 'tmask silu_c xs c'.split(),
    'pe_f': 'ss ada ada ada ada ada ada ada ada par st ada ada ada ada ada ada ada ada mod ada ada ada ada ada ada ada ada mod'.split(),
    'act_f': 'sq sq sq sq sq sq sq sq lnx rs modrow modrow modrow modrow lam_abs lam_z expA hh hh hh hh hh hh hh hh modrow'.split(),
    'dve_f': 'zero parT der stT xn modT G hg hd hs hs hl hs hl hs hl hs hl hs hl hs hl hs hl hl lam1 lam2 lam3 lam4 lam5 lamm13 lama13 lamm11 lama11 lamm9 lama9 lamm7 lama7 lamm5 lama5 lamm3 lama3 lamm1 lama1 lam6 lam_y lam_sp modT gate'.split(),
    'pe_a': 'crow lora lora kks bsum gram tr z z y y z z y y z z y y z z y y z z y y z z y y z z x1 u o gram tr z z y y z z y y z z y y z z y y z z y y z z y y z z x1 u o gram tr z z y y z z y y z z y y z z y y z z y y z z y y z z x1 u o gram tr z z y y z z y y z z y y z z y y z z y y z z y y z z x1 u o mt'.split(),
    'act_a': 'crow twd thw tha kk2 kf lnk rn decay exps ti rows y y y y y y y y y y y y x1 o ti rows y y y y y y y y y y y y x1 o ti rows y y y y y y y y y y y y x1 o ti rows y y y y y y y y y y y y x1 o mrow'.split(),
    'dve_a': 'diff pm kk lw1 scan mid lrel lex kkn bv pend bt prep gr gr t t t t t t t t t t t t t t u sum st gr gr t t t t t t t t t t t t t t u sum st gr gr t t t t t t t t t t t t t t u sum st gr gr t t t t t t t t t t t t t t u sum st'.split(),
    'pe_d': 'crow qs ks bcast bcast gb gram tr z z y y z z y y z z y y z z y y z z y y z z y y z z x1 u o gb gram tr z z y y z z y y z z y y z z y y z z y y z z y y z z x1 u o gb gram tr z z y y z z y y z z y y z z y y z z y y z z y y z z x1 u o gb gram tr z z y y z z y y z z y y z z y y z z y y z z y y z z x1 u o'.split(),
    'act_d': 'crow cv0 gabs gz ths sq lnq lnk rn egc ti col dexp y y y y y y y y y y y y u o ti col dexp y y y y y y y y y y y y u o ti col dexp y y y y y y y y y y y y u o ti col dexp y y y y y y y y y y y y u o'.split(),
    'dve_d': 'cvt cvt cvt cs1 cs2 cs3 cv silu2 g1 g2 g3 g4 g5 gm13 ga13 gm11 ga11 gm9 ga9 gm7 ga7 gm5 ga5 gm3 ga3 gm1 ga1 g6 gmax gsp gneg gc qk ar kbe prep dm gr gr rows t t t t t t t t t t t t t t x1 st dm gr gr rows t t t t t t t t t t t t t t x1 st dm gr gr rows t t t t t t t t t t t t t t x1 st dm gr gr rows t t t t t t t t t t t t t t x1 st'.split(),
    'pe_b': 'rot rot gram tr o gram tr o gram tr o gram tr o'.split(),
    'act_b': 'o o o o'.split(),
    'dve_b': 'rot rope rot rope sv prep gr rows st gr rows st gr rows st gr rows st'.split(),
    'pe_c': 'crow gates gates hrow'.split(),
    'act_c': 'cv0 crow thr thi au lnu root hrow'.split(),
    'dve_c': 'cvt cvt cvt cs1 cs2 cs3 xc u2 ix lndiff b h'.split(),
    'pe_s': 'rows oT rows oT rows oT'.split(),
    'act_s': 'rows rows rows'.split(),
    'dve_s': '1 2 3 4 5 6 7 so oT 11 12 13 14 15 16 17 18 so oT 21 22 23 so oT'.split(),
    'pe_p': 'proj proj proj proj proj proj proj proj proj proj proj proj proj proj proj proj proj proj proj proj proj proj proj proj proj proj proj proj proj proj'.split(),
    'act_p': 'proj proj proj proj proj proj proj proj proj proj proj proj proj proj proj proj proj proj proj proj proj proj proj proj proj proj proj proj proj proj'.split(),
    'act_w': 'hi hi hi hi hi hi hi hi hi hi hi hi hi hi hi hi hi hi hi hi hi hi hi hi hi hi hi hi hi hi hi hi hi hi hi hi hi hi hi hi hi hi hi hi hi hi hi hi hi hi hi hi hi hi hi hi hi hi hi hi hi hi hi hi hi hi hi hi hi hi'.split(),
    'pool_w': 'lo lo lo lo lo lo lo lo lo lo lo lo lo lo lo lo lo lo lo lo lo lo lo lo lo lo lo lo lo lo lo lo lo lo lo lo lo lo lo lo lo lo lo lo lo lo lo lo lo lo lo lo lo lo lo lo lo lo lo lo lo lo lo lo lo lo lo lo lo lo'.split(),
    'pe_n': 'mean var var var'.split(),
    'act_n': 'sq ln rn tz sq ln rn tz sq ln rn tz tz'.split(),
    'dve_n': 'cen normed gains bonus siluz gated normed siluz gated normed siluz gated siluz gated'.split(),
    'pe_m': 'gl gate gl gate gl gate gl gate gl gate gl gate gl gate gl gate gl gl gate gate gl gate gl gate gl gate gl gate gl gate gl gate gl gl gate gate gl gate gl gate gl gate gl gate gl gate gl gate gl gate gl gate gl gate gl gate gl gate gl gate gl gate gl gate out out out out out out out out'.split(),
    'act_m': 'th th th th th th th th th th th th th th th th th th th th th th th th th th mhi th mhi th mhi th mhi th mhi th mhi th mhi mhi'.split(),
    'dve_m': 'mul mul mul mul mul mul mul mul mul mg mul mg mul mg mul mg mul mg mul mg mul mg mul mg mul mg mul mg mul mg mul mg mul mg mul mg mul mg mul mg mul mg mul mg mlo mul mg mlo mul mg mlo mul mg mlo mul mg mlo mul mg mlo mul mg mlo mlo xs x xs x xs x xs x xs x xs x xs x xs x'.split(),
    'pe9': 'ss y y y y ys'.split(),
    'act9': 'sq sq sq sq sq sq sq sq ln rs y y y y'.split(),
    'dve9': 'y ys'.split(),
}


_INS = ['x_prompt', 'x_sample', 'c_prompt', 'c_sample', 'state_rwkv_wkv', 'state_ret', 'state_lru_conv', 'state_gdn',
        'state_gdn_conv', 'ada_w', 'w_in', 'rwkv_w2', 'rwkv_a2', 'lru_gate_w', 'gdn_A_log', 'gdn_dt_bias', 'w_up', 'w_out']
_STATES = [('wkv', (HEADS, HD, HD)), ('shift', (A_SHIFT,)), ('ret', (HEADS, HD, HD)), ('lru_h', (W,)),
           ('lru_conv', (CONV - 1, W)), ('gdn', (HEADS, HD, HD)), ('gdn_conv', (CONV - 1, QKV))]
_OUTS = ([('y_prompt', (1, SEQ, D_MODEL)), ('y_sample', (NB, 1, D_MODEL))]
         + [('p_' + n, (DEPTH, 1) + s) for n, s in _STATES] + [('s_' + n, (DEPTH, NB) + s) for n, s in _STATES])
PAST_LEN = 4096


def constants():
    import numpy as np
    f = np.float32
    cst = np.zeros((P, CONST_N), f)

    def put(name, value, p0=0):
        lo, hi = CONST_COLS[name]
        value = np.asarray(value, f)
        cst[p0:p0 + value.shape[0], lo:hi] = value.reshape(value.shape[0], -1)

    p, t = np.arange(P), np.arange(C)
    put("ident", np.eye(P))
    put("bones", p[:, None] // HD == p[None, :] // HD)
    put("ones", np.ones((P, P)))
    rot = np.zeros((P, P), f)
    for m in range(P):
        rot[m + 32 if m % HD < 32 else m - 32, m] = -1.0 if m % HD < 32 else 1.0
    put("rotp", rot)
    strict, incl = t[None, :] > p[:, None], t[None, :] >= p[:, None]
    put("rmask", np.stack([strict, incl, strict, incl], 1))
    put("negm", np.where(incl, 0.0, -1e30))
    lg = np.log(1.0 - 2.0 ** (-5.0 - np.arange(HEADS, dtype=np.float64)))
    rel = t[None, None, :] - p[:, None, None]
    put("rdec", np.where(rel >= 0, np.exp(lg[None, :, None] * np.maximum(rel, 0)), 0.0))
    head = 2 * np.arange(2)[None, :] + (p[:, None] // HD)
    put("qdec", np.exp(lg[head][:, :, None] * (t + 1.0)))
    put("kdec", np.exp(lg[None, :] * (C - 1.0 - p[:, None])))
    put("gc", np.exp(lg[head] * C))
    put("gam", np.exp(lg[p % HEADS])[:, None])
    pos = np.concatenate([np.arange(SEQ), np.full(NB, PAST_LEN)]).astype(f)
    inv = (f(10000.0) ** (-np.arange(32, dtype=f) / f(32))).astype(f)
    ang = (pos[None, :] * inv[p % 32][:, None]).astype(f)
    put("cos", np.cos(ang.astype(np.float64)))
    put("sin", np.sin(ang.astype(np.float64)))
    reset = np.ones(TT)
    reset[0:SEQ:C] = 0.0
    reset[SEQ:] = 0.0
    put("reset", np.tile(reset, (P, 1)))
    for base in (0, 32):
        put("sel4", (np.arange(HEADS)[:, None, None] == np.arange(HEADS)[None, :, None]) * np.ones((1, 1, P)), base)
        put("sel2", np.arange(HEADS)[:, None, None] == head.T[None, :, :], base)
    put("eps", np.full((P, 1), 1e-6))
    put("epsgn", np.full((P, 1), 64e-5))
    masks = np.zeros((P, 14, P), f)
    for lv in range(7):
        b = 1 << lv
        m = (p[:, None] // (2 * b) == p[None, :] // (2 * b)) & (p[:, None] // b % 2 == 1) & (p[None, :] // b % 2 == 0)
        masks[:, lv], masks[:, 7 + lv] = m, m.T
    return cst, masks.reshape(P, -1)


def packed(inputs):
    import numpy as np
    rows = lambda name: np.reshape(inputs[name], (DEPTH, -1, P))
    order = ("ada_b", "norm_g", "rwkv_mu", "rwkv_w0", "rwkv_a0", "rwkv_k_k", "rwkv_k_a", "rwkv_r_k", "rwkv_ln_g", "rwkv_ln_b",
             "lru_conv_w", "lru_conv_b", "lru_gate_b", "lru_lambda", "gdn_conv_w")
    gdn_g = np.concatenate([inputs["gdn_norm_g"]] * 2, -1)[:, None, :]
    final_g = np.stack([np.reshape(inputs["final_g"], (KT, P))] * DEPTH)
    params = np.concatenate([rows(n) for n in order] + [gdn_g, final_g], 1)
    states = np.zeros((DEPTH, 64, A_SHIFT), params.dtype)
    states[:, 0:8] = inputs["state_rwkv_shift"]
    states[:, 8:16, 0:W] = inputs["state_lru_h"]
    states[:, 16:40, 0:W] = np.reshape(inputs["state_lru_conv"], (DEPTH, 24, W))
    states[:, 40:64, 0:QKV] = np.reshape(inputs["state_gdn_conv"], (DEPTH, 24, QKV))
    return np.ascontiguousarray(params), states


def kernel(**inputs):
    import numpy as _np
    import concourse.bacc as _bacc
    from concourse import mybir as _mybir
    from concourse.bass_utils import run_bass_kernel_spmd as _run

    nc = _bacc.Bacc("TRN2", target_bir_lowering=False, num_devices=1)
    arrays, ins, outs = {}, {}, {}
    given = {name: _np.ascontiguousarray(inputs[name]) for name in _INS}
    given["consts"], given["tree_masks"] = constants()
    given["param_rows"], given["state_rows"] = packed(inputs)
    for name, x in given.items():
        arrays[f"in_{name}"] = x
        ins[name] = nc.dram_tensor(f"in_{name}", x.shape, _mybir.dt.from_np(x.dtype), kind="ExternalInput").ap()
    for name, shape in _OUTS:
        outs[name] = nc.dram_tensor(f"out_{name}", shape, _mybir.dt.float32, kind="ExternalOutput").ap()
    build_program(nc, ins, outs, STEPS)
    r = _run(nc, [arrays], core_ids=[0])
    return tuple(r.results[0][f"out_{name}"] for name, _ in _OUTS)
```
